# Optimizing a Trainium2 kernel written in Bass

```python
import jax
import jax.numpy as jnp
from jax import lax
import numpy as np

D_MODEL = 1024
BATCH = 1
SEQ = 256
DEPTH = 2

GRID_W = 64
CTX_LEN = 256
N_DIR = 2
N_BRANCH = 2
NORM_EPS = 1e-6

SSM_EXPAND = 2
D_SSM = SSM_EXPAND * D_MODEL
SSM_HEAD_DIM = 64
SSM_HEADS = D_SSM // SSM_HEAD_DIM
SSM_GROUPS = 4
SSM_HEADS_PER_GROUP = SSM_HEADS // SSM_GROUPS
SSM_STATE = 128
SSM_CONV = 3
SSM_CHUNK = 128
D_XBC = D_SSM + 2 * SSM_GROUPS * SSM_STATE

D_RWKV = D_MODEL
RWKV_HEAD = 64
RWKV_HEADS = D_RWKV // RWKV_HEAD
RWKV_CONV = 3
LORA_W = 64
LORA_A = 64
LORA_G = 128
RWKV_LN_EPS = 64e-5

D_FF = 2816
FFN_CONV = 3

IN_SIZES = (D_SSM, D_XBC, SSM_HEADS, 3 * D_RWKV, N_DIR * LORA_W, N_DIR * LORA_A, LORA_G, N_BRANCH * D_MODEL)
D_IN = D_SSM + D_XBC + SSM_HEADS + 3 * D_RWKV + N_DIR * LORA_W + N_DIR * LORA_A + LORA_G + N_BRANCH * D_MODEL

kernel_name = "hybrid_ssd_rwkv7_convffn_dit"

def _split_points(sizes):
    pts, acc = [], 0
    for s in sizes[:-1]:
        acc += s
        pts.append(acc)
    return pts

def group_rmsnorm(x, groups, g):
    shp = x.shape
    xf = x.astype(jnp.float32).reshape(shp[:-1] + (groups, shp[-1] // groups))
    xf = xf * lax.rsqrt(jnp.mean(xf * xf, axis=-1, keepdims=True) + NORM_EPS)
    return xf.reshape(shp).astype(x.dtype) * g

def rmsnorm(x, g):
    return group_rmsnorm(x, 1, g)

def modulate(h, shift, scale):
    return h * (1 + scale) + shift

def adaln(cond, w, b):
    return jnp.split(jax.nn.silu(cond) @ w + b, 6, axis=-1)

def dwconv1d(t, w):
    K, C = w.shape
    return lax.conv_general_dilated(t, w[:, None, :], window_strides=(1,), padding=[(K // 2, K // 2)],
                                    dimension_numbers=('NWC', 'WIO', 'NWC'), feature_group_count=C)

def dwconv2d_grid(t, w):
    b, T, C = t.shape
    g = t.reshape(b, T // GRID_W, GRID_W, C)
    out = lax.conv_general_dilated(g, w[:, :, None, :], window_strides=(1, 1), padding=[(1, 1), (1, 1)],
                                   dimension_numbers=('NHWC', 'HWIO', 'NHWC'), feature_group_count=C)
    return out.reshape(b, T, C)

def seg_conv1d(t, w):
    return jnp.concatenate([dwconv1d(t[:, :CTX_LEN], w), dwconv1d(t[:, CTX_LEN:], w)], axis=1)

def seg_reverse(t):
    return jnp.concatenate([jnp.flip(t[:, :CTX_LEN], axis=1), jnp.flip(t[:, CTX_LEN:], axis=1)], axis=1)

def directional(fn, d, *args):
    if d == 0:
        return fn(*args)
    return seg_reverse(fn(*[seg_reverse(t) for t in args]))

def grid_transpose(t, rows, cols):
    b = t.shape[0]
    rest = t.shape[2:]
    return jnp.swapaxes(t.reshape((b, rows, cols) + rest), 1, 2).reshape((b, rows * cols) + rest)

def ssd_scan(x, dt, A, Bm, Cm):
    b, T, G, J, P = x.shape
    N = Bm.shape[-1]
    Q = SSM_CHUNK
    nc = T // Q
    x = x.reshape(b, nc, Q, G, J, P)
    dt = dt.reshape(b, nc, Q, G, J)
    Bm = Bm.reshape(b, nc, Q, G, N)
    Cm = Cm.reshape(b, nc, Q, G, N)
    xdt = x * dt[..., None]
    cs = jnp.cumsum(jnp.moveaxis(dt * A, 2, -1), axis=-1)
    mask = jnp.tril(jnp.ones((Q, Q), dtype=bool))
    Lmat = jnp.exp(jnp.where(mask, cs[..., :, None] - cs[..., None, :], -jnp.inf))
    cb = jnp.einsum('bclgn,bcsgn->bcgls', Cm, Bm)
    y_diag = jnp.einsum('bcgls,bcgjls,bcsgjp->bclgjp', cb, Lmat, xdt)
    decay_to_end = jnp.exp(cs[..., -1:] - cs)
    states = jnp.einsum('bcsgn,bcgjs,bcsgjp->bcgjpn', Bm, decay_to_end, xdt)
    chunk_decay = jnp.exp(cs[..., -1])

    def step(h, inp):
        st, dec = inp
        return dec[..., None, None] * h + st, h

    h0 = jnp.zeros((b, G, J, P, N), x.dtype)
    _, h_in = lax.scan(step, h0, (jnp.moveaxis(states, 1, 0), jnp.moveaxis(chunk_decay, 1, 0)))
    h_in = jnp.moveaxis(h_in, 0, 1)
    y_off = jnp.einsum('bclgn,bcgjpn,bcgjl->bclgjp', Cm, h_in, jnp.exp(cs))
    return (y_diag + y_off).reshape(b, T, G, J, P)

def rwkv7_scan(r, w, k, v, a, bvec):
    def step(S, inp):
        r_t, w_t, k_t, v_t, a_t, b_t = inp
        sa = jnp.einsum('bhvk,bhk->bhv', S, a_t)
        S = S * w_t[:, :, None, :] + sa[..., None] * b_t[:, :, None, :] + v_t[..., None] * k_t[:, :, None, :]
        return S, jnp.einsum('bhvk,bhk->bhv', S, r_t)

    bsz, T, H, N = r.shape
    S0 = jnp.zeros((bsz, H, N, N), r.dtype)
    seq = [jnp.moveaxis(t, 1, 0) for t in (r, w, k, v, a, bvec)]
    _, y = lax.scan(step, S0, seq)
    return jnp.moveaxis(y, 0, 1)

def token_mixer(h, w_in, ssm_conv_w, ssm_conv_b, ssm_dt_bias, ssm_a_log, ssm_d, ssm_norm, ssm_out,
                rwkv_conv_w, rwkv_w0, rwkv_w2, rwkv_a0, rwkv_a2, rwkv_g2, rwkv_k_k, rwkv_k_a, rwkv_r_k,
                rwkv_ln_w, rwkv_ln_b, rwkv_out, w_o):
    f32 = jnp.float32
    bsz, T, _ = h.shape
    z, xbc, dt_raw, rkv, w_dn, a_dn, g_dn, gate_pre = jnp.split(h @ w_in, _split_points(IN_SIZES), axis=-1)

    xbc = jax.nn.silu(seg_conv1d(xbc, ssm_conv_w) + ssm_conv_b)
    xs, Bm, Cm = jnp.split(xbc, [D_SSM, D_SSM + SSM_GROUPS * SSM_STATE], axis=-1)
    xs_h = xs.astype(f32).reshape(bsz, T, SSM_GROUPS, SSM_HEADS_PER_GROUP, SSM_HEAD_DIM)
    Bm = Bm.astype(f32).reshape(bsz, T, SSM_GROUPS, SSM_STATE)
    Cm = Cm.astype(f32).reshape(bsz, T, SSM_GROUPS, SSM_STATE)
    y_ssm = ssm_d.astype(f32).reshape(SSM_GROUPS, SSM_HEADS_PER_GROUP)[..., None] * xs_h
    for d in range(N_DIR):
        dt = jax.nn.softplus(dt_raw.astype(f32) + ssm_dt_bias[d]).reshape(bsz, T, SSM_GROUPS, SSM_HEADS_PER_GROUP)
        A = -jnp.exp(ssm_a_log[d].astype(f32)).reshape(SSM_GROUPS, SSM_HEADS_PER_GROUP)
        y_ssm = y_ssm + directional(lambda xx, dd, bb, cc: ssd_scan(xx, dd, A, bb, cc), d, xs_h, dt, Bm, Cm)
    y_ssm = y_ssm.reshape(bsz, T, D_SSM).astype(h.dtype) * jax.nn.silu(z)
    out_ssm = group_rmsnorm(y_ssm, SSM_GROUPS, ssm_norm) @ ssm_out

    r, k, v = jnp.split(seg_conv1d(rkv, rwkv_conv_w).astype(f32), 3, axis=-1)

    def heads(t):
        return t.reshape(bsz, T, RWKV_HEADS, RWKV_HEAD)

    kk = heads(k * rwkv_k_k)
    kk = kk / jnp.maximum(jnp.linalg.norm(kk, axis=-1, keepdims=True), 1e-12)
    w_dn = w_dn.reshape(bsz, T, N_DIR, LORA_W)
    a_dn = a_dn.reshape(bsz, T, N_DIR, LORA_A)
    ys, ks = [], []
    for d in range(N_DIR):
        w_log = -jax.nn.softplus(-(rwkv_w0[d] + jnp.tanh(w_dn[:, :, d]) @ rwkv_w2[d])) - 0.5
        decay = jnp.exp(-jnp.exp(w_log.astype(f32)))
        a = jax.nn.sigmoid((rwkv_a0[d] + a_dn[:, :, d] @ rwkv_a2[d]).astype(f32))
        kd = k * (1 + (a - 1) * rwkv_k_a)
        ys.append(directional(rwkv7_scan, d, heads(r), heads(decay), heads(kd), heads(v), -kk, kk * heads(a)))
        ks.append(kd)
    yh = ys[0] + ys[1]
    mu = jnp.mean(yh, axis=-1, keepdims=True)
    var = jnp.mean(jnp.square(yh - mu), axis=-1, keepdims=True)
    yh = (yh - mu) * lax.rsqrt(var + RWKV_LN_EPS)
    y_rw = yh.reshape(bsz, T, D_RWKV) * rwkv_ln_w + rwkv_ln_b
    bonus = jnp.sum(heads(r) * heads(ks[0] + ks[1]) * rwkv_r_k, axis=-1, keepdims=True) * heads(v)
    y_rw = y_rw + bonus.reshape(bsz, T, D_RWKV)
    g = jax.nn.sigmoid(g_dn) @ rwkv_g2
    out_rw = (y_rw.astype(h.dtype) * g) @ rwkv_out

    gate_ssm, gate_rw = jnp.split(jax.nn.sigmoid(gate_pre), N_BRANCH, axis=-1)
    return (gate_ssm * out_ssm + gate_rw * out_rw) @ w_o

def conv_ffn(h, w_up, conv_w, conv_b, w_down, on_grid):
    gate_pre, val = jnp.split(h @ w_up, 2, axis=-1)
    if on_grid:
        gate_pre = dwconv2d_grid(gate_pre, conv_w) + conv_b
    else:
        gate_pre = dwconv1d(gate_pre, conv_w[FFN_CONV // 2]) + conv_b
    return (jax.nn.gelu(gate_pre, approximate=True) * val) @ w_down

def setup_inputs(seed: int = 0) -> dict:
    key = jax.random.key(seed)
    ks = jax.random.split(key, 35)
    f32 = jnp.float32

    def nrm(k, shape, scale):
        return jax.random.normal(k, shape, f32) * scale

    def gain(k, shape):
        return 1.0 + 0.05 * jax.random.normal(k, shape, f32)

    L, D = DEPTH, D_MODEL
    dt0 = jnp.exp(jax.random.uniform(ks[13], (L, N_DIR, SSM_HEADS), f32, np.log(1e-3), np.log(1e-1)))
    return {
        "x": nrm(ks[0], (BATCH, SEQ, D), 1.0),
        "c": nrm(ks[1], (BATCH, D), 1.0),
        "ctx": nrm(ks[2], (BATCH, CTX_LEN, D), 1.0),
        "c_ctx": nrm(ks[3], (D,), 1.0),
        "ada_w": nrm(ks[4], (L, D, 6 * D), 0.5 * D ** -0.5),
        "ada_b": nrm(ks[5], (L, 6 * D), 0.02),
        "norm_mix_pre": gain(ks[6], (L, D)),
        "norm_mix_post": gain(ks[7], (L, D)),
        "norm_ffn_pre": gain(ks[8], (L, D)),
        "norm_ffn_post": gain(ks[9], (L, D)),
        "w_in": nrm(ks[10], (L, D, D_IN), D ** -0.5),
        "ssm_conv_w": nrm(ks[11], (L, SSM_CONV, D_XBC), SSM_CONV ** -0.5),
        "ssm_conv_b": nrm(ks[12], (L, D_XBC), 0.02),
        "ssm_dt_bias": jnp.log(jnp.expm1(dt0)),
        "ssm_a_log": jnp.log(jax.random.uniform(ks[14], (L, N_DIR, SSM_HEADS), f32, 1.0, 16.0)),
        "ssm_d": gain(ks[15], (L, SSM_HEADS)),
        "ssm_norm": gain(ks[16], (L, D_SSM)),
        "ssm_out": nrm(ks[17], (L, D_SSM, D), D_SSM ** -0.5),
        "rwkv_conv_w": nrm(ks[18], (L, RWKV_CONV, 3 * D_RWKV), RWKV_CONV ** -0.5),
        "rwkv_w0": jax.random.uniform(ks[19], (L, N_DIR, D_RWKV), f32, -4.0, 1.0),
        "rwkv_w2": nrm(ks[20], (L, N_DIR, LORA_W, D_RWKV), 0.1 * LORA_W ** -0.5),
        "rwkv_a0": nrm(ks[21], (L, N_DIR, D_RWKV), 0.1),
        "rwkv_a2": nrm(ks[22], (L, N_DIR, LORA_A, D_RWKV), 0.1 * LORA_A ** -0.5),
        "rwkv_g2": nrm(ks[23], (L, LORA_G, D_RWKV), LORA_G ** -0.5),
        "rwkv_k_k": 0.85 + 0.05 * jax.random.normal(ks[24], (L, D_RWKV), f32),
        "rwkv_k_a": gain(ks[25], (L, D_RWKV)),
        "rwkv_r_k": nrm(ks[26], (L, RWKV_HEADS, RWKV_HEAD), 0.1),
        "rwkv_ln_w": gain(ks[27], (L, D_RWKV)),
        "rwkv_ln_b": nrm(ks[28], (L, D_RWKV), 0.02),
        "rwkv_out": nrm(ks[29], (L, D_RWKV, D), D_RWKV ** -0.5),
        "w_o": nrm(ks[30], (L, D, D), D ** -0.5),
        "ffn_w_in": nrm(ks[31], (L, D, 2 * D_FF), D ** -0.5),
        "ffn_conv_w": nrm(ks[32], (L, FFN_CONV, FFN_CONV, D_FF), 1.0 / FFN_CONV),
        "ffn_conv_b": nrm(ks[33], (L, D_FF), 0.02),
        "ffn_w_out": nrm(ks[34], (L, D_FF, D), D_FF ** -0.5),
    }

def reference(x, c, ctx, c_ctx, ada_w, ada_b, norm_mix_pre, norm_mix_post, norm_ffn_pre, norm_ffn_post,
              w_in, ssm_conv_w, ssm_conv_b, ssm_dt_bias, ssm_a_log, ssm_d, ssm_norm, ssm_out,
              rwkv_conv_w, rwkv_w0, rwkv_w2, rwkv_a0, rwkv_a2, rwkv_g2, rwkv_k_k, rwkv_k_a, rwkv_r_k,
              rwkv_ln_w, rwkv_ln_b, rwkv_out, w_o, ffn_w_in, ffn_conv_w, ffn_conv_b, ffn_w_out):
    rows = x.shape[1] // GRID_W
    xl, xc = x, ctx
    for i in range(DEPTH):
        last = i == DEPTH - 1
        mod_l = [m[:, None, :] for m in adaln(c, ada_w[i], ada_b[i])]
        mod_c = adaln(c_ctx, ada_w[i], ada_b[i])

        hl = modulate(rmsnorm(xl, norm_mix_pre[i]), mod_l[0], mod_l[1])
        hc = modulate(rmsnorm(xc, norm_mix_pre[i]), mod_c[0], mod_c[1])
        col_major = i % 2 == 1
        if col_major:
            hl = grid_transpose(hl, rows, GRID_W)
        y = token_mixer(jnp.concatenate([hc, hl], axis=1), w_in[i], ssm_conv_w[i], ssm_conv_b[i],
                        ssm_dt_bias[i], ssm_a_log[i], ssm_d[i], ssm_norm[i], ssm_out[i],
                        rwkv_conv_w[i], rwkv_w0[i], rwkv_w2[i], rwkv_a0[i], rwkv_a2[i], rwkv_g2[i],
                        rwkv_k_k[i], rwkv_k_a[i], rwkv_r_k[i], rwkv_ln_w[i], rwkv_ln_b[i], rwkv_out[i], w_o[i])
        yc, yl = y[:, :CTX_LEN], y[:, CTX_LEN:]
        if col_major:
            yl = grid_transpose(yl, GRID_W, rows)
        xl = xl + mod_l[2] * rmsnorm(yl, norm_mix_post[i])

        hl = modulate(rmsnorm(xl, norm_ffn_pre[i]), mod_l[3], mod_l[4])
        fl = conv_ffn(hl, ffn_w_in[i], ffn_conv_w[i], ffn_conv_b[i], ffn_w_out[i], True)
        xl = xl + mod_l[5] * rmsnorm(fl, norm_ffn_post[i])

        if not last:
            xc = xc + mod_c[2] * rmsnorm(yc, norm_mix_post[i])
            hc = modulate(rmsnorm(xc, norm_ffn_pre[i]), mod_c[3], mod_c[4])
            fc = conv_ffn(hc, ffn_w_in[i], ffn_conv_w[i], ffn_conv_b[i], ffn_w_out[i], False)
            xc = xc + mod_c[5] * rmsnorm(fc, norm_ffn_post[i])
    return xl


_drawn_inputs = setup_inputs


def setup_inputs(seed=0):
    import zlib

    import numpy as np

    out = dict(_drawn_inputs(seed))
    spreads = {}
    factors = {'norm_mix_post': 2.667,
     'norm_ffn_post': 2.713,
     'ssm_conv_b': 6.119,
     'ssm_d': 8.0,
     'ssm_norm': 3.439,
     'rwkv_w2': 8.0,
     'rwkv_a0': 5.248,
     'rwkv_a2': 4.682,
     'rwkv_k_k': 24.049,
     'rwkv_k_a': 3.717,
     'rwkv_ln_w': 6.073,
     'rwkv_ln_b': 23.479,
     'ffn_conv_b': 6.619}
    for name, (base, spread) in spreads.items():
        noise = np.random.default_rng([zlib.crc32(name.encode()), seed]).standard_normal(out[name].shape)
        drawn = base * np.exp(spread * noise) if base else spread * noise
        out[name] = jnp.asarray(drawn.astype(out[name].dtype))
    for name, factor in factors.items():
        out[name] = (out[name] * factor).astype(out[name].dtype)
    return out
```

```python
from contextlib import ExitStack, contextmanager

import numpy as np
import concourse.bass as bass
from concourse import mybir

F32 = mybir.dt.float32
ACT = mybir.ActivationFunctionType
ALU = mybir.AluOpType

P = 128
DEPTH = 2
D = 1024
KT = D // P
CTX, LAT = 256, 256
T = CTX + LAT
GRID_W = 64
ROWS = LAT // GRID_W
EPS = 1e-6
D_SSM, HEADS, GROUPS, HPG = 2048, 32, 4, 8
XS_T = D_SSM // P
XBC_T = XS_T + 8
Q = 128
NCH = T // Q
RC = 64
NRC = T // RC
RK_T = 24
LN_EPS = 64e-5
WSCALE = float(np.exp(-0.5))
FF_T = 2816 // P
SLOTS = 4
WSLOTS = 4
WBLK = 2048

B_ADA, B_XBC, B_Z, B_SO, B_GS, B_RKV, B_LORA, B_RO, B_GR, B_WO, B_FI, B_FO = 24, 12, 8, 8, 4, 12, 2, 4, 4, 4, 22, 11
NBLK = DEPTH * (B_ADA + B_XBC + B_Z + B_SO + B_GS + B_RKV + B_LORA + B_RO + B_GR + B_WO + B_FI + B_FO)

COLS, _n = {}, 0
for _name, _w in (("npre", 8), ("npost", 8), ("fpre", 8), ("fpost", 8), ("scw", 72), ("scb", 24), ("snorm", 16),
                  ("rcw", 72), ("w0", 16), ("a0", 16), ("kk", 8), ("ka", 8), ("rk", 8), ("lnw", 8), ("lnb", 8),
                  ("fcw", 9 * FF_T), ("fcb", FF_T), ("adab", 48), ("dskip", 16)):
    COLS[_name] = _n
    _n += _w
PARAMS = _n

CCOL, _n = {}, 0
for _name, _w in (("ident", 128), ("ones", 128), ("headones", 128), ("tri", 256), ("mask2", 256), ("strict2", 256),
                  ("lvl", 12 * 64), ("id64", 64)):
    CCOL[_name] = _n
    _n += _w
CONSTS = _n

SSD_ORDER = ((0, 1, 2, 3), (1, 0, 3, 2))
RW_ORDER = ((0, 1, 2, 3, 4, 5, 6, 7), (3, 2, 1, 0, 7, 6, 5, 4))


PRIMED = ("slot_free", "y_ready", "yz_ready", "dve_done")


class Count:

    def __init__(self, sem, unit, primed):
        self.sem, self.unit, self.n, self.primed, self.i, self.per = sem, unit, primed, primed, None, 0

    def _value(self):
        if self.i is None or not self.per:
            return self.n
        assert self.n > 0, "a wait on a register's value stays above zero: prime the semaphore"
        return self.n + self.i * self.per

    def sent(self):
        self.n += self.unit
        return self.sem, self.unit

    def next(self):
        self.n += self.unit
        return self.sem, self._value()

    def so_far(self):
        return self.sem, self._value()


class Engine:

    def __init__(self, e, name, sems, table):
        self.e, self.name, self.sems, self.table = e, name, sems, table
        self.counts, self.loops, self.step_no, self.wblk, self.own = {}, 0, 0, 0, f"{name}_done"
        self.last = None

    def count(self, name):
        if name not in self.counts:
            c = Count(self.sems[name], 16 if name.startswith(("w_loaded", "dma")) else 1, int(name.startswith(PRIMED)))
            if self.loop_now:
                c.i, c.per = self.loop_now[0], self.loop_now[1].get(name, 0)
            self.counts[name] = c
        return self.counts[name]

    loop_now = None

    def done(self, name=None):
        c = self.count(name or self.own)
        out = c.sent()
        self.last = (c.sem, c._value())
        return out

    def mine(self):
        return self.last or self.count(self.own).so_far()

    def slot(self):
        s = self.step_no % SLOTS
        self.step_no += 1
        return s

    def skip(self, n=1):
        for _ in range(n):
            s = self.slot()
            self.count(f"slot_full{s}").n += 1
            self.count(f"slot_free{s}").n += 1

    def full(self):
        s = self.slot()
        self.count(f"slot_free{s}").n += 1
        return s, self.count(f"slot_full{s}").next()

    def freed(self, s):
        c = self.count(f"slot_free{s}")
        self.last = (c.sem, c._value())
        return c.sem, 1

    @contextmanager
    def loop(self, trips):
        key = (self.name, self.loops)
        self.loops += 1
        per = self.table.get(key, {})
        start = {k: c.n for k, c in self.counts.items()}
        at, wat = self.step_no, self.wblk
        with self.e.Fori(0, trips) as i:
            self.loop_now = (i, per)
            for k, c in self.counts.items():
                c.i, c.per = i, per.get(k, 0)
            self.last = None
            yield i
        self.loop_now, self.last = None, None
        start = {k: start.get(k, c.primed) for k, c in self.counts.items()}
        found = {k: c.n - start[k] for k, c in self.counts.items() if c.n != start[k]}
        assert not per or per == found, (key, per, found)
        self.table[key] = found
        for k, c in self.counts.items():
            c.i, c.per = None, 0
            c.n = start[k] + trips * found.get(k, 0)
        assert (self.step_no - at) % SLOTS == 0 and (self.wblk - wat) % WSLOTS == 0, (key, self.step_no - at)
        self.step_no, self.wblk = at, wat


def build(nc, ins, out, table):
    stream, x_in, cond_in, par_in, const_in, headp_in, wdt_in, lora_in = ins
    x_mid = nc.dram_tensor("x_mid", (P, KT * T), F32, kind="Internal").ap()

    with ExitStack() as ctx:
        def sb(name, *shape):
            return ctx.enter_context(nc.sbuf_tensor(name, [P, *shape], F32))

        W = sb("W", WSLOTS, WBLK)
        A = sb("A", RK_T, T)
        hT = sb("hT", KT, T)
        O = sb("O", KT, T)
        lo = sb("lo", 3, T)
        scr = sb("scr", 16384)
        mod = sb("mod", 48, 2)
        par = sb("par", DEPTH, PARAMS)
        cst = sb("cst", CONSTS)
        headp = sb("headp", DEPTH, 2, 2, HEADS)
        wdt = sb("wdt", DEPTH, KT, HEADS)
        cond = sb("cond", KT, 2)
        gsc = sb("gsc", KT, 2)
        rst = sb("rst", T)
        lst = sb("lst", 3, P)
        rows = lo
        ps = ctx.enter_context(nc.psum_tensor("ps", [P, 2 * SLOTS, 512], F32))

        names = ([f"slot_full{s}" for s in range(SLOTS)] + [f"slot_free{s}" for s in range(SLOTS)]
                 + [f"w_loaded{s}" for s in range(WSLOTS)]
                 + ["w_used", "pe_passed", "act_passed", "pe_done", "act_done", "dve_done", "pool_done",
                    "dma_const", "dma_x", "dma_wa", "dma_g2", "dma_out",
                    "cond_ready", "row_ready", "sq_ready", "std_ready", "norm_ready", "h_ctx_ready", "h_lat_ready",
                    "tap_ready", "conv_ready", "conv_silu", "abs_ready", "exp_ready", "log_ready", "expA_ready",
                    "dta_ready", "cs_ready", "dec_in_ready", "dec_ready", "wdec_ready", "staged", "xw_ready", "btok_ready",
                    "h_ssd_ready", "cbm_ready", "diff_ready", "e_ready", "ec_ready", "xdt_ready", "ct_ready", "w_ready",
                    "y_ready", "zs_ready", "yz_ready", "ysq_ready", "yn_ready", "out_ready", "gate_ready", "o_ready",
                    "lora_ready", "kksq_ready", "kkmax_ready", "kkstd_ready", "vs_ready", "vtok_ready", "sa_ready",
                    "cum_ready", "exps_ready", "ops_ready", "tok_ready", "aa_ready", "xn_ready", "q_ready", "r_ready",
                    "ug_ready", "mt_ready", "kv_ready", "s_ready", "rp_ready", "yb_ready", "yc_ready", "ycsq_ready",
                    "ystd_ready", "yr_ready", "loop_ready", "wo_ready", "gelu_ready", "tap2_ready", "ffn_ready",
                    "fo_ready", "x_ready", "x_used", "scr_free"])
        sems = {n: ctx.enter_context(nc.semaphore(n)) for n in names}

        def cc(name, w=None, off=0):
            return cst[:, CCOL[name] + off:CCOL[name] + off + w]

        ident, ones, headones = cc("ident", P), cc("ones", P), cc("headones", P)
        tri = [cc("tri", P, P * d) for d in range(2)]
        mask2 = [cc("mask2", P, P * d) for d in range(2)]
        lvl = [[cc("lvl", RC, RC * (2 * m + d)) for d in range(2)] for m in range(6)]
        id64 = cc("id64", RC)
        reset = rst[:, :]

        def col(L, name, k=0, w=1):
            return par[:, L, COLS[name] + k:COLS[name] + k + w]

        def colr(L, name, k):
            return par[:, L, bass.ds(COLS[name] + k, 1)]

        def span(a, w):
            return scr[:, a:a + w]

        X = span(0, KT * T).rearrange("p (k t) -> p k t", k=KT)
        SQ = span(KT * T, KT * T).rearrange("p (k t) -> p k t", k=KT)

        YSQ = [span(2048 * g, 2048).rearrange("p (k t) -> p k t", k=4) for g in range(GROUPS)]
        GR = [span(8192 + 512 * g, 512) for g in range(GROUPS)]
        ZS = span(12288, 2048).rearrange("p (r m t) -> p r m t", r=2, m=2)
        SG = span(0, KT * T).rearrange("p (k t) -> p k t", k=KT)

        Wb = [span(1024 * d, 1024).rearrange("p (h l) -> p h l", h=HPG) for d in range(2)]
        xg = span(0, 2048).rearrange("p (j t) -> p j t", j=4)
        Cb = [span(2048 + 1024 * d, 1024).rearrange("p (h l) -> p h l", h=HPG) for d in range(2)]
        Bg, Cg = span(4096, T), span(4608, T)
        btok = span(5120, T).rearrange("p (c n) -> p c n", c=NCH)
        xtok = span(5632, 2048).rearrange("p (c h x) -> p c h x", c=NCH, h=HPG)
        Hs = [[span(7680 + 1536 * d + 512 * o, 512).rearrange("p (h x) -> p h x", h=HPG) for o in range(3)] for d in range(2)]
        xdt = [span(10752 + 512 * d, 512).rearrange("p (h x) -> p h x", h=HPG) for d in range(2)]
        xw = [span(11776 + 512 * d, 512).rearrange("p (h x) -> p h x", h=HPG) for d in range(2)]
        cbm = [span(12800 + 512 * d, 512).rearrange("p (c l) -> p c l", c=NCH) for d in range(2)]
        small = [span(13824 + 256 * j, 256) for j in range(8)]
        dtv, dta, ncs, wde, dec, sm_a, sm_b, sm_c = small
        dtag = span(13824 + 2048, 64).rearrange("p (d c h) -> p d c h", d=2, c=NCH)
        expA = span(13824 + 2048 + 64, 64)

        def heads4(ap):
            return ap.rearrange("p (d c h) -> p d c h", d=2, c=NCH)

        RD = 6144
        at = [span(RD * d, 512) for d in range(2)]
        rt = [span(RD * d + 512, 512) for d in range(2)]
        bt = [span(RD * d + 1024, 512) for d in range(2)]
        kt = [span(RD * d + 1536, 512) for d in range(2)]
        art = [span(RD * d, 1024).rearrange("p (two c t) -> p c two t", two=2, c=NRC) for d in range(2)]

        def e8(ap):
            return ap.rearrange("p (e t) -> p e t", e=8)

        Xi = [e8(at[d]) for d in range(2)]
        Ni = [e8(bt[d]) for d in range(2)]
        Qi = [e8(kt[d]) for d in range(2)]
        AAb = [span(RD * d + 2048, 1024).rearrange("p (e a t) -> p e a t", e=8, a=2) for d in range(2)]
        AAk = [span(RD * d + 3072, 1024).rearrange("p (e a t) -> p e a t", e=8, a=2) for d in range(2)]
        RA = [span(RD * d + 4096, 1024).rearrange("p (e a t) -> p e a t", e=8, a=2) for d in range(2)]
        RAq = [span(RD * d + 4096, 1024).rearrange("p (h q a t) -> p q h a t", h=2, q=4, a=2) for d in range(2)]
        MT = [e8(span(RD * d + 4096, 512)) for d in range(2)]
        Kv = [e8(span(RD * d + 4608, 512)) for d in range(2)]
        btk = [span(RD * d + 5120, 512).rearrange("p (q h k) -> p q h k", q=4, h=2) for d in range(2)]
        ktk = [span(RD * d + 5632, 512).rearrange("p (q h k) -> p q h k", q=4, h=2) for d in range(2)]
        sg = [span(RD * d + 2048, 512) for d in range(2)]
        pre = [span(RD * d + 2560, 512) for d in range(2)]
        exc = [span(RD * d + 3072, 512) for d in range(2)]
        inc = [span(RD * d + 3584, 512) for d in range(2)]
        asg = [span(RD * d + 4096, 512) for d in range(2)]
        kd = [span(RD * d + 4608, 512) for d in range(2)]
        vtk = span(12288, 512).rearrange("p (q h k) -> p q h k", q=4, h=2)
        vS, kkn, kds, yac, tm1, tm2 = [span(12800 + 512 * j, 512) for j in range(6)]
        wc = [span(15872 + 8 * d, 8) for d in range(2)]

        def by_pq(ap):
            return ap.rearrange("p (q two t) -> p two q t", two=2, t=RC)

        def seg2(ap):
            return ap.rearrange("p (s t) -> p s t", s=2)

        N_OUT = {0: (0, T), 1: (CTX, T)}

        block = ctx.enter_context(nc.Block())

        @block.sync
        def _(sp):
            E = Engine(sp, "sp", sems, table)
            wv = stream
            for b in range(WSLOTS):
                sp.dma_start(W[:, b, :], wv[b]).then_inc(*E.count(f"w_loaded{b}").sent())
            groups = NBLK // WSLOTS
            with sp.Fori(1, groups) as i:
                for j in range(WSLOTS):
                    sp.wait_ge(sems["w_used"], i * WSLOTS + (j - WSLOTS + 2))
                    sp.dma_start(W[:, j, :], wv[i * WSLOTS + j]).then_inc(sems[f"w_loaded{j}"], 16)
            for b in range(groups * WSLOTS, NBLK):
                sp.wait_ge(sems["w_used"], b - WSLOTS + 2)
                sp.dma_start(W[:, b % WSLOTS, :], wv[b]).then_inc(sems[f"w_loaded{b % WSLOTS}"], 16)

        @block.tensor
        def _(pe):
            E = Engine(pe, "pe", sems, table)

            def mm(o, l, r, start=True, stop=True):
                return pe.matmul(o, l, r, start=start, stop=stop)

            def passed():
                if E.loop_now:
                    pe.sem_inc(sems["pe_passed"], 1)

            def take():
                s = E.slot()
                pe.wait_ge(*E.count(f"slot_free{s}").so_far())
                passed()
                E.count(f"slot_free{s}").n += 1
                return s, ps[:, 2 * s:2 * s + 2, :]

            def full(s):
                return E.count(f"slot_full{s}").sent()

            def weights():
                s = E.wblk % WSLOTS
                E.wblk += 1
                pe.wait_ge(*E.count(f"w_loaded{s}").next())
                return W[:, s, :]

            def dense_block(src, lo_, hi, tiles=2):
                w = weights().rearrange("p (k m) -> p k m", k=KT)
                s, o = take()
                for m in range(tiles):
                    for k in range(KT):
                        ins_ = mm(o[:, m, 0:hi - lo_], w[:, k, P * m:P * (m + 1)], src[:, k, lo_:hi], k == 0, k == KT - 1)
                        if m == 0 and k == 0:
                            ins_.then_inc(*E.count("w_used").sent())
                ins_.then_inc(*full(s))

            def dense(src, blocks, lo_=0, hi=T):
                trips, rest = divmod(blocks, WSLOTS)
                if trips > 1:
                    with E.loop(trips):
                        for _ in range(WSLOTS):
                            dense_block(src, lo_, hi)
                else:
                    rest = blocks
                for _ in range(rest):
                    dense_block(src, lo_, hi)

            def channel_sum(src, n, lo_=0, hi=T):
                s, o = take()
                for k in range(n):
                    i_ = mm(o[:, 0, 0:hi - lo_], ones, src[:, k, lo_:hi], k == 0, k == n - 1)
                i_.then_inc(*full(s))

            def adaln():
                with E.loop(6):
                    for n in range(2):
                        s, o = take()
                        for half in range(2):
                            w = weights().rearrange("p (k n) -> p k n", k=4)
                            for k in range(4):
                                i_ = mm(o[0:2, 0, :], cond[:, 4 * half + k, :], w[:, k, :], half + k == 0, half == 1 and k == 3)
                                if k == 0:
                                    i_.then_inc(*E.count("w_used").sent())
                        i_.then_inc(*full(s))
                    for n in range(2):
                        s, o = take()
                        pe.wait_ge(*E.count("row_ready").next())
                        passed()
                        for j in range(4):
                            i_ = pe.transpose(o[:, 0, 2 * j:2 * j + 2], rows[0:2, n, P * j:P * (j + 1)], ident[0:2, 0:2])
                        i_.then_inc(*full(s))

            def ssd():
                s, o = take()
                for c in range(NCH):
                    for k in range(KT):
                        i_ = mm(o[:, 0, HEADS * c:HEADS * (c + 1)], hT[:, k, Q * c:Q * (c + 1)], wdt[:, L, k, :], k == 0, k == KT - 1)
                i_.then_inc(*full(s))
                pe.wait_ge(*E.count("dta_ready").next())
                s, o = take()
                for d in range(2):
                    mm(o[:, 0, P * d:P * (d + 1)], tri[d], dta[:, P * d:P * (d + 1)])
                mm(o[:, 1, 0:256], ones, dta).then_inc(*full(s))
                with E.loop(GROUPS):
                    pe.wait_ge(*E.count("staged").next())
                    for part in ((("B", 0),), (("x", 0), ("x", 1)), (("x", 2),), (("x", 3),)):
                        s, o = take()
                        for bank, (what, c) in enumerate(part):
                            for j in range(4):
                                src = Bg[:, Q * j:Q * (j + 1)] if what == "B" else xg[:, j, Q * c:Q * (c + 1)]
                                i_ = pe.transpose(o[:, bank, P * j:P * (j + 1)], src, ident)
                        i_.then_inc(*full(s))
                    for o_ in range(3):
                        s, o = take()
                        for d in range(2):
                            pe.wait_ge(*E.count("xw_ready").next())
                            if o_ == 0 and d == 0:
                                pe.wait_ge(*E.count("btok_ready").next())
                            i_ = mm(o[:, d, :], btok[:, SSD_ORDER[d][o_], :], xw[d])
                        i_.then_inc(*full(s))
                    s, o = take()
                    for c in range(NCH):
                        i_ = mm(o[:, 0, Q * c:Q * (c + 1)], Bg[:, Q * c:Q * (c + 1)], Cg[:, Q * c:Q * (c + 1)])
                    i_.then_inc(*full(s))
                    for c in range(NCH):
                        for d in range(2):
                            s, o = take()
                            for h in range(HPG):
                                i_ = mm(o[:, h // 4, P * (h % 4):P * (h % 4 + 1)],
                                        dtag[:, d, c, h:h + 1].to_broadcast((P, P)), tri[d])
                            i_.then_inc(*full(s))
                        s, o = take()
                        pe.wait_ge(*E.count("w_ready").next())
                        pe.wait_ge(*E.count("ct_ready").next())
                        pe.wait_ge(*E.count("xdt_ready").next())
                        for h in range(HPG):
                            y = o[64 * (h % 2):64 * (h % 2) + 64, 0, P * (h // 2):P * (h // 2 + 1)]
                            terms = []
                            for d in range(2):
                                terms.append((xdt[d][:, h, :], Wb[d][:, h, :]))
                                k = SSD_ORDER[d].index(c)
                                if k:
                                    terms.append((Hs[d][k - 1][:, h, :], Cb[d][:, h, :]))
                            for n, (l, r) in enumerate(terms):
                                i_ = mm(y, l, r, n == 0, n == len(terms) - 1)
                        i_.then_inc(*full(s))

            def rwkv():
                with E.loop(KT):
                    s, o = take()
                    pe.wait_ge(*E.count("kksq_ready").next())
                    mm(o[:, 0, :], headones, tm1)
                    pe.wait_ge(*E.count("vs_ready").next())
                    for q in range(4):
                        i_ = pe.transpose(o[:, 1, P * q:P * (q + 1)], vS[:, P * q:P * (q + 1)], ident)
                    i_.then_inc(*full(s))
                    for d in range(2):
                        s, o = take()
                        half = slice(64 * d, 64 * d + 64)
                        if d == 0:
                            pe.wait_ge(*E.count("dma_wa").next())
                        mm(o[:, 0, :], lst[half, 0, :], lo[half, 0, :])
                        mm(o[:, 1, :], lst[half, 1, :], lo[half, 1, :]).then_inc(*full(s))
                    for d in range(2):
                        pe.wait_ge(*E.count("ops_ready").next())
                        s, o = take()
                        for q in range(4):
                            pe.transpose(o[:, 0, P * q:P * (q + 1)], at[d][:, P * q:P * (q + 1)], ident)
                            i_ = pe.transpose(o[:, 1, P * q:P * (q + 1)], bt[d][:, P * q:P * (q + 1)], ident)
                        i_.then_inc(*full(s))
                        s, o = take()
                        for q in range(4):
                            i_ = pe.transpose(o[:, 0, P * q:P * (q + 1)], kt[d][:, P * q:P * (q + 1)], ident)
                        i_.then_inc(*full(s))
                        for src in (bt, kt):
                            s, o = take()
                            for h in range(2):
                                hs = slice(64 * h, 64 * h + 64)
                                for p in range(2):
                                    for q in range(4):
                                        c = 2 * q + p
                                        i_ = mm(o[64 * p:64 * p + 64, h, P * q:P * (q + 1)].rearrange("p (a t) -> p a t", a=2),
                                                src[d][hs, RC * c:RC * (c + 1)], art[d][hs, c])
                            i_.then_inc(*full(s))

                    def each(o, bank, l, r, w=RC, off=0):
                        for p in range(2):
                            pp = slice(64 * p, 64 * p + 64)
                            for e in range(8):
                                i2 = mm(o[pp, bank + (e * w) // 512, (e * w) % 512:(e * w) % 512 + w], l(pp, e), r(pp, e))
                        return i2

                    for d in range(2):
                        pe.wait_ge(*E.count("aa_ready").next())
                        s, o = take()
                        each(o, 0, lambda pp, e: AAb[d][pp, e, 0, :], lambda pp, e: id64[pp]).then_inc(*full(s))
                    for m in range(1, 6):
                        for d in range(2):
                            pe.wait_ge(*E.count("xn_ready").next())
                            s, o = take()
                            each(o, 0, lambda pp, e: AAb[d][pp, e, 0, :], lambda pp, e: Xi[d][pp, e, :]).then_inc(*full(s))
                        for d in range(2):
                            pe.wait_ge(*E.count("q_ready").next())
                            s, o = take()
                            i_ = each(o, 0, lambda pp, e: Qi[d][pp, e, :], lambda pp, e: Ni[d][pp, e, :])
                            if m < 5:
                                i_ = each(o, 1, lambda pp, e: Ni[d][pp, e, :], lambda pp, e: Qi[d][pp, e, :])
                            i_.then_inc(*full(s))
                    for d in range(2):
                        if d == 0:
                            pe.wait_ge(*E.count("vtok_ready").next())
                        s, o = take()
                        each(o, 0, lambda pp, e: AAk[d][pp, e, 0, :], lambda pp, e: vtk[pp, e % 4, e // 4, :]).then_inc(*full(s))
                    for d in range(2):
                        pe.wait_ge(*E.count("xn_ready").next())
                        pe.wait_ge(*E.count("r_ready").next())
                        pe.wait_ge(*E.count("tok_ready").next())
                        s, o = take()
                        each(o, 0, lambda pp, e: Ni[d][pp, e, :], lambda pp, e: RA[d][pp, e], w=P).then_inc(*full(s))

                    def cross(o, terms):
                        for p in range(2):
                            pp = slice(64 * p, 64 * p + 64)
                            for h in range(2):
                                for q in range(4):
                                    for n, (l, r) in enumerate(terms):
                                        i2 = mm(o[64 * h:64 * h + 64, p, RC * q:RC * (q + 1)], l(pp, h, q), r(pp, h, q),
                                                n == 0, n == len(terms) - 1)
                        return i2

                    for d in range(2):
                        pe.wait_ge(*E.count("ug_ready").next())
                        s, o = take()
                        cross(o, [(lambda pp, h, q: Qi[d][pp, 4 * h + q, :], lambda pp, h, q: btk[d][pp, q, h, :])]).then_inc(*full(s))
                    for d in range(2):
                        s, o = take()
                        cross(o, [(lambda pp, h, q: btk[d][pp, q, h, :], lambda pp, h, q: Xi[d][pp, 4 * h + q, :]),
                                  (lambda pp, h, q: ktk[d][pp, q, h, :], lambda pp, h, q: vtk[pp, q, h, :])]).then_inc(*full(s))
                    for k in range(2, NRC):
                        for d in range(2):
                            prev = RW_ORDER[d][k - 1]
                            pe.wait_ge(*E.count("s_ready").next())
                            s, o = take()
                            for h in range(2):
                                hs = slice(64 * h, 64 * h + 64)
                                i_ = mm(o[hs, 0, 0:RC], MT[d][hs, prev, :], Ni[d][hs, prev, :])
                            i_.then_inc(*full(s))
                    for d in range(2):
                        s, o = take()
                        cross(o, [(lambda pp, h, q: Qi[d][pp, 4 * h + q, :], lambda pp, h, q: AAb[d][pp, 4 * h + q, 1, :])]).then_inc(*full(s))
                    for d in range(2):
                        s, o = take()
                        cross(o, [(lambda pp, h, q: Xi[d][pp, 4 * h + q, :], lambda pp, h, q: AAb[d][pp, 4 * h + q, 1, :]),
                                  (lambda pp, h, q: vtk[pp, q, h, :], lambda pp, h, q: AAk[d][pp, 4 * h + q, 1, :])]).then_inc(*full(s))
                    s, o = take()
                    for d in range(2):
                        pe.wait_ge(*E.count("s_ready").next())
                        pe.wait_ge(*E.count("rp_ready").next())
                        passed()
                        for h in range(2):
                            hs = slice(64 * h, 64 * h + 64)
                            for c in range(NRC):
                                i_ = mm(o[hs, d, RC * c:RC * (c + 1)], Ni[d][hs, c, :], rt[d][hs, RC * c:RC * (c + 1)])
                    i_.then_inc(*full(s))
                    s, o = take()
                    pe.wait_ge(*E.count("yb_ready").next())
                    mm(o[:, 0, :], headones, yac)
                    mm(o[:, 1, :], headones, tm1).then_inc(*full(s))
                    s, o = take()
                    pe.wait_ge(*E.count("ycsq_ready").next())
                    pe.wait_ge(*E.count("dma_g2").next())
                    mm(o[:, 0, :], headones, vS)
                    mm(o[:, 1, :], lst[:, 2, :], lo[:, 2, :]).then_inc(*full(s))

            def ffn_down(lo_, hi):
                slots = [take() for _ in range(SLOTS)]

                def blk(first, last):
                    w = weights().rearrange("p (k m) -> p k m", k=2)
                    return w

                for b in range(B_FO):
                    w = weights().rearrange("p (k m) -> p k m", k=2)
                    for k in range(2):
                        for m in range(8):
                            s, o = slots[m // 2]
                            i_ = mm(o[:, m % 2, 0:hi - lo_], w[:, k, P * m:P * (m + 1)], A[:, 2 * b + k, lo_:hi],
                                    b + k == 0, b == B_FO - 1 and k == 1)
                            if k == 0 and m == 0:
                                i_.then_inc(*E.count("w_used").sent())
                            if b == B_FO - 1 and k == 1 and m % 2:
                                i_.then_inc(*full(s))

            pe.wait_ge(*E.count("dma_const").next())
            E.count("dma_const")
            pe.wait_ge(sems["dma_const"], 16 * 5)
            pe.wait_ge(*E.count("cond_ready").next())
            for L in range(DEPTH):
                o_lo, o_hi = N_OUT[L]
                adaln()
                pe.wait_ge(*E.count("sq_ready").next())
                channel_sum(SQ, KT)
                pe.wait_ge(*E.count("h_ctx_ready").next())
                pe.wait_ge(*E.count("h_lat_ready").next())
                dense(hT, B_XBC)
                pe.wait_ge(*E.count("scr_free").next())
                ssd()
                dense(hT, B_Z, o_lo, o_hi)
                pe.wait_ge(*E.count("ysq_ready").next())
                for g in range(GROUPS):
                    channel_sum(YSQ[g], 4, o_lo, o_hi)
                pe.wait_ge(*E.count("yn_ready").next())
                with E.loop(2):
                    for _ in range(4):
                        w = weights().rearrange("p (k m) -> p k m", k=XS_T)
                        s, o = take()
                        for k in range(XS_T):
                            i_ = mm(o[:, 0, 0:o_hi - o_lo], w[:, k, :], A[:, k, o_lo:o_hi], k == 0, k == XS_T - 1)
                            if k == 0:
                                i_.then_inc(*E.count("w_used").sent())
                        i_.then_inc(*full(s))
                dense(hT, B_GS, o_lo, o_hi)
                dense(hT, B_RKV)
                dense_block(hT, 0, T)
                dense_block(hT, 0, T, tiles=1)
                pe.wait_ge(*E.count("lora_ready").next())
                rwkv()
                pe.wait_ge(*E.count("yr_ready").next())
                dense(A, B_RO, o_lo, o_hi)
                dense(hT, B_GR, o_lo, o_hi)
                pe.wait_ge(*E.count("o_ready").next())
                dense(O, B_WO, o_lo, o_hi)
                pe.wait_ge(*E.count("sq_ready").next())
                channel_sum(SQ, KT, o_lo, o_hi)
                pe.wait_ge(*E.count("sq_ready").next())
                channel_sum(SQ, KT, o_lo, o_hi)
                if L == 0:
                    pe.wait_ge(*E.count("h_ctx_ready").next())
                pe.wait_ge(*E.count("h_lat_ready").next())
                dense(hT, B_FI, o_lo, o_hi)
                pe.wait_ge(*E.count("ffn_ready").next())
                ffn_down(o_lo, o_hi)
                pe.wait_ge(*E.count("sq_ready").next())
                channel_sum(SQ, KT, o_lo, o_hi)

        @block.scalar
        def _(act):
            E = Engine(act, "act", sems, table)
            go = act.activation

            def rstd(lo_, hi, scale, eps, out_, bank=0):
                s, w = E.full()
                act.wait_ge(*w)
                go(out_[:, 0:hi - lo_], ps[:, 2 * s + bank, 0:hi - lo_], ACT.Sqrt, bias=eps, scale=scale).then_inc(*E.freed(s))

            def square_x(src, lo_, hi):
                go(SQ[:, :, lo_:hi], src[:, :, lo_:hi], ACT.Square).then_inc(*E.done("sq_ready"))

            def modulate_ctx(shift):
                act.wait_ge(*E.count("norm_ready").next())
                for k in range(KT):
                    i_ = go(hT[:, k, 0:CTX], SQ[:, k, 0:CTX], ACT.Identity, bias=mod[:, 8 * shift + k, 1:2], scale=gsc[:, k, 1:2])
                i_.then_inc(*E.done("h_ctx_ready"))

            def passed():
                if E.loop_now:
                    act.sem_inc(sems["act_passed"], 1)

            def conv_tiles(name, bias, silu, trips):
                with E.loop(trips) as i:
                    for b in range(4):
                        s, w = E.full()
                        act.wait_ge(*w)
                        passed()
                        for m in range(2):
                            t = i * 8 + (2 * b + m)
                            go(A[:, t, :], ps[:, 2 * s + m, :], ACT.Identity, bias=colr(L, bias, t) if bias else 0.0,
                               scale=colr(L, name, 24 + t)).then_inc(*E.done("tap_ready"))
                        if silu:
                            for m in range(2):
                                t = i * 8 + (2 * b + m)
                                act.wait_ge(*E.count("conv_ready").next())
                                passed()
                                go(A[:, t, :], A[:, t, :], ACT.Silu).then_inc(*E.done("conv_silu"))

            def ssd():
                E.skip(1)
                act.wait_ge(*E.count("abs_ready").next())
                go(sm_a, sm_a, ACT.Abs).then_inc(*E.done())
                act.wait_ge(*E.mine())
                go(sm_a, sm_a, ACT.Exp, scale=-1.0).then_inc(*E.done())
                go(expA, headp[:, L, 1], ACT.Exp).then_inc(*E.done())
                act.wait_ge(*E.mine())
                go(sm_b, sm_a, ACT.Ln, bias=1.0).then_inc(*E.done("log_ready"))
                E.skip(1)
                act.wait_ge(*E.count("dec_in_ready").next())
                go(dec, dec, ACT.Exp).then_inc(*E.done())
                go(wde, wde, ACT.Exp).then_inc(*E.done("dec_ready"))
                with E.loop(GROUPS):
                    s, w = E.full()
                    act.wait_ge(*w)
                    go(btok.rearrange("p c n -> p (c n)"), ps[:, 2 * s, :], ACT.Copy).then_inc(*E.done("btok_ready"))
                    act.wait_ge(*E.mine())
                    act.sem_inc(*E.freed(s))
                    for part in ((0, 1), (2,), (3,)):
                        s, w = E.full()
                        act.wait_ge(*w)
                        c, n = part[0], len(part)
                        go(scr[:, 5632 + 512 * c:5632 + 512 * (c + n)], ps[:, 2 * s:2 * s + n, :].rearrange("p b t -> p (b t)"), ACT.Copy)\
                            .then_inc(*E.freed(s))
                    E.skip(4)
                    for c in range(NCH):
                        for d in range(2):
                            s, w = E.full()
                            act.wait_ge(*w)
                            act.wait_ge(*E.count("diff_ready").next())
                            if SSD_ORDER[d].index(c):
                                go(Cb[d], ps[:, 2 * s:2 * s + 2, :].rearrange("p b (h l) -> p (b h) l", h=4), ACT.Exp)\
                                    .then_inc(*E.done("ec_ready"))
                            else:
                                go(Cb[d][0:1, 0, 0:1], ps[0:1, 2 * s, 0:1], ACT.Exp).then_inc(*E.done("ec_ready"))
                            act.wait_ge(*E.mine())
                            act.sem_inc(*E.freed(s))
                            go(Wb[d], Wb[d], ACT.Exp).then_inc(*E.done("e_ready"))
                        E.skip(1)

            def rwkv():
                with E.loop(KT) as c:
                    s, w = E.full()
                    act.wait_ge(*w)
                    act.wait_ge(*E.count("kkmax_ready").next())
                    go(vtk.rearrange("p q h k -> p (q h k)"), ps[:, 2 * s + 1, :], ACT.Copy).then_inc(*E.done("vtok_ready"))
                    act.wait_ge(*E.mine())
                    act.sem_inc(*E.freed(s))
                    go(tm1, tm1, ACT.Sqrt).then_inc(*E.done("kkstd_ready"))
                    act.wait_ge(*E.count("loop_ready").next())
                    for d in range(2):
                        s, w = E.full()
                        act.wait_ge(*w)
                        passed()
                        go(sg[d], ps[:, 2 * s, :], ACT.Sigmoid, bias=colr(L, "w0", c + 8 * d)).then_inc(*E.done())
                        go(asg[d], ps[:, 2 * s + 1, :], ACT.Sigmoid, bias=colr(L, "a0", c + 8 * d)).then_inc(*E.freed(s))
                        act.wait_ge(*E.mine())
                        act.sem_inc(*E.done("sa_ready"))
                    for d in range(2):
                        act.wait_ge(*E.count("cum_ready").next())
                        go(wc[d], e8(pre[d])[:, :, RC - 1], ACT.Exp, scale=-WSCALE).then_inc(*E.done())
                        go(exc[d], exc[d], ACT.Exp, scale=-WSCALE).then_inc(*E.done())
                        go(sg[d], inc[d], ACT.Exp, scale=-WSCALE).then_inc(*E.done())
                        act.wait_ge(*E.mine())
                        go(inc[d], inc[d], ACT.Exp, scale=WSCALE).then_inc(*E.done("exps_ready"))
                    for d in range(2):
                        s, w = E.full()
                        act.wait_ge(*w)
                        act.wait_ge(*E.count("ops_ready").next())
                        go(RAq[d][:, :, :, 1, :], ps[:, 2 * s, :].rearrange("p (q h k) -> p q h k", q=4, h=2), ACT.Copy).then_inc(*E.done())
                        go(btk[d].rearrange("p q h k -> p (q h k)"), ps[:, 2 * s + 1, :], ACT.Copy).then_inc(*E.freed(s))
                        s, w = E.full()
                        act.wait_ge(*w)
                        go(ktk[d].rearrange("p q h k -> p (q h k)"), ps[:, 2 * s, :], ACT.Copy).then_inc(*E.freed(s))
                        act.wait_ge(*E.mine())
                        act.sem_inc(*E.done("tok_ready"))
                        E.skip(2)
                    E.skip(2 + 20)
                    for d in range(2):
                        s, w = E.full()
                        act.wait_ge(*w)
                        go(RA[d][:, :, 0, :], e8(ps[:, 2 * s, :]), ACT.Copy).then_inc(*E.done("r_ready"))
                        act.wait_ge(*E.mine())
                        act.sem_inc(*E.freed(s))
                    for d in range(2):
                        s, w = E.full()
                        act.wait_ge(*w)
                        ug = ps[:, 2 * s:2 * s + 2, :].rearrange("p b (e a t) -> p (b e) a t", e=4, a=2)
                        go(Xi[d], ug[:, :, 0, :], ACT.Copy).then_inc(*E.done())
                        go(Qi[d], ug[:, :, 1, :], ACT.Copy).then_inc(*E.done("ug_ready"))
                        act.wait_ge(*E.mine())
                        act.sem_inc(*E.freed(s))
                    E.skip(2 + 2 + 12 + 2 + 2 + 1 + 1)
                    act.wait_ge(*E.count("yc_ready").next())
                    go(vS, tm2, ACT.Square).then_inc(*E.done("ycsq_ready"))
                    s, w = E.full()
                    act.wait_ge(*w)
                    go(kkn, ps[:, 2 * s, :], ACT.Sqrt, bias=LN_EPS, scale=1.0 / 64).then_inc(*E.done("ystd_ready"))

            act.wait_ge(sems["dma_const"], 16 * 5)
            go(cond[:, :, :], cond[:, :, :], ACT.Silu).then_inc(*E.done("cond_ready"))
            for L in range(DEPTH):
                lo_, hi = N_OUT[L]
                n = hi - lo_
                with E.loop(6):
                    for r in range(2):
                        s, w = E.full()
                        act.wait_ge(*w)
                        go(rows[0:2, r, :], ps[0:2, 2 * s, :], ACT.Copy).then_inc(*E.done("row_ready"))
                        act.wait_ge(*E.mine())
                        act.sem_inc(*E.freed(s))
                    E.skip(2)
                act.wait_ge(*(E.count("dma_x").next() if L == 0 else E.count("x_ready").so_far()))
                square_x(X, 0, T)
                rstd(0, T, 1.0 / D, EPS, rst)
                modulate_ctx(0)
                conv_tiles("scw", "scb", True, 3)
                ssd()
                with E.loop(2) as i:
                    for b in range(4):
                        s, w = E.full()
                        act.wait_ge(*w)
                        act.wait_ge(*E.count("yz_ready").so_far())
                        E.count("yz_ready").n += 1
                        go(ZS[:, b % 2, :, 0:n], ps[:, 2 * s:2 * s + 2, 0:n], ACT.Silu).then_inc(*E.done("zs_ready"))
                        act.wait_ge(*E.mine())
                        act.sem_inc(*E.freed(s))
                act.wait_ge(*E.count("yz_ready").so_far())
                for g in range(GROUPS):
                    i_ = go(YSQ[g][:, :, lo_:hi], A[:, 4 * g:4 * g + 4, lo_:hi], ACT.Square)
                i_.then_inc(*E.done("ysq_ready"))
                for g in range(GROUPS):
                    rstd(lo_, hi, 4.0 / D_SSM, EPS, GR[g])
                with E.loop(2) as i:
                    for b in range(4):
                        s, w = E.full()
                        act.wait_ge(*w)
                        passed()
                        go(O[:, i * 4 + b, lo_:hi], ps[:, 2 * s, 0:n], ACT.Copy).then_inc(*E.freed(s))
                for b in range(4):
                    s, w = E.full()
                    act.wait_ge(*w)
                    go(SG[:, 2 * b:2 * b + 2, lo_:hi], ps[:, 2 * s:2 * s + 2, 0:n], ACT.Sigmoid).then_inc(*E.freed(s))
                act.wait_ge(*E.mine())
                act.sem_inc(*E.done("gate_ready"))
                conv_tiles("rcw", None, False, 3)
                E.count("conv_ready").n += RK_T
                s, w = E.full()
                act.wait_ge(*w)
                go(lo[:, 0, :], ps[:, 2 * s, :], ACT.Tanh).then_inc(*E.done())
                go(lo[:, 1, :], ps[:, 2 * s + 1, :], ACT.Copy).then_inc(*E.freed(s))
                s, w = E.full()
                act.wait_ge(*w)
                go(lo[:, 2, :], ps[:, 2 * s, :], ACT.Sigmoid).then_inc(*E.freed(s))
                act.wait_ge(*E.mine())
                act.sem_inc(*E.done("lora_ready"))
                rwkv()
                E.count("loop_ready").n += 1
                for b in range(4):
                    s, w = E.full()
                    act.wait_ge(*w)
                    go(SG[:, 2 * b:2 * b + 2, lo_:hi], ps[:, 2 * s:2 * s + 2, 0:n], ACT.Copy).then_inc(*E.freed(s))
                for b in range(4):
                    s, w = E.full()
                    act.wait_ge(*w)
                    go(lo[:, 0:2, 0:n], ps[:, 2 * s:2 * s + 2, 0:n], ACT.Sigmoid).then_inc(*E.done("gate_ready"))
                    act.wait_ge(*E.count("out_ready").next())
                    act.wait_ge(*E.mine())
                    act.sem_inc(*E.freed(s))
                for b in range(4):
                    s, w = E.full()
                    act.wait_ge(*w)
                    go(hT[:, 2 * b:2 * b + 2, lo_:hi], ps[:, 2 * s:2 * s + 2, 0:n], ACT.Copy).then_inc(*E.freed(s))
                act.wait_ge(*E.mine())
                square_x(hT, lo_, hi)
                rstd(lo_, hi, 1.0 / D, EPS, rst)
                act.wait_ge(*E.count("x_ready").next())
                square_x(X, lo_, hi)
                rstd(lo_, hi, 1.0 / D, EPS, rst)
                if L == 0:
                    modulate_ctx(3)
                def ffn_tile(s, w, t):
                    act.wait_ge(*w)
                    passed()
                    go(A[:, t, lo_:hi], ps[:, 2 * s, 0:n], ACT.Identity, bias=colr(L, "fcb", t), scale=colr(L, "fcw", 4 * FF_T + t))\
                        .then_inc(*E.done("tap2_ready"))
                    act.wait_ge(*E.count("conv_ready").next())
                    passed()
                    go(A[:, t, lo_:hi], A[:, t, lo_:hi], ACT.Gelu_apprx_tanh).then_inc(*E.done("gelu_ready"))
                with E.loop(5) as i:
                    for b in range(4):
                        ffn_tile(*E.full(), i * 4 + b)
                for t in range(20, 22):
                    ffn_tile(*E.full(), t)
                for b in range(4):
                    s, w = E.full()
                    act.wait_ge(*w)
                    go(O[:, 2 * b:2 * b + 2, lo_:hi], ps[:, 2 * s:2 * s + 2, 0:n], ACT.Copy).then_inc(*E.freed(s))
                act.wait_ge(*E.mine())
                square_x(O, lo_, hi)
                rstd(lo_, hi, 1.0 / D, EPS, rst)
                E.count("x_ready").n += 1


        @block.vector
        def _(v):
            E = Engine(v, "dve", sems, table)
            tt, ts, stt = v.tensor_tensor, v.tensor_scalar, v.scalar_tensor_tensor

            def own():
                v.wait_ge(*E.mine())

            def recip(lo_, hi):
                s, w = E.full()
                v.wait_ge(sems[f"slot_free{s}"], E.count(f"slot_free{s}").so_far()[1])
                v.reciprocal(rst[:, 0:hi - lo_], rst[:, 0:hi - lo_]).then_inc(*E.done())

            def permuted(ap, L):
                return ap.rearrange("p (w r) -> p r w", r=ROWS) if L == 1 else ap.rearrange("p (r w) -> p r w", r=ROWS)

            def grid(ap):
                return ap.rearrange("p (r w) -> p r w", r=ROWS)

            def prenorm(L, gain, shift, perm, lo_=0):
                own()
                stt(out=gsc[:, :, :], in0=mod[:, 8 * (shift + 1):8 * (shift + 2), :], scalar=1.0,
                    in1=par[:, L, COLS[gain]:COLS[gain] + 8].unsqueeze(2).to_broadcast((P, KT, 2)), op0=ALU.add, op1=ALU.mult)\
                    .then_inc(*E.done())
                recip(lo_, T)
                own()
                tt(SQ[:, :, lo_:T], X[:, :, lo_:T], rst[:, 0:T - lo_].unsqueeze(1).to_broadcast((P, KT, T - lo_)), ALU.mult)\
                    .then_inc(*E.done("norm_ready"))
                own()
                for k in range(KT):
                    i_ = ts(permuted(hT[:, k, CTX:T], 1 if perm else 0), grid(SQ[:, k, CTX:T]), gsc[:, k, 0:1], mod[:, 8 * shift + k, 0:1],
                            ALU.mult, ALU.add)
                i_.then_inc(*E.done("h_lat_ready"))

            def postnorm(L, src, gain, gate, perm, lo_):
                own()
                tt(gsc[:, :, :], mod[:, 8 * gate:8 * gate + 8, :],
                   par[:, L, COLS[gain]:COLS[gain] + 8].unsqueeze(2).to_broadcast((P, KT, 2)), ALU.mult).then_inc(*E.done())
                recip(lo_, T)
                own()
                tt(SQ[:, :, lo_:T], src[:, :, lo_:T], rst[:, 0:T - lo_].unsqueeze(1).to_broadcast((P, KT, T - lo_)), ALU.mult)\
                    .then_inc(*E.done())
                own()
                for k in range(KT):
                    if lo_ == 0:
                        stt(out=X[:, k, 0:CTX], in0=SQ[:, k, 0:CTX], scalar=gsc[:, k, 1:2], in1=X[:, k, 0:CTX], op0=ALU.mult, op1=ALU.add)
                    i_ = stt(out=grid(X[:, k, CTX:T]), in0=permuted(SQ[:, k, CTX:T], 1 if perm else 0), scalar=gsc[:, k, 0:1],
                             in1=grid(X[:, k, CTX:T]), op0=ALU.mult, op1=ALU.add)
                i_.then_inc(*E.done("x_ready"))

            def conv_tiles(name, trips):
                with E.loop(trips) as i:
                    for b in range(4):
                        s, w = E.full()
                        for m in range(2):
                            t = i * 8 + (2 * b + m)
                            v.wait_ge(*E.count("tap_ready").next())
                            src, dst = seg2(ps[:, 2 * s + m, :]), seg2(A[:, t, :])
                            stt(out=dst[:, :, 1:256], in0=src[:, :, 0:255], scalar=colr(L, name, t), in1=dst[:, :, 1:256],
                                op0=ALU.mult, op1=ALU.add).then_inc(*E.done())
                            own()
                            i_ = stt(out=dst[:, :, 0:255], in0=src[:, :, 1:256], scalar=colr(L, name, 48 + t), in1=dst[:, :, 0:255],
                                     op0=ALU.mult, op1=ALU.add)
                            i_.then_inc(*E.done("conv_ready"))
                        own()
                        v.sem_inc(*E.freed(s))

            def ssd():
                s, w = E.full()
                v.wait_ge(*w)
                raw = ps[:, 2 * s, 0:P].rearrange("p (c h) -> p c h", c=NCH)
                for d in range(2):
                    i_ = tt(heads4(sm_a)[:, d], raw, headp[:, L, 0, d, :].unsqueeze(1).to_broadcast((P, NCH, HEADS)), ALU.add)
                i_.then_inc(*E.freed(s))
                own()
                ts(dtv, sm_a, 0.0, None, ALU.max).then_inc(*E.done("abs_ready"))
                v.wait_ge(*E.count("log_ready").next())
                ts(sm_c, sm_a, 1.0, None, ALU.add).then_inc(*E.done())
                own()
                stt(out=sm_a, in0=sm_c, scalar=-1.0, in1=sm_a, op0=ALU.add, op1=ALU.subtract).then_inc(*E.done())
                own()
                v.reciprocal(sm_c, sm_c).then_inc(*E.done())
                own()
                tt(sm_a, sm_a, sm_c, ALU.mult).then_inc(*E.done())
                tt(dtv, dtv, sm_b, ALU.add).then_inc(*E.done())
                own()
                tt(dtv, dtv, sm_a, ALU.subtract).then_inc(*E.done())
                own()
                for d in range(2):
                    i_ = stt(out=heads4(dta)[:, d], in0=heads4(dtv)[:, d], scalar=-1.0,
                             in1=expA[:, HEADS * d:HEADS * (d + 1)].unsqueeze(1).to_broadcast((P, NCH, HEADS)), op0=ALU.mult, op1=ALU.mult)
                i_.then_inc(*E.done("dta_ready"))
                s, w = E.full()
                v.wait_ge(*w)
                ts(ncs, ps[:, 2 * s, 0:256], -1.0, None, ALU.mult).then_inc(*E.done())
                v.tensor_copy(dec, ps[:, 2 * s + 1, 0:256]).then_inc(*E.freed(s))
                own()
                tt(wde, dec, ncs, ALU.add).then_inc(*E.done("dec_in_ready"))
                v.wait_ge(*E.count("dec_ready").next())
                tt(wde, wde, dtv, ALU.mult).then_inc(*E.done("wdec_ready"))
                own()
                with E.loop(GROUPS) as g:
                    hsl = bass.ds(g * HPG, HPG)

                    def per_head(ap, d, c):
                        return heads4(ap)[:, d, c, hsl].unsqueeze(2).to_broadcast((P, HPG, 64))

                    E.skip(2)
                    for _ in range(2):
                        s, w = E.full()
                    v.wait_ge(sems[f"slot_free{(s - 2) % SLOTS}"], E.count(f"slot_free{(s - 2) % SLOTS}").so_far()[1])
                    v.wait_ge(sems[f"slot_free{(s - 1) % SLOTS}"], E.count(f"slot_free{(s - 1) % SLOTS}").so_far()[1])
                    v.wait_ge(sems[f"slot_free{s}"], E.count(f"slot_free{s}").so_far()[1])
                    for o_ in range(3):
                        for d in range(2):
                            c = SSD_ORDER[d][o_]
                            tt(xw[d], xtok[:, c], per_head(wde, d, c), ALU.mult).then_inc(*E.done("xw_ready"))
                        s, w = E.full()
                        v.wait_ge(*w)
                        for d in range(2):
                            c = SSD_ORDER[d][o_]
                            st = ps[:, 2 * s + d, :].rearrange("p (h x) -> p h x", h=HPG)
                            if o_ == 0:
                                v.tensor_copy(Hs[d][0], st).then_inc(*E.done())
                            else:
                                tt(Hs[d][o_], Hs[d][o_ - 1], per_head(dec, d, c), ALU.mult).then_inc(*E.done())
                                own()
                                tt(Hs[d][o_], Hs[d][o_], st, ALU.add).then_inc(*E.done())
                        own()
                        v.sem_inc(*E.freed(s))
                    s, w = E.full()
                    v.wait_ge(*w)
                    for d in range(2):
                        i_ = tt(cbm[d], ps[:, 2 * s, :].rearrange("p (c l) -> p c l", c=NCH), tri[d].unsqueeze(1).to_broadcast((P, NCH, P)), ALU.mult)
                    i_.then_inc(*E.freed(s))
                    own()
                    for c in range(NCH):
                        for d in range(2):
                            s, w = E.full()
                            v.wait_ge(*w)
                            for h in range(HPG):
                                i_ = ts(Wb[d][:, h, :], ps[:, 2 * s + h // 4, P * (h % 4):P * (h % 4 + 1)],
                                        heads4(ncs)[:, d, c, bass.ds(g * HPG + h, 1)], 0.0, ALU.add, ALU.min)
                            i_.then_inc(*E.done("diff_ready"))
                        for d in range(2):
                            v.wait_ge(*E.count("e_ready").next())
                            i_ = tt(Wb[d], Wb[d], cbm[d][:, c, :].unsqueeze(1).to_broadcast((P, HPG, P)), ALU.mult)
                        i_.then_inc(*E.done("w_ready"))
                        s, w = E.full()
                        v.wait_ge(*w)
                        for j in range(4):
                            i_ = stt(out=A[:, g * 4 + j, Q * c:Q * (c + 1)], in0=A[:, g * 4 + j, Q * c:Q * (c + 1)],
                                     scalar=colr(L, "dskip", g * 4 + j), in1=ps[:, 2 * s, P * j:P * (j + 1)], op0=ALU.mult, op1=ALU.add)
                        i_.then_inc(*E.done("y_ready"))
                        own()
                        v.sem_inc(*E.freed(s))

            def rwkv():
                with E.loop(KT) as c:
                    r_, k_, v_ = A[:, c, :], A[:, 8 + c, :], A[:, 16 + c, :]
                    own()
                    ts(kkn, k_, colr(L, "kk", c), None, ALU.mult).then_inc(*E.done())
                    own()
                    tt(tm1, kkn, kkn, ALU.mult).then_inc(*E.done("kksq_ready"))
                    s, w = E.full()
                    v.wait_ge(*w)
                    ts(tm1, ps[:, 2 * s, :], 1e-24, None, ALU.max).then_inc(*E.done("kkmax_ready"))
                    v.wait_ge(*E.count("kkstd_ready").next())
                    v.reciprocal(tm1, tm1).then_inc(*E.done())
                    own()
                    tt(kkn, kkn, tm1, ALU.mult).then_inc(*E.done())
                    E.skip(2)
                    for d in range(2):
                        v.wait_ge(*E.count("sa_ready").next())
                        v.tensor_tensor_scan(pre[d], reset, sg[d], 0.0, ALU.mult, ALU.add).then_inc(*E.done())
                        own()
                        if d == 0:
                            tt(exc[d], pre[d], sg[d], ALU.subtract).then_inc(*E.done())
                            i_ = v.tensor_copy(inc[d], pre[d])
                        else:
                            tt(e8(exc[d]), e8(pre[d])[:, :, RC - 1:RC].to_broadcast((P, 8, RC)), e8(pre[d]), ALU.subtract).then_inc(*E.done())
                            own()
                            i_ = tt(inc[d], exc[d], sg[d], ALU.add)
                        i_.then_inc(*E.done("cum_ready"))
                    for d in range(2):
                        ts(kd[d], asg[d], -1.0, colr(L, "ka", c), ALU.add, ALU.mult).then_inc(*E.done())
                        own()
                        stt(out=kd[d], in0=kd[d], scalar=1.0, in1=k_, op0=ALU.add, op1=ALU.mult).then_inc(*E.done())
                        own()
                        if d == 0:
                            i_ = v.tensor_copy(kds, kd[d])
                        else:
                            i_ = tt(kds, kds, kd[d], ALU.add)
                        i_.then_inc(*E.done())
                        v.wait_ge(*E.count("exps_ready").next())
                        stt(out=at[d], in0=kkn, scalar=-1.0, in1=exc[d], op0=ALU.mult, op1=ALU.mult)
                        tt(rt[d], r_, sg[d], ALU.mult)
                        tt(bt[d], kkn, asg[d], ALU.mult).then_inc(*E.done())
                        own()
                        tt(bt[d], bt[d], inc[d], ALU.mult)
                        tt(kt[d], kd[d], inc[d], ALU.mult).then_inc(*E.done("ops_ready"))
                    for d in range(2):
                        E.skip(2)
                        for dst in (AAb, AAk):
                            s, w = E.full()
                            v.wait_ge(*w)
                            tt(dst[d].rearrange("p e a t -> p e (a t)"), ps[:, 2 * s:2 * s + 2, :].rearrange("p b (q x) -> p (b q) x", q=4),
                               mask2[d].unsqueeze(1).to_broadcast((P, 8, P)), ALU.mult).then_inc(*E.freed(s))
                        own()
                        v.sem_inc(*E.done("aa_ready"))
                    idb = id64.unsqueeze(1).to_broadcast((P, 8, RC))
                    for d in range(2):
                        s, w = E.full()
                        v.wait_ge(*w)
                        tt(Xi[d], e8(ps[:, 2 * s, :]), lvl[0][d].unsqueeze(1).to_broadcast((P, 8, RC)), ALU.mult).then_inc(*E.freed(s))
                        tt(Ni[d], AAb[d][:, :, 0, :], lvl[0][1 - d].unsqueeze(1).to_broadcast((P, 8, RC)), ALU.mult).then_inc(*E.done())
                        own()
                        tt(Xi[d], Xi[d], idb, ALU.add)
                        tt(Ni[d], Ni[d], idb, ALU.add).then_inc(*E.done("xn_ready"))
                    for m in range(1, 6):
                        for d in range(2):
                            s, w = E.full()
                            v.wait_ge(*w)
                            tt(Qi[d], e8(ps[:, 2 * s, :]), lvl[m][d].unsqueeze(1).to_broadcast((P, 8, RC)), ALU.mult).then_inc(*E.done("q_ready"))
                            own()
                            v.sem_inc(*E.freed(s))
                        for d in range(2):
                            s, w = E.full()
                            v.wait_ge(*w)
                            i_ = tt(Ni[d], Ni[d], e8(ps[:, 2 * s, :]), ALU.add)
                            if m < 5:
                                i_ = tt(Xi[d], Xi[d], e8(ps[:, 2 * s + 1, :]), ALU.add)
                            i_.then_inc(*E.done("xn_ready"))
                            own()
                            v.sem_inc(*E.freed(s))
                    E.skip(4)
                    idpq = id64.unsqueeze(1).unsqueeze(1).to_broadcast((P, 2, 4, RC))
                    for d in range(2):
                        s, w = E.full()
                        v.wait_ge(*w)
                        for p in range(2):
                            i_ = tt(MT[d].rearrange("p (q two) t -> p two q t", two=2)[:, p], ps[:, 2 * s + p, 0:256].rearrange("p (q t) -> p q t", q=4),
                                    idpq[:, 0], ALU.add)
                        i_.then_inc(*E.freed(s))
                    for d in range(2):
                        s, w = E.full()
                        v.wait_ge(*w)
                        for p in range(2):
                            i_ = tt(Kv[d].rearrange("p (q two) t -> p two q t", two=2)[:, p], ps[:, 2 * s + p, 0:256].rearrange("p (q t) -> p q t", q=4),
                                    wc[d].rearrange("p (q two) -> p two q", two=2)[:, p].unsqueeze(2).to_broadcast((P, 4, RC)), ALU.mult)
                        i_.then_inc(*E.freed(s))
                    own()
                    for d in range(2):
                        v.memset(Ni[d][:, RW_ORDER[d][0], :], 0.0)
                        v.tensor_copy(Ni[d][:, RW_ORDER[d][1], :], Kv[d][:, RW_ORDER[d][0], :]).then_inc(*E.done("s_ready"))
                    for k in range(2, NRC):
                        for d in range(2):
                            prev, here = RW_ORDER[d][k - 1], RW_ORDER[d][k]
                            s, w = E.full()
                            v.wait_ge(*w)
                            stt(out=Ni[d][:, here, :], in0=ps[:, 2 * s, 0:RC], scalar=wc[d][:, prev:prev + 1], in1=Kv[d][:, prev, :],
                                op0=ALU.mult, op1=ALU.add).then_inc(*E.done("s_ready"))
                            own()
                            v.sem_inc(*E.freed(s))
                    for d in range(2):
                        s, w = E.full()
                        v.wait_ge(*w)
                        for p in range(2):
                            i_ = tt(by_pq(rt[d])[:, p], by_pq(rt[d])[:, p], ps[:, 2 * s + p, 0:256].rearrange("p (q t) -> p q t", q=4), ALU.add)
                        i_.then_inc(*E.done("rp_ready"))
                        own()
                        v.sem_inc(*E.freed(s))
                    for d in range(2):
                        s, w = E.full()
                        v.wait_ge(*w)
                        if d:
                            own()
                        for p in range(2):
                            src = ps[:, 2 * s + p, 0:256].rearrange("p (q t) -> p q t", q=4)
                            if d == 0:
                                i_ = v.tensor_copy(by_pq(yac)[:, p], src)
                            else:
                                i_ = tt(by_pq(yac)[:, p], by_pq(yac)[:, p], src, ALU.add)
                        i_.then_inc(*E.freed(s))
                    s, w = E.full()
                    v.wait_ge(*w)
                    own()
                    tt(yac, yac, ps[:, 2 * s, :], ALU.add).then_inc(*E.done())
                    own()
                    tt(yac, yac, ps[:, 2 * s + 1, :], ALU.add).then_inc(*E.freed(s))
                    stt(out=tm1, in0=kds, scalar=colr(L, "rk", c), in1=r_, op0=ALU.mult, op1=ALU.mult).then_inc(*E.done("yb_ready"))
                    s, w = E.full()
                    v.wait_ge(*w)
                    stt(out=tm2, in0=ps[:, 2 * s, :], scalar=-1.0 / 64, in1=yac, op0=ALU.mult, op1=ALU.add).then_inc(*E.done("yc_ready"))
                    tt(tm1, ps[:, 2 * s + 1, :], v_, ALU.mult).then_inc(*E.freed(s))
                    s, w = E.full()
                    v.wait_ge(*w)
                    v.wait_ge(*E.count("ystd_ready").next())
                    v.reciprocal(kkn, kkn).then_inc(*E.done())
                    own()
                    tt(tm2, tm2, kkn, ALU.mult).then_inc(*E.done())
                    own()
                    ts(tm2, tm2, colr(L, "lnw", c), colr(L, "lnb", c), ALU.mult, ALU.add).then_inc(*E.done())
                    own()
                    tt(tm2, tm2, tm1, ALU.add).then_inc(*E.done())
                    own()
                    tt(r_, tm2, ps[:, 2 * s + 1, :], ALU.mult).then_inc(*E.freed(s))
                    own()
                    v.sem_inc(*E.done("loop_ready"))

            for name in names:
                if name.startswith(PRIMED):
                    v.sem_inc(sems[name], 1)
            v.wait_ge(sems["dma_const"], 16 * 5)
            v.wait_ge(*E.count("dma_x").next())
            for L in range(DEPTH):
                lo_, hi = N_OUT[L]
                n = hi - lo_
                with E.loop(6) as i:
                    E.skip(2)
                    for r in range(2):
                        s, w = E.full()
                        v.wait_ge(*w)
                        first = (i * 2 + r) * 4
                        tt(mod[:, bass.ds(first, 4), :], ps[:, 2 * s, 0:8].rearrange("p (j c) -> p j c", j=4),
                           par[:, L, bass.ds(first + COLS["adab"], 4)].unsqueeze(2).to_broadcast((P, 4, 2)), ALU.add).then_inc(*E.freed(s))
                own()
                prenorm(L, "npre", 0, L == 1)
                conv_tiles("scw", 3)
                v.wait_ge(*E.count("h_ctx_ready").next())
                v.wait_ge(*E.mine())
                v.sem_inc(*E.done("scr_free"))
                ssd()
                with E.loop(2) as i:
                    for b in range(4):
                        E.skip(1)
                        v.wait_ge(*E.count("zs_ready").next())
                        for m in range(2):
                            t = i * 8 + (2 * b + m)
                            i_ = tt(A[:, t, lo_:hi], A[:, t, lo_:hi], ZS[:, b % 2, m, 0:n], ALU.mult)
                        i_.then_inc(*E.done("yz_ready"))
                for g in range(GROUPS):
                    s, w = E.full()
                    v.wait_ge(sems[f"slot_free{s}"], E.count(f"slot_free{s}").so_far()[1])
                    rg = GR[g][:, 0:n]
                    v.reciprocal(rg, rg).then_inc(*E.done())
                    own()
                    for j in range(4):
                        t = 4 * g + j
                        i_ = stt(out=A[:, t, lo_:hi], in0=A[:, t, lo_:hi], scalar=col(L, "snorm", t), in1=rg, op0=ALU.mult, op1=ALU.mult)
                i_.then_inc(*E.done("yn_ready"))
                E.skip(8 + 4)
                v.wait_ge(*E.count("gate_ready").next())
                tt(O[:, :, lo_:hi], O[:, :, lo_:hi], SG[:, :, lo_:hi], ALU.mult).then_inc(*E.done())
                conv_tiles("rcw", 3)
                own()
                v.sem_inc(*E.done("loop_ready"))
                E.skip(2)
                v.memset(reset, 1.0).then_inc(*E.done())
                own()
                v.memset(e8(reset)[:, :, 0:1], 0.0).then_inc(*E.done())
                rwkv()
                v.wait_ge(*E.mine())
                v.sem_inc(*E.done("yr_ready"))
                E.skip(4)
                for b in range(4):
                    E.skip(1)
                    v.wait_ge(*E.count("gate_ready").next())
                    gated = SG[:, 2 * b:2 * b + 2, lo_:hi]
                    tt(gated, gated, lo[:, 0:2, 0:n], ALU.mult).then_inc(*E.done("out_ready"))
                    own()
                    tt(O[:, 2 * b:2 * b + 2, lo_:hi], O[:, 2 * b:2 * b + 2, lo_:hi], gated, ALU.add).then_inc(*E.done())
                own()
                v.sem_inc(*E.done("o_ready"))
                E.skip(4)
                v.wait_ge(*E.count("dma_x").next())
                postnorm(L, hT, "npost", 2, L == 1, lo_)
                if L == 0:
                    prenorm(L, "fpre", 3, False)
                else:
                    prenorm(L, "fpre", 3, False, lo_)

                def ffn_tile(s, t):
                    v.wait_ge(*E.count("tap2_ready").next())
                    first = True
                    if lo_ == 0:
                        src, dst = ps[:, 2 * s, 0:CTX], A[:, t, 0:CTX]
                        for o_, a, b in ((3, 1, 0), (5, 0, 1)):
                            stt(out=dst[:, a:a + 255], in0=src[:, b:b + 255], scalar=colr(L, "fcw", t + FF_T * o_), in1=dst[:, a:a + 255],
                                op0=ALU.mult, op1=ALU.add).then_inc(*E.done())
                            own()
                    src, dst = grid(ps[:, 2 * s, CTX - lo_:T - lo_]), grid(A[:, t, CTX:T])
                    for dr in (-1, 0, 1):
                        for dc in (-1, 0, 1):
                            if dr == dc == 0:
                                continue
                            r0, r1 = max(0, -dr), ROWS - max(0, dr)
                            c0, c1 = max(0, -dc), GRID_W - max(0, dc)
                            i_ = stt(out=dst[:, r0:r1, c0:c1], in0=src[:, r0 + dr:r1 + dr, c0 + dc:c1 + dc],
                                     scalar=colr(L, "fcw", t + FF_T * (3 * (dr + 1) + dc + 1)), in1=dst[:, r0:r1, c0:c1],
                                     op0=ALU.mult, op1=ALU.add)
                            if (dr, dc) != (1, 1):
                                i_.then_inc(*E.done())
                                own()
                    i_.then_inc(*E.done("conv_ready"))
                    v.wait_ge(*E.count("gelu_ready").next())
                    tt(A[:, t, lo_:hi], A[:, t, lo_:hi], ps[:, 2 * s + 1, 0:n], ALU.mult).then_inc(*E.freed(s))
                with E.loop(5) as i:
                    for b in range(4):
                        ffn_tile(E.full()[0], i * 4 + b)
                for t in range(20, 22):
                    ffn_tile(E.full()[0], t)
                own()
                v.sem_inc(*E.done("ffn_ready"))
                E.skip(4)
                postnorm(L, O, "fpost", 5, False, lo_)

        @block.gpsimd
        def _(g_):
            E = Engine(g_, "pool", sems, table)
            for dst, src in ((cond[:, :, :].rearrange("p k c -> p (k c)"), cond_in), (par[:, :, :].rearrange("p l n -> p (l n)"), par_in),
                             (cst[:, :], const_in), (headp[:, :, :, :, :].rearrange("p a b c d -> p (a b c d)"), headp_in),
                             (wdt[:, :, :, :].rearrange("p a b c -> p (a b c)"), wdt_in)):
                g_.dma_start(dst, src).then_inc(sems["dma_const"], 16)
            xv = X.rearrange("p k t -> p (k t)")
            g_.dma_start(xv, x_in).then_inc(*E.count("dma_x").sent())
            for L in range(DEPTH):
                lo_, hi = N_OUT[L]
                if L == 0:
                    g_.dma_start(lst[:, 0:2, :].rearrange("p a n -> p (a n)"), lora_in[0, :, 0:2 * P]).then_inc(*E.count("dma_wa").sent())
                g_.wait_ge(*E.count("conv_silu").next())
                E.count("conv_silu").n += 23
                g_.wait_ge(*E.count("conv_silu").so_far())
                g_.wait_ge(*E.count("scr_free").next())
                g_.wait_ge(*E.count("wdec_ready").next())
                with E.loop(GROUPS) as g:
                    g_.wait_ge(*E.count("y_ready").so_far())
                    E.count("y_ready").n += NCH
                    g_.tensor_copy(xg, A[:, bass.ds(g * 4, 4), :])
                    g_.tensor_copy(Bg, A[:, XS_T + g, :])
                    g_.tensor_copy(Cg, A[:, XS_T + 4 + g, :])
                    for d in range(2):
                        i_ = g_.tensor_copy(dtag[:, d], heads4(dta)[:, d, :, bass.ds(g * HPG, HPG)])
                    i_.then_inc(*E.done("staged"))
                    g_.wait_ge(*E.mine())
                    for c in range(NCH):
                        if c == 0:
                            g_.wait_ge(*E.count("xw_ready").next())
                            E.count("xw_ready").n += 5
                        else:
                            g_.wait_ge(sems["y_ready"], E.count("y_ready").so_far()[1] - NCH + c)
                        for d in range(2):
                            i_ = g_.tensor_tensor(xdt[d], xtok[:, c], heads4(dtv)[:, d, c, bass.ds(g * HPG, HPG)].unsqueeze(2).to_broadcast((P, HPG, 64)), ALU.mult)
                        i_.then_inc(*E.done("xdt_ready"))
                        for d in range(2):
                            g_.wait_ge(*E.count("ec_ready").next())
                            if SSD_ORDER[d].index(c):
                                i_ = g_.tensor_tensor(Cb[d], Cb[d], Cg[:, Q * c:Q * (c + 1)].unsqueeze(1).to_broadcast((P, HPG, P)), ALU.mult)
                        i_.then_inc(*E.done("ct_ready"))
                g_.wait_ge(*E.count("loop_ready").next())
                with E.loop(KT) as c:
                    g_.wait_ge(*E.count("loop_ready").so_far())
                    E.count("loop_ready").n += 1
                    g_.dma_start(lst[:, 2, :], lora_in[c + KT * L, :, 2 * P:3 * P]).then_inc(*E.count("dma_g2").sent())
                    g_.tensor_copy(vS, A[:, 16 + c, :]).then_inc(*E.done("vs_ready"))
                    E.count("sa_ready").next()
                    g_.wait_ge(*E.count("sa_ready").next())
                    g_.dma_start(lst[:, 0:2, :].rearrange("p a n -> p (a n)"), lora_in[c + (KT * L + 1), :, 0:2 * P]).then_inc(*E.count("dma_wa").sent())
                g_.wait_ge(*E.count("o_ready").next())
                g_.dma_start(xv, x_in if L == 0 else x_mid).then_inc(*E.count("dma_x").sent())
                g_.wait_ge(*E.count("x_ready").next())
                g_.wait_ge(*E.count("x_ready").next())
                if L == 0:
                    g_.dma_start(x_mid, xv).then_inc(*E.count("dma_out").sent())
                    g_.wait_ge(*E.count("dma_out").so_far())
            g_.dma_start(out.rearrange("p (k t) -> p k t", k=KT), X[:, :, CTX:T]).then_inc(*E.count("dma_out").sent())
            g_.wait_ge(*E.count("dma_out").so_far())


INS = ("stream", "x_in", "cond", "par", "consts", "headp", "wdt", "lora")


def constants():
    c = np.zeros((P, CONSTS), np.float32)

    def put(name, a, off=0):
        c[:, CCOL[name] + off:CCOL[name] + off + a.shape[1]] = a

    i = np.arange(P)
    put("ident", np.eye(P))
    put("ones", np.ones((P, P)))
    put("headones", (i[:, None] // 64 == i[None] // 64) * 1.0)
    r, t = i[:, None] % RC, np.arange(RC)[None]
    for d in range(2):
        put("tri", (i[:, None] <= i[None]) * 1.0 if d == 0 else (i[:, None] >= i[None]) * 1.0, P * d)
        put("mask2", np.concatenate([(r < t), (r <= t)] if d == 0 else [(r > t), (r >= t)], 1) * 1.0, P * d)
        for m in range(6):
            b = 1 << m
            same = r // (2 * b) == t // (2 * b)
            low = (r // b % 2 == 1) & (t // b % 2 == 0)
            high = (r // b % 2 == 0) & (t // b % 2 == 1)
            put("lvl", (same & (low if d == 0 else high)) * 1.0, RC * (2 * m + d))
    put("id64", (r == t) * 1.0)
    return c


def lay_out(inp):
    g = {k: np.asarray(v) for k, v in inp.items()}

    def cols256(w):
        n = w.shape[1]
        return w.reshape(KT, P, n // 256, 256).transpose(2, 1, 0, 3).reshape(n // 256, P, WBLK)

    def tab(a):
        return a.reshape(-1, P).T

    blocks = []
    pars, headp, wdt, lora = [], [], [], []
    for L in range(DEPTH):
        wi = g["w_in"][L]
        o = np.cumsum([0, 2048, 3072, 32, 3072, 128, 128, 128, 2048])
        z, xbc, dt, rkv, wd, ad, gd, gate = [wi[:, o[j]:o[j + 1]] for j in range(8)]
        blocks.append(g["ada_w"][L].reshape(2, 4, P, 12, 512).transpose(3, 0, 2, 1, 4).reshape(24, P, WBLK))
        blocks += [cols256(xbc), cols256(z)]
        blocks.append(g["ssm_out"][L].reshape(16, P, 8, P).transpose(2, 1, 0, 3).reshape(8, P, WBLK))
        blocks += [cols256(gate[:, :D]), cols256(rkv), cols256(np.concatenate([wd, ad], 1)),
                   cols256(np.concatenate([gd, np.zeros_like(gd)], 1)), cols256(g["rwkv_out"][L]), cols256(gate[:, D:]),
                   cols256(g["w_o"][L])]
        fi = g["ffn_w_in"][L]
        pair = np.concatenate([fi[:, :2816].reshape(D, FF_T, 1, P), fi[:, 2816:].reshape(D, FF_T, 1, P)], 2)
        blocks.append(cols256(pair.reshape(D, 2 * 2816)))
        blocks.append(g["ffn_w_out"][L].reshape(11, 2, P, D).transpose(0, 2, 1, 3).reshape(11, P, WBLK))
        wdt.append(dt.reshape(KT, P, HEADS).transpose(1, 0, 2).reshape(P, -1))
        p = np.zeros((P, PARAMS), np.float32)

        def put(name, a):
            p[:, COLS[name]:COLS[name] + a.shape[1]] = a

        for name, key in (("npre", "norm_mix_pre"), ("npost", "norm_mix_post"), ("fpre", "norm_ffn_pre"), ("fpost", "norm_ffn_post"),
                          ("scw", "ssm_conv_w"), ("scb", "ssm_conv_b"), ("snorm", "ssm_norm"), ("rcw", "rwkv_conv_w"),
                          ("w0", "rwkv_w0"), ("a0", "rwkv_a0"), ("kk", "rwkv_k_k"), ("ka", "rwkv_k_a"), ("rk", "rwkv_r_k"),
                          ("lnw", "rwkv_ln_w"), ("lnb", "rwkv_ln_b"), ("fcw", "ffn_conv_w"), ("fcb", "ffn_conv_b"), ("adab", "ada_b")):
            put(name, tab(g[key][L]))
        put("dskip", tab(np.repeat(g["ssm_d"][L], 64)))
        pars.append(p)
        headp.append(np.stack([g["ssm_dt_bias"][L], g["ssm_a_log"][L]]).reshape(-1))
        lora.append(np.stack([g["rwkv_w2"][L].reshape(P, KT, P), g["rwkv_a2"][L].reshape(P, KT, P), g["rwkv_g2"][L].reshape(P, KT, P)], 2)
                    .transpose(1, 0, 2, 3).reshape(KT, P, 3 * P))
    tokens = np.concatenate([g["ctx"][0], g["x"][0]], 0)
    return {
        "stream": np.concatenate(blocks, 0),
        "x_in": tokens.reshape(T, KT, P).transpose(2, 1, 0).reshape(P, -1),
        "cond": np.stack([g["c"][0], g["c_ctx"]], 0).reshape(2, KT, P).transpose(2, 1, 0).reshape(P, -1),
        "par": np.concatenate(pars, 1),
        "consts": constants(),
        "headp": np.repeat(np.concatenate(headp)[None], P, 0),
        "wdt": np.concatenate(wdt, 1),
        "lora": np.concatenate(lora + [np.zeros((1, P, 3 * P), np.float32)], 0),
    }


def program(nc, arrays, table):
    ins = [nc.dram_tensor("in_" + n, arrays[n].shape, F32, kind="ExternalInput").ap() for n in INS]
    out = nc.dram_tensor("out", (P, KT * LAT), F32, kind="ExternalOutput").ap()
    build(nc, ins, out, table)


def kernel(**inputs):
    import concourse.bacc as _bacc
    from concourse.bass_utils import run_bass_kernel_spmd as _run

    arrays = {k: np.ascontiguousarray(v) for k, v in lay_out(inputs).items()}
    table = {}
    for _ in range(2):
        nc = _bacc.Bacc("TRN2", target_bir_lowering=False, num_devices=1)
        program(nc, arrays, table)
    r = _run(nc, [{"in_" + k: v for k, v in arrays.items()}], core_ids=[0])
    got = r.results[0]["out"]
    return np.ascontiguousarray(got.reshape(P, KT, LAT).transpose(2, 1, 0).reshape(1, LAT, D))
```

```python
from contextlib import ExitStack, contextmanager

import numpy as np
import concourse.bass as bass
from concourse import mybir

F32 = mybir.dt.float32
ACT = mybir.ActivationFunctionType
ALU = mybir.AluOpType

P = 128
DEPTH = 2
D = 1024
KT = D // P
CTX, LAT = 256, 256
T = CTX + LAT
GRID_W = 64
ROWS = LAT // GRID_W
EPS = 1e-6
D_SSM, HEADS, GROUPS, HPG = 2048, 32, 4, 8
XS_T = D_SSM // P
XBC_T = XS_T + 8
Q = 128
NCH = T // Q
RC = 64
HB = 32
NRC = T // RC
RK_T = 24
LN_EPS = 64e-5
WSCALE = float(np.exp(-0.5))
FF_T = 2816 // P
SLOTS = 4
WSLOTS = 4
WBLK = 2048

B_ADA, B_XBC, B_Z, B_SO, B_GS, B_RKV, B_LORA, B_RO, B_GR, B_WO, B_FI, B_FO = 24, 12, 8, 8, 4, 12, 2, 4, 4, 4, 22, 11
TO_RWKV = B_ADA + B_XBC + B_Z + B_SO + B_GS + B_RKV + B_LORA
PER_LAYER = TO_RWKV + B_RO + B_GR + B_WO + B_FI + B_FO
NBLK = DEPTH * PER_LAYER
RING_STOPS = tuple(TO_RWKV + PER_LAYER * L for L in range(DEPTH))

COLS, _n = {}, 0
for _name, _w in (("npre", 8), ("npost", 8), ("fpre", 8), ("fpost", 8), ("scw", 72), ("scb", 24), ("snorm", 16),
                  ("rcw", 72), ("w0", 16), ("a0", 16), ("kk", 8), ("ka", 8), ("rk", 8), ("lnw", 8), ("lnb", 8),
                  ("fcw", 9 * FF_T), ("fcb", FF_T), ("adab", 48), ("dskip", 16)):
    COLS[_name] = _n
    _n += _w
PARAMS = _n

CCOL, _n = {}, 0
for _name, _w in (("ident", 128), ("ones", 128), ("headones", 128), ("tri", 256), ("mask2", 256),
                  ("lvl", 10 * 32), ("id32", 32), ("half", 64), ("id64", 64)):
    CCOL[_name] = _n
    _n += _w
CONSTS = _n

SSD_ORDER = ((0, 1, 2, 3), (1, 0, 3, 2))
RW_ORDER = ((0, 1, 2, 3, 4, 5, 6, 7), (3, 2, 1, 0, 7, 6, 5, 4))


PRIMED = ("slot_free", "y_ready", "yz_ready", "dve_done")


class Count:

    def __init__(self, sem, unit, primed):
        self.sem, self.unit, self.n, self.primed, self.i, self.per = sem, unit, primed, primed, None, 0

    def _value(self):
        if self.i is None or not self.per:
            return self.n
        assert self.n > 0, "a wait on a register's value stays above zero: prime the semaphore"
        return self.n + self.i * self.per

    def sent(self):
        self.n += self.unit
        return self.sem, self.unit

    def next(self):
        self.n += self.unit
        return self.sem, self._value()

    def so_far(self):
        return self.sem, self._value()


class Engine:

    def __init__(self, e, name, sems, table):
        self.e, self.name, self.sems, self.table = e, name, sems, table
        self.counts, self.loops, self.step_no, self.wblk, self.own = {}, 0, 0, 0, f"{name}_done"
        self.last = None

    def count(self, name):
        if name not in self.counts:
            c = Count(self.sems[name], 16 if name.startswith(("w_loaded", "dma")) else 1, int(name.startswith(PRIMED)))
            if self.loop_now:
                c.i, c.per = self.loop_now[0], self.loop_now[1].get(name, 0)
            self.counts[name] = c
        return self.counts[name]

    loop_now = None

    def done(self, name=None):
        c = self.count(name or self.own)
        out = c.sent()
        self.last = (c.sem, c._value())
        return out

    def mine(self):
        return self.last or self.count(self.own).so_far()

    def slot(self):
        s = self.step_no % SLOTS
        self.step_no += 1
        return s

    def skip(self, n=1):
        for _ in range(n):
            s = self.slot()
            self.count(f"slot_full{s}").n += 1
            self.count(f"slot_free{s}").n += 1

    def full(self):
        s = self.slot()
        self.count(f"slot_free{s}").n += 1
        return s, self.count(f"slot_full{s}").next()

    def freed(self, s):
        c = self.count(f"slot_free{s}")
        self.last = (c.sem, c._value())
        return c.sem, 1

    @contextmanager
    def loop(self, trips):
        key = (self.name, self.loops)
        self.loops += 1
        per = self.table.get(key, {})
        start = {k: c.n for k, c in self.counts.items()}
        at, wat = self.step_no, self.wblk
        with self.e.Fori(0, trips) as i:
            self.loop_now = (i, per)
            for k, c in self.counts.items():
                c.i, c.per = i, per.get(k, 0)
            self.last = None
            yield i
        self.loop_now, self.last = None, None
        start = {k: start.get(k, c.primed) for k, c in self.counts.items()}
        found = {k: c.n - start[k] for k, c in self.counts.items() if c.n != start[k]}
        assert not per or per == found, (key, per, found)
        self.table[key] = found
        for k, c in self.counts.items():
            c.i, c.per = None, 0
            c.n = start[k] + trips * found.get(k, 0)
        assert (self.step_no - at) % SLOTS == 0 and (self.wblk - wat) % WSLOTS == 0, (key, self.step_no - at)
        self.step_no, self.wblk = at, wat


def build(nc, ins, out, table):
    stream, x_in, cond_in, par_in, const_in, headp_in, wdt_in, lora_in = ins
    x_mid = nc.dram_tensor("x_mid", (P, KT * T), F32, kind="Internal").ap()

    with ExitStack() as ctx:
        def sb(name, *shape):
            return ctx.enter_context(nc.sbuf_tensor(name, [P, *shape], F32))

        W = sb("W", WSLOTS, WBLK)
        A = sb("A", RK_T, T)
        hT = sb("hT", KT, T)
        O = sb("O", KT, T)
        lo = sb("lo", 3, T)
        scr = sb("scr", 16384)
        mod = sb("mod", 48, 2)
        par = sb("par", DEPTH, PARAMS)
        cst = sb("cst", CONSTS)
        headp = sb("headp", DEPTH, 2, 2, HEADS)
        wdt = sb("wdt", DEPTH, KT, HEADS)
        cond = sb("cond", KT, 2)
        uv_more = sb("uv_more", 512)
        gsc = sb("gsc", KT, 2)
        rst = sb("rst", T)
        lst = sb("lst", 3, P)
        rows = lo
        ps = ctx.enter_context(nc.psum_tensor("ps", [P, 2 * SLOTS, 512], F32))

        names = ([f"slot_full{s}" for s in range(SLOTS)] + [f"slot_free{s}" for s in range(SLOTS)]
                 + [f"w_loaded{s}" for s in range(WSLOTS)]
                 + ["w_used", "pe_passed", "act_passed", "pe_done", "act_done", "dve_done", "pool_done",
                    "dma_const", "dma_x", "dma_wa", "dma_g2", "dma_out",
                    "cond_ready", "row_ready", "sq_ready", "std_ready", "norm_ready", "h_ctx_ready", "h_lat_ready",
                    "tap_ready", "conv_ready", "conv_silu", "abs_ready", "exp_ready", "log_ready", "expA_ready",
                    "dta_ready", "cs_ready", "dec_in_ready", "dec_ready", "wdec_ready", "staged", "xw_ready", "btok_ready",
                    "h_ssd_ready", "cbm_ready", "diff_ready", "e_ready", "ec_ready", "xdt_ready", "ct_ready", "w_ready",
                    "y_ready", "zs_ready", "yz_ready", "ysq_ready", "yn_ready", "out_ready", "gate_ready", "o_ready",
                    "lora_ready", "kksq_ready", "kkmax_ready", "kkstd_ready", "vs_ready", "vtok_ready", "sa_ready",
                    "cum_ready", "exps_ready", "ops_ready", "tok_ready", "aa_ready", "xn_ready", "q_ready", "r_ready",
                    "ug_ready", "mt_ready", "kv_ready", "s_ready", "rp_ready", "yb_ready", "yc_ready", "ycsq_ready",
                    "ystd_ready", "yr_ready", "ring_free", "wo_ready", "gelu_ready", "tap2_ready", "ffn_ready",
                    "fo_ready", "x_ready", "x_used", "scr_free"])
        sems = {n: ctx.enter_context(nc.semaphore(n)) for n in names}

        def cc(name, w=None, off=0):
            return cst[:, CCOL[name] + off:CCOL[name] + off + w]

        ident, ones, headones = cc("ident", P), cc("ones", P), cc("headones", P)
        tri = [cc("tri", P, P * d) for d in range(2)]
        mask2 = [cc("mask2", P, P * d) for d in range(2)]
        lvl = [[cc("lvl", HB, HB * (2 * m + d)) for d in range(2)] for m in range(5)]
        id32, half = cc("id32", HB), cc("half", RC)
        id64 = cc("id64", RC)
        reset = rst[:, :]

        def col(L, name, k=0, w=1):
            return par[:, L, COLS[name] + k:COLS[name] + k + w]

        def colr(L, name, k):
            return par[:, L, bass.ds(COLS[name] + k, 1)]

        def span(a, w):
            return scr[:, a:a + w]

        X = span(0, KT * T).rearrange("p (k t) -> p k t", k=KT)
        SQ = span(KT * T, KT * T).rearrange("p (k t) -> p k t", k=KT)

        YSQ = [span(2048 * g, 2048).rearrange("p (k t) -> p k t", k=4) for g in range(GROUPS)]
        GR = [span(8192 + 512 * g, 512) for g in range(GROUPS)]
        ZS = span(12288, 2048).rearrange("p (r m t) -> p r m t", r=2, m=2)
        SG = span(0, KT * T).rearrange("p (k t) -> p k t", k=KT)

        Of = O[:, :, :].rearrange("p k t -> p (k t)")
        lof = lo[:, :, :].rearrange("p k t -> p (k t)")
        Wb = [[a[:, 1024 * d:1024 * (d + 1)].rearrange("p (h l) -> p h l", h=HPG) for d in range(2)] for a in (span(0, 2048), Of)]
        xg = span(0, 2048).rearrange("p (j t) -> p j t", j=4)
        Cb = [[a[:, 1024 * d:1024 * (d + 1)].rearrange("p (h l) -> p h l", h=HPG) for d in range(2)]
              for a in (span(2048, 2048), Of[:, 2048:4096])]
        Bg, Cg = span(4096, T), span(4608, T)
        btok = span(5120, T).rearrange("p (c n) -> p c n", c=NCH)
        xtok = span(5632, 2048).rearrange("p (c h x) -> p c h x", c=NCH, h=HPG)
        Hs = [[span(7680 + 1536 * d + 512 * o, 512).rearrange("p (h x) -> p h x", h=HPG) for o in range(3)] for d in range(2)]
        xdt = [[a[:, 512 * d:512 * (d + 1)].rearrange("p (h x) -> p h x", h=HPG) for d in range(2)] for a in (span(10752, 1024), lof)]
        xw = [span(11776 + 512 * d, 512).rearrange("p (h x) -> p h x", h=HPG) for d in range(2)]
        cbm = [span(12800 + 512 * d, 512).rearrange("p (c l) -> p c l", c=NCH) for d in range(2)]
        small = [span(13824 + 256 * j, 256) for j in range(8)]
        dtv, dta, ncs, wde, dec, sm_a, sm_b, sm_c = small
        dtag = span(13824 + 2048, 64).rearrange("p (d c h) -> p d c h", d=2, c=NCH)
        expA = span(13824 + 2048 + 64, 64)

        def heads4(ap):
            return ap.rearrange("p (d c h) -> p d c h", d=2, c=NCH)

        RD = 6144
        Wf = W[:, :, :].rearrange("p s n -> p (s n)")

        def ring(k, w=512):
            return Wf[:, k:k + w]

        at = [ring(2048 * d) for d in range(2)]
        rt = [ring(2048 * d + 512) for d in range(2)]
        bk = [ring(2048 * d + 1024, 1024) for d in range(2)]
        bt = [bk[d].rearrange("p (q f t) -> p q f t", q=4, f=4)[:, :, 0:4:3, :] for d in range(2)]
        kt = [bk[d].rearrange("p (q f t) -> p q f t", q=4, f=4)[:, :, 1:3, :] for d in range(2)]
        art = [ring(2048 * d, 1024).rearrange("p (two c t) -> p c two t", two=2, c=NRC) for d in range(2)]
        sg, asg, pre, exc, inc, kkn, kds, vS = [ring(4096 + 512 * j) for j in range(8)]
        rq = [span(RD * d + 512, 512) for d in range(2)]

        def e8(ap):
            return ap.rearrange("p (e t) -> p e t", e=8)

        Dh = [span(RD * d + 1792, 256).rearrange("p (e t) -> p e t", e=8) for d in range(2)]
        Qh = [span(RD * d + 1536, 256).rearrange("p (e t) -> p e t", e=8) for d in range(2)]
        Nh = [span(RD * d, 256).rearrange("p (e t) -> p e t", e=8) for d in range(2)]
        Xh = [span(RD * d + 256, 256).rearrange("p (e t) -> p e t", e=8) for d in range(2)]
        Ni = [e8(span(RD * d + 1024, 512)) for d in range(2)]
        Qi = [e8(span(RD * d + 1536, 512)) for d in range(2)]
        AA = [[span(RD * d + 2048 + 1024 * p, 1024).rearrange("p (e a t) -> p e a t", e=8, a=2) for p in range(2)] for d in range(2)]
        RA = [span(RD * d + 4096, 1024).rearrange("p (e a t) -> p e a t", e=8, a=2) for d in range(2)]
        RAq = [span(RD * d + 4096, 1024).rearrange("p (h q a t) -> p q h a t", h=2, q=4, a=2) for d in range(2)]
        MT = [e8(span(RD * d + 4096, 512)) for d in range(2)]
        Kv = [e8(span(RD * d + 4608, 512)) for d in range(2)]
        BK = [span(RD * d + 5120, 1024).rearrange("p (c h k) -> p c h k", c=NRC, h=2) for d in range(2)]
        UV = [[e8(span(12288 + 512 * p, 512) if d == 0 else (span(13312, 512), uv_more[:, :])[p]) for p in range(2)] for d in range(2)]
        yac, yc, ycsq, bonus = [span(13824 + 512 * j, 512) for j in range(4)]
        ystd = ycsq
        wc = [span(15872 + 8 * d, 8) for d in range(2)]
        wcu = [span(15888 + 8 * d, 8) for d in range(2)]

        def by_pq(ap):
            return ap.rearrange("p (q two t) -> p two q t", two=2, t=RC)

        def quads(ap):
            return ap.rearrange("p (q two t) -> p q two t", two=2, t=RC)

        def seg2(ap):
            return ap.rearrange("p (s t) -> p s t", s=2)

        across = [[(2 * HB * p + HB * d, 2 * HB * p + HB * d + HB) for p in range(2)] for d in range(2)]

        N_OUT = {0: (0, T), 1: (CTX, T)}

        block = ctx.enter_context(nc.Block())

        @block.sync
        def _(sp):
            E = Engine(sp, "sp", sems, table)
            wv = stream
            first = 0
            for last in RING_STOPS + (NBLK,):
                if first:
                    sp.wait_ge(*E.count("ring_free").next())
                for b in range(first, first + WSLOTS):
                    sp.dma_start(W[:, b % WSLOTS, :], wv[b]).then_inc(sems[f"w_loaded{b % WSLOTS}"], 16)
                rounds = (last - first) // WSLOTS
                with sp.Fori(1, rounds) as i:
                    for j in range(WSLOTS):
                        sp.wait_ge(sems["w_used"], i * WSLOTS + (first + j - WSLOTS + 2))
                        s = (first + j) % WSLOTS
                        sp.dma_start(W[:, s, :], wv[i * WSLOTS + (first + j)]).then_inc(sems[f"w_loaded{s}"], 16)
                for b in range(first + rounds * WSLOTS, last):
                    sp.wait_ge(sems["w_used"], b - WSLOTS + 2)
                    sp.dma_start(W[:, b % WSLOTS, :], wv[b]).then_inc(sems[f"w_loaded{b % WSLOTS}"], 16)
                first = last

        @block.tensor
        def _(pe):
            E = Engine(pe, "pe", sems, table)

            def mm(o, l, r, start=True, stop=True):
                return pe.matmul(o, l, r, start=start, stop=stop)

            def passed():
                if E.loop_now:
                    pe.sem_inc(sems["pe_passed"], 1)

            def take():
                s = E.slot()
                pe.wait_ge(*E.count(f"slot_free{s}").so_far())
                passed()
                E.count(f"slot_free{s}").n += 1
                return s, ps[:, 2 * s:2 * s + 2, :]

            def full(s):
                return E.count(f"slot_full{s}").sent()

            def weights():
                s = E.wblk % WSLOTS
                E.wblk += 1
                pe.wait_ge(*E.count(f"w_loaded{s}").next())
                return W[:, s, :]

            def dense_block(src, lo_, hi, tiles=2):
                w = weights().rearrange("p (k m) -> p k m", k=KT)
                s, o = take()
                for m in range(tiles):
                    for k in range(KT):
                        ins_ = mm(o[:, m, 0:hi - lo_], w[:, k, P * m:P * (m + 1)], src[:, k, lo_:hi], k == 0, k == KT - 1)
                        if m == 0 and k == 0:
                            ins_.then_inc(*E.count("w_used").sent())
                ins_.then_inc(*full(s))

            def dense(src, blocks, lo_=0, hi=T):
                trips, rest = divmod(blocks, WSLOTS)
                if trips > 1:
                    with E.loop(trips):
                        for _ in range(WSLOTS):
                            dense_block(src, lo_, hi)
                else:
                    rest = blocks
                for _ in range(rest):
                    dense_block(src, lo_, hi)

            def channel_sum(src, n, lo_=0, hi=T):
                s, o = take()
                for k in range(n):
                    i_ = mm(o[:, 0, 0:hi - lo_], ones, src[:, k, lo_:hi], k == 0, k == n - 1)
                i_.then_inc(*full(s))

            def adaln():
                with E.loop(6):
                    for n in range(2):
                        s, o = take()
                        for half in range(2):
                            w = weights().rearrange("p (k n) -> p k n", k=4)
                            for k in range(4):
                                i_ = mm(o[0:2, 0, :], cond[:, 4 * half + k, :], w[:, k, :], half + k == 0, half == 1 and k == 3)
                                if k == 0:
                                    i_.then_inc(*E.count("w_used").sent())
                        i_.then_inc(*full(s))
                    for n in range(2):
                        s, o = take()
                        pe.wait_ge(*E.count("row_ready").next())
                        passed()
                        for j in range(4):
                            i_ = pe.transpose(o[:, 0, 2 * j:2 * j + 2], rows[0:2, n, P * j:P * (j + 1)], ident[0:2, 0:2])
                        i_.then_inc(*full(s))

            def ssd():
                s, o = take()
                for c in range(NCH):
                    for k in range(KT):
                        i_ = mm(o[:, 0, HEADS * c:HEADS * (c + 1)], hT[:, k, Q * c:Q * (c + 1)], wdt[:, L, k, :], k == 0, k == KT - 1)
                i_.then_inc(*full(s))
                pe.wait_ge(*E.count("dta_ready").next())
                s, o = take()
                for d in range(2):
                    mm(o[:, 0, P * d:P * (d + 1)], tri[d], dta[:, P * d:P * (d + 1)])
                mm(o[:, 1, 0:256], ones, dta).then_inc(*full(s))
                with E.loop(GROUPS):
                    pe.wait_ge(*E.count("staged").next())
                    for part in ((("B", 0),), (("x", 0), ("x", 1)), (("x", 2),), (("x", 3),)):
                        s, o = take()
                        for bank, (what, c) in enumerate(part):
                            for j in range(4):
                                src = Bg[:, Q * j:Q * (j + 1)] if what == "B" else xg[:, j, Q * c:Q * (c + 1)]
                                i_ = pe.transpose(o[:, bank, P * j:P * (j + 1)], src, ident)
                        i_.then_inc(*full(s))
                    for o_ in range(3):
                        s, o = take()
                        for d in range(2):
                            pe.wait_ge(*E.count("xw_ready").next())
                            if o_ == 0 and d == 0:
                                pe.wait_ge(*E.count("btok_ready").next())
                            i_ = mm(o[:, d, :], btok[:, SSD_ORDER[d][o_], :], xw[d])
                        i_.then_inc(*full(s))
                    s, o = take()
                    for c in range(NCH):
                        i_ = mm(o[:, 0, Q * c:Q * (c + 1)], Bg[:, Q * c:Q * (c + 1)], Cg[:, Q * c:Q * (c + 1)])
                    i_.then_inc(*full(s))

                    def cumulated(c):
                        for d in range(2):
                            s, o = take()
                            for h in range(HPG):
                                i_ = mm(o[:, h // 4, P * (h % 4):P * (h % 4 + 1)],
                                        dtag[:, d, c, h:h + 1].to_broadcast((P, P)), tri[d])
                            i_.then_inc(*full(s))

                    def output(c):
                        s, o = take()
                        pe.wait_ge(*E.count("w_ready").next())
                        pe.wait_ge(*E.count("ct_ready").next())
                        for j in range(HPG // 2):
                            terms = []
                            for d in range(2):
                                terms.append((xdt[c % 2][d], Wb[c % 2][d]))
                                k = SSD_ORDER[d].index(c)
                                if k:
                                    terms.append((Hs[d][k - 1], Cb[c % 2][d]))
                            for n, (l, r) in enumerate(terms):
                                for e in range(2):
                                    i_ = mm(o[64 * e:64 * e + 64, 0, P * j:P * (j + 1)], l[:, 2 * j + e, :], r[:, 2 * j + e, :],
                                            n == 0, n == len(terms) - 1)
                        i_.then_inc(*full(s))

                    cumulated(0)
                    for c in range(NCH):
                        if c + 1 < NCH:
                            cumulated(c + 1)
                        output(c)

            def front_sum():
                s, o = take()
                pe.wait_ge(*E.count("kksq_ready").next())
                mm(o[:, 0, :], headones, exc).then_inc(*full(s))

            def front_lora(d):
                s, o = take()
                half = slice(64 * d, 64 * d + 64)
                if d == 0:
                    pe.wait_ge(*E.count("dma_wa").next())
                mm(o[:, 0, :], lst[half, 0, :], lo[half, 0, :])
                mm(o[:, 1, :], lst[half, 1, :], lo[half, 1, :]).then_inc(*full(s))

            def tail_mean(c):
                s, o = take()
                pe.wait_ge(*E.count("yb_ready").next())
                mm(o[:, 0, o_lo:T], headones, yac[:, o_lo:T])
                mm(o[:, 1, o_lo:T], headones, A[:, 8 + c, o_lo:T]).then_inc(*full(s))

            def tail_var():
                s, o = take()
                pe.wait_ge(*E.count("ycsq_ready").next())
                pe.wait_ge(*E.count("dma_g2").next())
                mm(o[:, 0, o_lo:T], headones, ycsq[:, o_lo:T])
                mm(o[:, 1, o_lo:T], lst[:, 2, :], lo[:, 2, o_lo:T]).then_inc(*full(s))

            def rwkv_tile(c, front, tail):
                for d in range(2):
                    pe.wait_ge(*E.count("ops_ready").next())
                    s, o = take()
                    for ch in range(NRC):
                        i_ = pe.transpose(o[:, ch // 4, P * (ch % 4):P * (ch % 4 + 1)], bk[d][:, P * ch:P * (ch + 1)], ident)
                    i_.then_inc(*full(s))
                    s, o = take()
                    if d == 0:
                        pe.wait_ge(*E.count("vs_ready").next())
                    for q in range(4):
                        i_ = pe.transpose(o[:, 0, P * q:P * (q + 1)], at[d][:, P * q:P * (q + 1)], ident)
                        if d == 0:
                            i_ = pe.transpose(o[:, 1, P * q:P * (q + 1)], vS[:, P * q:P * (q + 1)], ident)
                    i_.then_inc(*full(s))
                    for p in range(2):
                        s, o = take()
                        for q in range(4):
                            for f, h in ((0, 0), (1, 1), (0, 1), (1, 0)):
                                hs = slice(64 * h, 64 * h + 64)
                                ch = 2 * q + p
                                i_ = mm(o[64 * f:64 * f + 64, h, P * q:P * (q + 1)].rearrange("p (a t) -> p a t", a=2),
                                        bk[d][hs, P * ch + 64 * f:P * ch + 64 * f + 64], art[d][hs, ch])
                        i_.then_inc(*full(s))

                def each(o, bank, l, r, w=RC, off=0):
                    for e in range(8):
                        for p in range(2):
                            pp = slice(64 * p, 64 * p + 64)
                            i2 = mm(o[pp, bank + (e * w) // 512, (e * w) % 512:(e * w) % 512 + w], l(pp, e), r(pp, e))
                    return i2

                def halves(o, off, l, r):
                    for e in range(8):
                        for g in range(4):
                            pp = slice(HB * g, HB * g + HB)
                            i2 = mm(o[pp, 0, off + HB * e:off + HB * (e + 1)], l[pp, e, :], r(pp, e) if callable(r) else r[pp, e, :])
                    return i2

                for d in range(2):
                    pe.wait_ge(*E.count("aa_ready").next())
                    s, o = take()
                    halves(o, 0, Dh[d], lambda pp, e: id32[pp]).then_inc(*full(s))
                for m in range(1, 6):
                    if m == 1 and tail:
                        tail_mean(c - 1)
                    if m == 2 and front:
                        front_sum()
                    if m == 2 and tail:
                        tail_var()
                    if m == 2 and front:
                        front_lora(0)
                    if m == 4 and front:
                        front_lora(1)
                    for d in range(2):
                        pe.wait_ge(*E.count("xn_ready").next())
                        s, o = take()
                        if m < 5:
                            i_ = halves(o, 0, Dh[d], Xh[d])
                        else:
                            for e in range(8):
                                for p in range(2):
                                    a, b = slice(*across[d][p]), slice(*across[1 - d][p])
                                    i_ = mm(o[b, 0, HB * e:HB * (e + 1)], AA[d][p][a, e, 0, HB * (1 - d):HB * (2 - d)], Xh[d][a, e, :])
                        i_.then_inc(*full(s))
                    for d in range(2):
                        pe.wait_ge(*E.count("q_ready").next())
                        s, o = take()
                        if m < 5:
                            halves(o, 0, Qh[d], Nh[d])
                            i_ = halves(o, 256, Nh[d], Qh[d])
                        else:
                            for e in range(8):
                                for p in range(2):
                                    a, b = slice(*across[d][p]), slice(*across[1 - d][p])
                                    i_ = mm(o[a, 0, HB * e:HB * (e + 1)], Qh[d][b, e, :], Nh[d][b, e, :])
                        i_.then_inc(*full(s))
                for d in range(2):
                    if d == 0:
                        pe.wait_ge(*E.count("vtok_ready").next())
                    s, o = take()
                    for e in range(8):
                        for p in range(2):
                            kh, hs = slice(64 - 64 * p, 128 - 64 * p), slice(64 * p, 64 * p + 64)
                            i_ = mm(o[hs, 0, RC * e:RC * (e + 1)], AA[d][p][kh, e, 0, :], UV[d][p][kh, e, :])
                    i_.then_inc(*full(s))
                for d in range(2):
                    pe.wait_ge(*E.count("xn_ready").next())
                    pe.wait_ge(*E.count("r_ready").next())
                    pe.wait_ge(*E.count("tok_ready").next())
                    s, o = take()
                    each(o, 0, lambda pp, e: Ni[d][pp, e, :], lambda pp, e: RA[d][pp, e], w=P).then_inc(*full(s))

                def cross(o, l, r, whole, qs=range(4)):
                    for q in qs:
                        for p, h in ((0, 0), (1, 1), (0, 1), (1, 0)):
                            pp = slice(0, P) if whole else slice(64 * p, 64 * p + 64)
                            i2 = mm(o[64 * h:64 * h + 64, p, RC * q:RC * (q + 1)], l(pp, p, h, q), r(pp, p, h, q))
                    return i2

                def G(pp, p, h, q):
                    return Qi[d][pp, 4 * h + q, :]

                def uv(pp, p, h, q):
                    return UV[d][p][pp, 4 * h + q, :]

                def b_k(pp, p, h, q):
                    return BK[d][pp, 2 * q + p, h, :]

                def inclusive(pp, p, h, q):
                    return AA[d][p][pp, 4 * h + q, 1, :]

                for d in range(2):
                    pe.wait_ge(*E.count("ug_ready").next())
                    s, o = take()
                    cross(o, G, b_k, False).then_inc(*full(s))
                for d in range(2):
                    s, o = take()
                    cross(o, b_k, uv, True).then_inc(*full(s))
                qs = range(o_lo // P, 4)
                for k in range(2, NRC):
                    for d in range(2):
                        prev = RW_ORDER[d][k - 1]
                        pe.wait_ge(*E.count("s_ready").next())
                        s, o = take()
                        for h in range(2):
                            hs = slice(64 * h, 64 * h + 64)
                            i_ = mm(o[hs, 0, 0:RC], MT[d][hs, prev, :], Ni[d][hs, prev, :])
                        i_.then_inc(*full(s))
                    if k < 6:
                        d = k % 2
                        s, o = take()
                        if k < 4:
                            cross(o, G, inclusive, False, qs).then_inc(*full(s))
                        else:
                            cross(o, uv, inclusive, True, qs).then_inc(*full(s))
                s, o = take()
                for d in range(2):
                    pe.wait_ge(*E.count("s_ready").next())
                    pe.wait_ge(*E.count("rp_ready").next())
                    passed()
                    for ch in range(o_lo // RC, NRC):
                        for h in range(2):
                            hs = slice(64 * h, 64 * h + 64)
                            i_ = mm(o[hs, d, RC * ch:RC * (ch + 1)], Ni[d][hs, ch, :], rq[d][hs, RC * ch:RC * (ch + 1)])
                i_.then_inc(*full(s))

            def rwkv():
                front_sum()
                front_lora(0)
                front_lora(1)
                rwkv_tile(0, True, False)
                with E.loop(KT - 2) as i:
                    rwkv_tile(i + 1, True, True)
                rwkv_tile(KT - 1, False, True)
                tail_mean(KT - 1)
                tail_var()

            def ffn_down(lo_, hi):
                slots = [take() for _ in range(SLOTS)]

                def blk(first, last):
                    w = weights().rearrange("p (k m) -> p k m", k=2)
                    return w

                for b in range(B_FO):
                    w = weights().rearrange("p (k m) -> p k m", k=2)
                    for k in range(2):
                        for m in range(8):
                            s, o = slots[m // 2]
                            i_ = mm(o[:, m % 2, 0:hi - lo_], w[:, k, P * m:P * (m + 1)], A[:, 2 * b + k, lo_:hi],
                                    b + k == 0, b == B_FO - 1 and k == 1)
                            if k == 0 and m == 0:
                                i_.then_inc(*E.count("w_used").sent())
                            if b == B_FO - 1 and k == 1 and m % 2:
                                i_.then_inc(*full(s))

            pe.wait_ge(*E.count("dma_const").next())
            E.count("dma_const")
            pe.wait_ge(sems["dma_const"], 16 * 5)
            pe.wait_ge(*E.count("cond_ready").next())
            for L in range(DEPTH):
                o_lo, o_hi = N_OUT[L]
                adaln()
                pe.wait_ge(*E.count("sq_ready").next())
                channel_sum(SQ, KT)
                pe.wait_ge(*E.count("h_ctx_ready").next())
                pe.wait_ge(*E.count("h_lat_ready").next())
                dense(hT, B_XBC)
                pe.wait_ge(*E.count("scr_free").next())
                ssd()
                dense(hT, B_Z, o_lo, o_hi)
                pe.wait_ge(*E.count("ysq_ready").next())
                for g in range(GROUPS):
                    channel_sum(YSQ[g], 4, o_lo, o_hi)
                pe.wait_ge(*E.count("yn_ready").next())
                with E.loop(2):
                    for _ in range(4):
                        w = weights().rearrange("p (k m) -> p k m", k=XS_T)
                        s, o = take()
                        for k in range(XS_T):
                            i_ = mm(o[:, 0, 0:o_hi - o_lo], w[:, k, :], A[:, k, o_lo:o_hi], k == 0, k == XS_T - 1)
                            if k == 0:
                                i_.then_inc(*E.count("w_used").sent())
                        i_.then_inc(*full(s))
                dense(hT, B_GS, o_lo, o_hi)
                dense(hT, B_RKV)
                dense_block(hT, 0, T)
                dense_block(hT, 0, T, tiles=1)
                pe.wait_ge(*E.count("lora_ready").next())
                rwkv()
                pe.wait_ge(*E.count("yr_ready").next())
                dense(A, B_RO, o_lo, o_hi)
                dense(hT, B_GR, o_lo, o_hi)
                pe.wait_ge(*E.count("o_ready").next())
                dense(O, B_WO, o_lo, o_hi)
                pe.wait_ge(*E.count("sq_ready").next())
                channel_sum(SQ, KT, o_lo, o_hi)
                pe.wait_ge(*E.count("sq_ready").next())
                channel_sum(SQ, KT, o_lo, o_hi)
                if L == 0:
                    pe.wait_ge(*E.count("h_ctx_ready").next())
                pe.wait_ge(*E.count("h_lat_ready").next())
                dense(hT, B_FI, o_lo, o_hi)
                pe.wait_ge(*E.count("ffn_ready").next())
                ffn_down(o_lo, o_hi)
                pe.wait_ge(*E.count("sq_ready").next())
                channel_sum(SQ, KT, o_lo, o_hi)

        @block.scalar
        def _(act):
            E = Engine(act, "act", sems, table)
            go = act.activation

            def rstd(lo_, hi, scale, eps, out_, bank=0):
                s, w = E.full()
                act.wait_ge(*w)
                go(out_[:, 0:hi - lo_], ps[:, 2 * s + bank, 0:hi - lo_], ACT.Sqrt, bias=eps, scale=scale).then_inc(*E.freed(s))

            def square_x(src, lo_, hi):
                go(SQ[:, :, lo_:hi], src[:, :, lo_:hi], ACT.Square).then_inc(*E.done("sq_ready"))

            def modulate_ctx(shift):
                act.wait_ge(*E.count("norm_ready").next())
                for k in range(KT):
                    i_ = go(hT[:, k, 0:CTX], SQ[:, k, 0:CTX], ACT.Identity, bias=mod[:, 8 * shift + k, 1:2], scale=gsc[:, k, 1:2])
                i_.then_inc(*E.done("h_ctx_ready"))

            def passed():
                if E.loop_now:
                    act.sem_inc(sems["act_passed"], 1)

            def conv_tiles(name, bias, silu, trips):
                with E.loop(trips) as i:
                    for b in range(4):
                        s, w = E.full()
                        act.wait_ge(*w)
                        passed()
                        for m in range(2):
                            t = i * 8 + (2 * b + m)
                            go(A[:, t, :], ps[:, 2 * s + m, :], ACT.Identity, bias=colr(L, bias, t) if bias else 0.0,
                               scale=colr(L, name, 24 + t)).then_inc(*E.done("tap_ready"))
                        if silu:
                            for m in range(2):
                                t = i * 8 + (2 * b + m)
                                act.wait_ge(*E.count("conv_ready").next())
                                passed()
                                go(A[:, t, :], A[:, t, :], ACT.Silu).then_inc(*E.done("conv_silu"))

            def ssd():
                E.skip(1)
                act.wait_ge(*E.count("abs_ready").next())
                go(sm_a, sm_a, ACT.Abs).then_inc(*E.done())
                act.wait_ge(*E.mine())
                go(sm_a, sm_a, ACT.Exp, scale=-1.0).then_inc(*E.done())
                go(expA, headp[:, L, 1], ACT.Exp).then_inc(*E.done())
                act.wait_ge(*E.mine())
                go(sm_b, sm_a, ACT.Ln, bias=1.0).then_inc(*E.done("log_ready"))
                E.skip(1)
                act.wait_ge(*E.count("dec_in_ready").next())
                go(dec, dec, ACT.Exp).then_inc(*E.done())
                go(wde, wde, ACT.Exp).then_inc(*E.done("dec_ready"))
                with E.loop(GROUPS):
                    s, w = E.full()
                    act.wait_ge(*w)
                    go(btok.rearrange("p c n -> p (c n)"), ps[:, 2 * s, :], ACT.Copy).then_inc(*E.done("btok_ready"))
                    act.wait_ge(*E.mine())
                    act.sem_inc(*E.freed(s))
                    for part in ((0, 1), (2,), (3,)):
                        s, w = E.full()
                        act.wait_ge(*w)
                        c, n = part[0], len(part)
                        go(scr[:, 5632 + 512 * c:5632 + 512 * (c + n)], ps[:, 2 * s:2 * s + n, :].rearrange("p b t -> p (b t)"), ACT.Copy)\
                            .then_inc(*E.freed(s))
                    E.skip(4)
                    for c in range(NCH):
                        for d in range(2):
                            s, w = E.full()
                            act.wait_ge(*w)
                            act.wait_ge(*E.count("diff_ready").next())
                            if SSD_ORDER[d].index(c):
                                go(Cb[c % 2][d], ps[:, 2 * s:2 * s + 2, :].rearrange("p b (h l) -> p (b h) l", h=4), ACT.Exp)\
                                    .then_inc(*E.done("ec_ready"))
                                act.wait_ge(*E.mine())
                            act.sem_inc(*E.freed(s))
                            go(Wb[c % 2][d], Wb[c % 2][d], ACT.Exp).then_inc(*E.done("e_ready"))
                        if c:
                            E.skip(1)
                    E.skip(1)

            def front_norm():
                E.skip(1)
                act.wait_ge(*E.count("kkmax_ready").next())
                go(exc, exc, ACT.Sqrt).then_inc(*E.done("kkstd_ready"))

            def front_sigmoids(c, d):
                s, w = E.full()
                act.wait_ge(*w)
                if front_sigmoids.later:
                    act.wait_ge(*E.count("ops_ready").next())
                front_sigmoids.later = True
                passed()
                go(sg, ps[:, 2 * s, :], ACT.Sigmoid, bias=colr(L, "w0", c + 8 * d)).then_inc(*E.done())
                go(asg, ps[:, 2 * s + 1, :], ACT.Sigmoid, bias=colr(L, "a0", c + 8 * d)).then_inc(*E.freed(s))
                act.wait_ge(*E.mine())
                act.sem_inc(*E.done("sa_ready"))
            front_sigmoids.later = False

            def front_decays(d):
                act.wait_ge(*E.count("cum_ready").next())
                go(wc[d], e8(pre)[:, :, RC - 1], ACT.Exp, scale=-WSCALE).then_inc(*E.done())
                go(exc, exc, ACT.Exp, scale=-WSCALE).then_inc(*E.done())
                go(sg, inc, ACT.Exp, scale=-WSCALE).then_inc(*E.done())
                act.wait_ge(*E.mine())
                go(inc, inc, ACT.Exp, scale=WSCALE).then_inc(*E.done("exps_ready"))

            def tail_square():
                E.skip(1)
                act.wait_ge(*E.count("yc_ready").next())
                go(ycsq[:, lo_:T], yc[:, lo_:T], ACT.Square).then_inc(*E.done("ycsq_ready"))

            def tail_std():
                s, w = E.full()
                act.wait_ge(*w)
                go(ystd[:, lo_:T], ps[:, 2 * s, lo_:T], ACT.Sqrt, bias=LN_EPS, scale=1.0 / 64).then_inc(*E.done("ystd_ready"))

            def rwkv_tile(c, front, tail):
                if tail:
                    act.wait_ge(*E.count("yb_ready").next())
                for d in range(2):
                    s, w = E.full()
                    act.wait_ge(*w)
                    go(BK[d].rearrange("p c h k -> p (c h k)"), ps[:, 2 * s:2 * s + 2, :].rearrange("p b x -> p (b x)"), ACT.Copy).then_inc(*E.freed(s))
                    s, w = E.full()
                    act.wait_ge(*w)
                    if d == 0:
                        for p in range(2):
                            kh = slice(64 - 64 * p, 128 - 64 * p)
                            for d_ in range(2):
                                i_ = go(UV[d_][p][kh].rearrange("p (h q) k -> p q h k", h=2),
                                        ps[kh, 2 * s + 1, :].rearrange("p (q h k) -> p q h k", q=4, h=2), ACT.Copy)
                        i_.then_inc(*E.done("vtok_ready"))
                    go(RAq[d][:, :, :, 1, :], ps[:, 2 * s, :].rearrange("p (q h k) -> p q h k", q=4, h=2), ACT.Copy).then_inc(*E.done("tok_ready"))
                    act.wait_ge(*E.mine())
                    act.sem_inc(*E.freed(s))
                    E.skip(2)
                E.skip(2)
                for m in range(1, 6):
                    if m == 1 and tail:
                        tail_square()
                    if m == 2 and front:
                        front_norm()
                    if m == 2 and tail:
                        tail_std()
                    if front and m in (2, 4):
                        front_sigmoids(c + 1, (m - 2) // 2)
                    if front and m in (3, 5):
                        front_decays((m - 3) // 2)
                    E.skip(4)
                for d in range(2):
                    s, w = E.full()
                    act.wait_ge(*w)
                    go(RA[d][:, :, 0, :], e8(ps[:, 2 * s, :]), ACT.Copy).then_inc(*E.done("r_ready"))
                    act.wait_ge(*E.mine())
                    act.sem_inc(*E.freed(s))
                for d in range(2):
                    s, w = E.full()
                    act.wait_ge(*w)
                    ug = ps[:, 2 * s:2 * s + 2, :].rearrange("p b (e a t) -> p (b e) a t", e=4, a=2)
                    for p in range(2):
                        hs = slice(64 * p, 64 * p + 64)
                        go(UV[d][p][hs], ug[hs, :, 0, :], ACT.Copy).then_inc(*E.done())
                    go(Qi[d], ug[:, :, 1, :], ACT.Copy).then_inc(*E.done("ug_ready"))
                    act.wait_ge(*E.mine())
                    act.sem_inc(*E.freed(s))
                E.skip(2 + 2 + 12 + 2 + 2 + 1)

            def rwkv():
                front_norm()
                for d in range(2):
                    front_sigmoids(0, d)
                    front_decays(d)
                rwkv_tile(0, True, False)
                with E.loop(KT - 2) as i:
                    rwkv_tile(i + 1, True, True)
                rwkv_tile(KT - 1, False, True)
                tail_square()
                tail_std()
                E.count("yb_ready").n += 1

            act.wait_ge(sems["dma_const"], 16 * 5)
            go(cond[:, :, :], cond[:, :, :], ACT.Silu).then_inc(*E.done("cond_ready"))
            for L in range(DEPTH):
                lo_, hi = N_OUT[L]
                n = hi - lo_
                with E.loop(6):
                    for r in range(2):
                        s, w = E.full()
                        act.wait_ge(*w)
                        go(rows[0:2, r, :], ps[0:2, 2 * s, :], ACT.Copy).then_inc(*E.done("row_ready"))
                        act.wait_ge(*E.mine())
                        act.sem_inc(*E.freed(s))
                    E.skip(2)
                act.wait_ge(*(E.count("dma_x").next() if L == 0 else E.count("x_ready").so_far()))
                square_x(X, 0, T)
                rstd(0, T, 1.0 / D, EPS, rst)
                modulate_ctx(0)
                conv_tiles("scw", "scb", True, 3)
                ssd()
                with E.loop(2) as i:
                    for b in range(4):
                        s, w = E.full()
                        act.wait_ge(*w)
                        act.wait_ge(*E.count("yz_ready").so_far())
                        E.count("yz_ready").n += 1
                        go(ZS[:, b % 2, :, 0:n], ps[:, 2 * s:2 * s + 2, 0:n], ACT.Silu).then_inc(*E.done("zs_ready"))
                        act.wait_ge(*E.mine())
                        act.sem_inc(*E.freed(s))
                act.wait_ge(*E.count("yz_ready").so_far())
                for g in range(GROUPS):
                    i_ = go(YSQ[g][:, :, lo_:hi], A[:, 4 * g:4 * g + 4, lo_:hi], ACT.Square)
                i_.then_inc(*E.done("ysq_ready"))
                for g in range(GROUPS):
                    rstd(lo_, hi, 4.0 / D_SSM, EPS, GR[g])
                with E.loop(2) as i:
                    for b in range(4):
                        s, w = E.full()
                        act.wait_ge(*w)
                        passed()
                        go(O[:, i * 4 + b, lo_:hi], ps[:, 2 * s, 0:n], ACT.Copy).then_inc(*E.freed(s))
                for b in range(4):
                    s, w = E.full()
                    act.wait_ge(*w)
                    go(SG[:, 2 * b:2 * b + 2, lo_:hi], ps[:, 2 * s:2 * s + 2, 0:n], ACT.Sigmoid).then_inc(*E.freed(s))
                act.wait_ge(*E.mine())
                act.sem_inc(*E.done("gate_ready"))
                conv_tiles("rcw", None, False, 3)
                E.count("conv_ready").n += RK_T
                s, w = E.full()
                act.wait_ge(*w)
                go(lo[:, 0, :], ps[:, 2 * s, :], ACT.Tanh).then_inc(*E.done())
                go(lo[:, 1, :], ps[:, 2 * s + 1, :], ACT.Copy).then_inc(*E.freed(s))
                s, w = E.full()
                act.wait_ge(*w)
                go(lo[:, 2, :], ps[:, 2 * s, :], ACT.Sigmoid).then_inc(*E.freed(s))
                act.wait_ge(*E.mine())
                act.sem_inc(*E.done("lora_ready"))
                rwkv()
                for b in range(4):
                    s, w = E.full()
                    act.wait_ge(*w)
                    go(SG[:, 2 * b:2 * b + 2, lo_:hi], ps[:, 2 * s:2 * s + 2, 0:n], ACT.Copy).then_inc(*E.freed(s))
                for b in range(4):
                    s, w = E.full()
                    act.wait_ge(*w)
                    go(lo[:, 0:2, 0:n], ps[:, 2 * s:2 * s + 2, 0:n], ACT.Sigmoid).then_inc(*E.done("gate_ready"))
                    act.wait_ge(*E.count("out_ready").next())
                    act.wait_ge(*E.mine())
                    act.sem_inc(*E.freed(s))
                for b in range(4):
                    s, w = E.full()
                    act.wait_ge(*w)
                    go(hT[:, 2 * b:2 * b + 2, lo_:hi], ps[:, 2 * s:2 * s + 2, 0:n], ACT.Copy).then_inc(*E.freed(s))
                act.wait_ge(*E.mine())
                square_x(hT, lo_, hi)
                rstd(lo_, hi, 1.0 / D, EPS, rst)
                act.wait_ge(*E.count("x_ready").next())
                square_x(X, lo_, hi)
                rstd(lo_, hi, 1.0 / D, EPS, rst)
                if L == 0:
                    modulate_ctx(3)
                def ffn_tile(s, w, t):
                    act.wait_ge(*w)
                    passed()
                    go(A[:, t, lo_:hi], ps[:, 2 * s, 0:n], ACT.Identity, bias=colr(L, "fcb", t), scale=colr(L, "fcw", 4 * FF_T + t))\
                        .then_inc(*E.done("tap2_ready"))
                    act.wait_ge(*E.count("conv_ready").next())
                    passed()
                    go(A[:, t, lo_:hi], A[:, t, lo_:hi], ACT.Gelu_apprx_tanh).then_inc(*E.done("gelu_ready"))
                with E.loop(5) as i:
                    for b in range(4):
                        ffn_tile(*E.full(), i * 4 + b)
                for t in range(20, 22):
                    ffn_tile(*E.full(), t)
                for b in range(4):
                    s, w = E.full()
                    act.wait_ge(*w)
                    go(O[:, 2 * b:2 * b + 2, lo_:hi], ps[:, 2 * s:2 * s + 2, 0:n], ACT.Copy).then_inc(*E.freed(s))
                act.wait_ge(*E.mine())
                square_x(O, lo_, hi)
                rstd(lo_, hi, 1.0 / D, EPS, rst)
                E.count("x_ready").n += 1


        @block.vector
        def _(v):
            E = Engine(v, "dve", sems, table)
            tt, ts, stt = v.tensor_tensor, v.tensor_scalar, v.scalar_tensor_tensor

            def own():
                v.wait_ge(*E.mine())

            def recip(lo_, hi):
                s, w = E.full()
                v.wait_ge(sems[f"slot_free{s}"], E.count(f"slot_free{s}").so_far()[1])
                v.reciprocal(rst[:, 0:hi - lo_], rst[:, 0:hi - lo_]).then_inc(*E.done())

            def permuted(ap, L):
                return ap.rearrange("p (w r) -> p r w", r=ROWS) if L == 1 else ap.rearrange("p (r w) -> p r w", r=ROWS)

            def grid(ap):
                return ap.rearrange("p (r w) -> p r w", r=ROWS)

            def prenorm(L, gain, shift, perm, lo_=0):
                own()
                stt(out=gsc[:, :, :], in0=mod[:, 8 * (shift + 1):8 * (shift + 2), :], scalar=1.0,
                    in1=par[:, L, COLS[gain]:COLS[gain] + 8].unsqueeze(2).to_broadcast((P, KT, 2)), op0=ALU.add, op1=ALU.mult)\
                    .then_inc(*E.done())
                recip(lo_, T)
                own()
                tt(SQ[:, :, lo_:T], X[:, :, lo_:T], rst[:, 0:T - lo_].unsqueeze(1).to_broadcast((P, KT, T - lo_)), ALU.mult)\
                    .then_inc(*E.done("norm_ready"))
                own()
                for k in range(KT):
                    i_ = ts(permuted(hT[:, k, CTX:T], 1 if perm else 0), grid(SQ[:, k, CTX:T]), gsc[:, k, 0:1], mod[:, 8 * shift + k, 0:1],
                            ALU.mult, ALU.add)
                i_.then_inc(*E.done("h_lat_ready"))

            def postnorm(L, src, gain, gate, perm, lo_):
                own()
                tt(gsc[:, :, :], mod[:, 8 * gate:8 * gate + 8, :],
                   par[:, L, COLS[gain]:COLS[gain] + 8].unsqueeze(2).to_broadcast((P, KT, 2)), ALU.mult).then_inc(*E.done())
                recip(lo_, T)
                own()
                tt(SQ[:, :, lo_:T], src[:, :, lo_:T], rst[:, 0:T - lo_].unsqueeze(1).to_broadcast((P, KT, T - lo_)), ALU.mult)\
                    .then_inc(*E.done())
                own()
                for k in range(KT):
                    if lo_ == 0:
                        stt(out=X[:, k, 0:CTX], in0=SQ[:, k, 0:CTX], scalar=gsc[:, k, 1:2], in1=X[:, k, 0:CTX], op0=ALU.mult, op1=ALU.add)
                    i_ = stt(out=grid(X[:, k, CTX:T]), in0=permuted(SQ[:, k, CTX:T], 1 if perm else 0), scalar=gsc[:, k, 0:1],
                             in1=grid(X[:, k, CTX:T]), op0=ALU.mult, op1=ALU.add)
                i_.then_inc(*E.done("x_ready"))

            def conv_tiles(name, trips):
                with E.loop(trips) as i:
                    for b in range(4):
                        s, w = E.full()
                        for m in range(2):
                            t = i * 8 + (2 * b + m)
                            v.wait_ge(*E.count("tap_ready").next())
                            src, dst = seg2(ps[:, 2 * s + m, :]), seg2(A[:, t, :])
                            stt(out=dst[:, :, 1:256], in0=src[:, :, 0:255], scalar=colr(L, name, t), in1=dst[:, :, 1:256],
                                op0=ALU.mult, op1=ALU.add).then_inc(*E.done())
                            own()
                            i_ = stt(out=dst[:, :, 0:255], in0=src[:, :, 1:256], scalar=colr(L, name, 48 + t), in1=dst[:, :, 0:255],
                                     op0=ALU.mult, op1=ALU.add)
                            i_.then_inc(*E.done("conv_ready"))
                        own()
                        v.sem_inc(*E.freed(s))

            def ssd():
                s, w = E.full()
                v.wait_ge(*w)
                raw = ps[:, 2 * s, 0:P].rearrange("p (c h) -> p c h", c=NCH)
                for d in range(2):
                    i_ = tt(heads4(sm_a)[:, d], raw, headp[:, L, 0, d, :].unsqueeze(1).to_broadcast((P, NCH, HEADS)), ALU.add)
                i_.then_inc(*E.freed(s))
                own()
                ts(dtv, sm_a, 0.0, None, ALU.max).then_inc(*E.done("abs_ready"))
                v.wait_ge(*E.count("log_ready").next())
                ts(sm_c, sm_a, 1.0, None, ALU.add).then_inc(*E.done())
                own()
                stt(out=sm_a, in0=sm_c, scalar=-1.0, in1=sm_a, op0=ALU.add, op1=ALU.subtract).then_inc(*E.done())
                own()
                v.reciprocal(sm_c, sm_c).then_inc(*E.done())
                own()
                tt(sm_a, sm_a, sm_c, ALU.mult).then_inc(*E.done())
                tt(dtv, dtv, sm_b, ALU.add).then_inc(*E.done())
                own()
                tt(dtv, dtv, sm_a, ALU.subtract).then_inc(*E.done())
                own()
                for d in range(2):
                    i_ = stt(out=heads4(dta)[:, d], in0=heads4(dtv)[:, d], scalar=-1.0,
                             in1=expA[:, HEADS * d:HEADS * (d + 1)].unsqueeze(1).to_broadcast((P, NCH, HEADS)), op0=ALU.mult, op1=ALU.mult)
                i_.then_inc(*E.done("dta_ready"))
                s, w = E.full()
                v.wait_ge(*w)
                ts(ncs, ps[:, 2 * s, 0:256], -1.0, None, ALU.mult).then_inc(*E.done())
                v.tensor_copy(dec, ps[:, 2 * s + 1, 0:256]).then_inc(*E.freed(s))
                own()
                tt(wde, dec, ncs, ALU.add).then_inc(*E.done("dec_in_ready"))
                v.wait_ge(*E.count("dec_ready").next())
                tt(wde, wde, dtv, ALU.mult).then_inc(*E.done("wdec_ready"))
                own()
                with E.loop(GROUPS) as g:
                    hsl = bass.ds(g * HPG, HPG)

                    def per_head(ap, d, c):
                        return heads4(ap)[:, d, c, hsl].unsqueeze(2).to_broadcast((P, HPG, 64))

                    E.skip(2)
                    for _ in range(2):
                        s, w = E.full()
                    v.wait_ge(sems[f"slot_free{(s - 2) % SLOTS}"], E.count(f"slot_free{(s - 2) % SLOTS}").so_far()[1])
                    v.wait_ge(sems[f"slot_free{(s - 1) % SLOTS}"], E.count(f"slot_free{(s - 1) % SLOTS}").so_far()[1])
                    v.wait_ge(sems[f"slot_free{s}"], E.count(f"slot_free{s}").so_far()[1])
                    for o_ in range(3):
                        for d in range(2):
                            c = SSD_ORDER[d][o_]
                            tt(xw[d], xtok[:, c], per_head(wde, d, c), ALU.mult).then_inc(*E.done("xw_ready"))
                        s, w = E.full()
                        v.wait_ge(*w)
                        for d in range(2):
                            c = SSD_ORDER[d][o_]
                            st = ps[:, 2 * s + d, :].rearrange("p (h x) -> p h x", h=HPG)
                            if o_ == 0:
                                v.tensor_copy(Hs[d][0], st).then_inc(*E.done())
                            else:
                                tt(Hs[d][o_], Hs[d][o_ - 1], per_head(dec, d, c), ALU.mult).then_inc(*E.done())
                                own()
                                tt(Hs[d][o_], Hs[d][o_], st, ALU.add).then_inc(*E.done())
                        own()
                        v.sem_inc(*E.freed(s))
                    s, w = E.full()
                    v.wait_ge(*w)
                    for d in range(2):
                        i_ = tt(cbm[d], ps[:, 2 * s, :].rearrange("p (c l) -> p c l", c=NCH), tri[d].unsqueeze(1).to_broadcast((P, NCH, P)), ALU.mult)
                    i_.then_inc(*E.freed(s))
                    own()

                    def differences(c):
                        for d in range(2):
                            s, w = E.full()
                            v.wait_ge(*w)
                            for h in range(HPG):
                                i_ = ts(Wb[c % 2][d][:, h, :], ps[:, 2 * s + h // 4, P * (h % 4):P * (h % 4 + 1)],
                                        heads4(ncs)[:, d, c, bass.ds(g * HPG + h, 1)], 0.0, ALU.add, ALU.min)
                            i_.then_inc(*E.done("diff_ready"))

                    differences(0)
                    for c in range(NCH):
                        if c + 1 < NCH:
                            differences(c + 1)
                        for d in range(2):
                            v.wait_ge(*E.count("e_ready").next())
                            i_ = tt(Wb[c % 2][d], Wb[c % 2][d], cbm[d][:, c, :].unsqueeze(1).to_broadcast((P, HPG, P)), ALU.mult)
                        i_.then_inc(*E.done("w_ready"))
                        s, w = E.full()
                        v.wait_ge(*w)
                        for j in range(4):
                            i_ = stt(out=A[:, g * 4 + j, Q * c:Q * (c + 1)], in0=A[:, g * 4 + j, Q * c:Q * (c + 1)],
                                     scalar=colr(L, "dskip", g * 4 + j), in1=ps[:, 2 * s, P * j:P * (j + 1)], op0=ALU.mult, op1=ALU.add)
                        i_.then_inc(*E.done("y_ready"))
                        own()
                        v.sem_inc(*E.freed(s))

            def front_square(c):
                own()
                ts(kkn, A[:, 8 + c, :], colr(L, "kk", c), None, ALU.mult).then_inc(*E.done())
                own()
                tt(exc, kkn, kkn, ALU.mult).then_inc(*E.done("kksq_ready"))

            def front_max():
                s, w = E.full()
                v.wait_ge(*w)
                ts(exc, ps[:, 2 * s, :], 1e-24, None, ALU.max).then_inc(*E.done("kkmax_ready"))
                own()
                v.sem_inc(*E.freed(s))

            def front_norm():
                v.wait_ge(*E.count("kkstd_ready").next())
                v.reciprocal(exc, exc).then_inc(*E.done())
                own()
                tt(kkn, kkn, exc, ALU.mult).then_inc(*E.done())

            def front_cumulate(d):
                own()
                v.wait_ge(*E.count("sa_ready").next())
                v.tensor_tensor_scan(pre, reset, sg, 0.0, ALU.mult, ALU.add).then_inc(*E.done())
                own()
                if d == 0:
                    tt(exc, pre, sg, ALU.subtract).then_inc(*E.done())
                    i_ = v.tensor_copy(inc, pre)
                else:
                    tt(e8(exc), e8(pre)[:, :, RC - 1:RC].to_broadcast((P, 8, RC)), e8(pre), ALU.subtract).then_inc(*E.done())
                    own()
                    i_ = tt(inc, exc, sg, ALU.add)
                i_.then_inc(*E.done("cum_ready"))

            def front_operands(c, d):
                r_, k_ = A[:, c, :], A[:, 8 + c, :]
                v.wait_ge(*E.count("exps_ready").next())
                kd = pre
                ts(kd, asg, -1.0, colr(L, "ka", c), ALU.add, ALU.mult).then_inc(*E.done())
                own()
                stt(out=kd, in0=kd, scalar=1.0, in1=k_, op0=ALU.add, op1=ALU.mult).then_inc(*E.done())
                stt(out=at[d], in0=kkn, scalar=-1.0, in1=exc, op0=ALU.mult, op1=ALU.mult)
                tt(rt[d], r_, sg, ALU.mult)
                tt(bt[d], quads(kkn), quads(asg), ALU.mult).then_inc(*E.done())
                own()
                if d == 0:
                    v.tensor_copy(kds, kd)
                else:
                    tt(kds, kds, kd, ALU.add).then_inc(*E.done())
                    own()
                    stt(out=k_, in0=kds, scalar=colr(L, "rk", c), in1=r_, op0=ALU.mult, op1=ALU.mult)
                tt(bt[d], bt[d], quads(inc), ALU.mult)
                tt(kt[d], quads(kd), quads(inc), ALU.mult).then_inc(*E.done("ops_ready"))

            def tail_center(c):
                s, w = E.full()
                v.wait_ge(*w)
                stt(out=yc[:, lo_:T], in0=ps[:, 2 * s, lo_:T], scalar=-1.0 / 64, in1=yac[:, lo_:T], op0=ALU.mult, op1=ALU.add).then_inc(*E.done("yc_ready"))
                tt(bonus[:, lo_:T], ps[:, 2 * s + 1, lo_:T], A[:, 16 + c, lo_:T], ALU.mult).then_inc(*E.freed(s))

            def tail_norm(c):
                s, w = E.full()
                v.wait_ge(*w)
                v.wait_ge(*E.count("ystd_ready").next())
                y, rs = yc[:, lo_:T], ystd[:, lo_:T]
                v.reciprocal(rs, rs).then_inc(*E.done())
                own()
                tt(y, y, rs, ALU.mult).then_inc(*E.done())
                own()
                ts(y, y, colr(L, "lnw", c), colr(L, "lnb", c), ALU.mult, ALU.add).then_inc(*E.done())
                own()
                tt(y, y, bonus[:, lo_:T], ALU.add).then_inc(*E.done())
                own()
                tt(A[:, c, lo_:T], y, ps[:, 2 * s + 1, lo_:T], ALU.mult).then_inc(*E.freed(s))

            def rwkv_tile(c, front, tail):
                own()
                for d in range(2):
                    v.tensor_copy(rq[d], rt[d]).then_inc(*E.done())
                    v.tensor_copy(wcu[d], wc[d]).then_inc(*E.done())
                own()
                for d in range(2):
                    E.skip(2)
                    for p in range(2):
                        s, w = E.full()
                        v.wait_ge(*w)
                        tt(AA[d][p].rearrange("p e a t -> p e (a t)"), ps[:, 2 * s:2 * s + 2, :].rearrange("p b (q x) -> p (b q) x", q=4),
                           mask2[d].unsqueeze(1).to_broadcast((P, 8, P)), ALU.mult).then_inc(*E.freed(s))
                    own()
                    for p in range(2):
                        hs = slice(64 * p, 64 * p + 64)
                        ts(Nh[d][hs], AA[d][p][hs, :, 0, 0:HB], half[hs, 0:1], None, ALU.mult).then_inc(*E.done())
                    own()
                    for p in range(2):
                        hs = slice(64 * p, 64 * p + 64)
                        i_ = stt(out=Dh[d][hs], in0=AA[d][p][hs, :, 0, HB:RC], scalar=half[hs, HB:HB + 1], in1=Nh[d][hs], op0=ALU.mult, op1=ALU.add)
                    i_.then_inc(*E.done("aa_ready"))
                if not front:
                    own()
                    v.sem_inc(*E.done("ring_free"))
                idb = id32.unsqueeze(1).to_broadcast((P, 8, HB))
                for d in range(2):
                    s, w = E.full()
                    v.wait_ge(*w)
                    own()
                    tt(Xh[d], ps[:, 2 * s, 0:256].rearrange("p (e t) -> p e t", e=8), lvl[0][d].unsqueeze(1).to_broadcast((P, 8, HB)), ALU.mult)\
                        .then_inc(*E.freed(s))
                    tt(Nh[d], Dh[d], lvl[0][1 - d].unsqueeze(1).to_broadcast((P, 8, HB)), ALU.mult).then_inc(*E.done())
                    own()
                    tt(Xh[d], Xh[d], idb, ALU.add)
                    tt(Nh[d], Nh[d], idb, ALU.add).then_inc(*E.done("xn_ready"))
                for m in range(1, 6):
                    if m == 1 and front:
                        front_square(c + 1)
                    if m == 1 and tail:
                        tail_center(c - 1)
                    if m == 2 and front:
                        front_max()
                    if m == 2 and tail:
                        tail_norm(c - 1)
                    if m == 2 and front:
                        E.skip(1)
                        front_norm()
                    if m == 3 and front:
                        front_cumulate(0)
                    if m == 4 and front:
                        E.skip(1)
                        front_operands(c + 1, 0)
                    if m == 5 and front:
                        front_cumulate(1)
                    for d in range(2):
                        s, w = E.full()
                        v.wait_ge(*w)
                        product = ps[:, 2 * s, 0:256].rearrange("p (e t) -> p e t", e=8)
                        if m < 5:
                            tt(Qh[d], product, lvl[m][d].unsqueeze(1).to_broadcast((P, 8, HB)), ALU.mult).then_inc(*E.done("q_ready"))
                            own()
                            v.sem_inc(*E.freed(s))
                        else:
                            for a, b in across[1 - d]:
                                i_ = v.tensor_copy(Qh[d][a:b], product[a:b])
                            i_.then_inc(*E.done("q_ready"))
                            tt(Ni[d].rearrange("p e (b t) -> p e b t", b=2), Nh[d].unsqueeze(2).to_broadcast((P, 8, 2, HB)),
                               half.rearrange("p (b t) -> p b t", b=2).unsqueeze(1).to_broadcast((P, 8, 2, HB)), ALU.mult).then_inc(*E.freed(s))
                    for d in range(2):
                        s, w = E.full()
                        v.wait_ge(*w)
                        if m < 5:
                            nx = scr[:, RD * d:RD * d + 512]
                            i_ = tt(nx, nx, ps[:, 2 * s, :], ALU.add)
                        else:
                            own()
                            for a, b in across[d]:
                                i_ = v.tensor_copy(Ni[d][a:b, :, HB * (1 - d):HB * (2 - d)],
                                                   ps[a:b, 2 * s, 0:256].rearrange("p (e t) -> p e t", e=8))
                        i_.then_inc(*E.done("xn_ready"))
                        own()
                        v.sem_inc(*E.freed(s))
                if front:
                    front_operands(c + 1, 1)
                E.skip(4)
                idpq = id64.unsqueeze(1).unsqueeze(1).to_broadcast((P, 2, 4, RC))
                for d in range(2):
                    s, w = E.full()
                    v.wait_ge(*w)
                    for p in range(2):
                        i_ = tt(MT[d].rearrange("p (q two) t -> p two q t", two=2)[:, p], ps[:, 2 * s + p, 0:256].rearrange("p (q t) -> p q t", q=4),
                                idpq[:, 0], ALU.add)
                    i_.then_inc(*E.freed(s))
                for d in range(2):
                    s, w = E.full()
                    v.wait_ge(*w)
                    for p in range(2):
                        i_ = tt(Kv[d].rearrange("p (q two) t -> p two q t", two=2)[:, p], ps[:, 2 * s + p, 0:256].rearrange("p (q t) -> p q t", q=4),
                                wcu[d].rearrange("p (q two) -> p two q", two=2)[:, p].unsqueeze(2).to_broadcast((P, 4, RC)), ALU.mult)
                    i_.then_inc(*E.freed(s))
                own()
                for d in range(2):
                    v.memset(Ni[d][:, RW_ORDER[d][0], :], 0.0)
                    v.tensor_copy(Ni[d][:, RW_ORDER[d][1], :], Kv[d][:, RW_ORDER[d][0], :]).then_inc(*E.done("s_ready"))
                q0 = lo_ // P
                for k in range(2, NRC):
                    for d in range(2):
                        prev, here = RW_ORDER[d][k - 1], RW_ORDER[d][k]
                        s, w = E.full()
                        v.wait_ge(*w)
                        stt(out=Ni[d][:, here, :], in0=ps[:, 2 * s, 0:RC], scalar=wcu[d][:, prev:prev + 1], in1=Kv[d][:, prev, :],
                            op0=ALU.mult, op1=ALU.add).then_inc(*E.done("s_ready"))
                        own()
                        v.sem_inc(*E.freed(s))
                    if k < 6:
                        d = k % 2
                        s, w = E.full()
                        v.wait_ge(*w)
                        if k == 5:
                            own()
                        dst = rq[d] if k < 4 else yac
                        for p in range(2):
                            part, new = by_pq(dst)[:, p, q0:4], ps[:, 2 * s + p, RC * q0:256].rearrange("p (q t) -> p q t", t=RC)
                            if k == 4:
                                i_ = v.tensor_copy(part, new)
                            else:
                                i_ = tt(part, part, new, ALU.add)
                        i_.then_inc(*(E.done("rp_ready") if k < 4 else E.freed(s)))
                        if k < 4:
                            own()
                            v.sem_inc(*E.freed(s))
                s, w = E.full()
                v.wait_ge(*w)
                own()
                tt(yac[:, lo_:T], yac[:, lo_:T], ps[:, 2 * s, lo_:T], ALU.add).then_inc(*E.done())
                own()
                tt(yac[:, lo_:T], yac[:, lo_:T], ps[:, 2 * s + 1, lo_:T], ALU.add).then_inc(*E.freed(s))
                own()
                v.sem_inc(*E.done("yb_ready"))

            def rwkv():
                v.wait_ge(*E.count("lora_ready").next())
                front_square(0)
                front_max()
                front_norm()
                for d in range(2):
                    E.skip(1)
                    front_cumulate(d)
                    front_operands(0, d)
                rwkv_tile(0, True, False)
                with E.loop(KT - 2) as i:
                    rwkv_tile(i + 1, True, True)
                rwkv_tile(KT - 1, False, True)
                tail_center(KT - 1)
                tail_norm(KT - 1)

            for name in names:
                if name.startswith(PRIMED):
                    v.sem_inc(sems[name], 1)
            v.wait_ge(sems["dma_const"], 16 * 5)
            v.wait_ge(*E.count("dma_x").next())
            for L in range(DEPTH):
                lo_, hi = N_OUT[L]
                n = hi - lo_
                with E.loop(6) as i:
                    E.skip(2)
                    for r in range(2):
                        s, w = E.full()
                        v.wait_ge(*w)
                        first = (i * 2 + r) * 4
                        tt(mod[:, bass.ds(first, 4), :], ps[:, 2 * s, 0:8].rearrange("p (j c) -> p j c", j=4),
                           par[:, L, bass.ds(first + COLS["adab"], 4)].unsqueeze(2).to_broadcast((P, 4, 2)), ALU.add).then_inc(*E.freed(s))
                own()
                prenorm(L, "npre", 0, L == 1)
                conv_tiles("scw", 3)
                v.wait_ge(*E.count("h_ctx_ready").next())
                v.wait_ge(*E.mine())
                v.sem_inc(*E.done("scr_free"))
                ssd()
                with E.loop(2) as i:
                    for b in range(4):
                        E.skip(1)
                        v.wait_ge(*E.count("zs_ready").next())
                        for m in range(2):
                            t = i * 8 + (2 * b + m)
                            i_ = tt(A[:, t, lo_:hi], A[:, t, lo_:hi], ZS[:, b % 2, m, 0:n], ALU.mult)
                        i_.then_inc(*E.done("yz_ready"))
                for g in range(GROUPS):
                    s, w = E.full()
                    v.wait_ge(sems[f"slot_free{s}"], E.count(f"slot_free{s}").so_far()[1])
                    rg = GR[g][:, 0:n]
                    v.reciprocal(rg, rg).then_inc(*E.done())
                    own()
                    for j in range(4):
                        t = 4 * g + j
                        i_ = stt(out=A[:, t, lo_:hi], in0=A[:, t, lo_:hi], scalar=col(L, "snorm", t), in1=rg, op0=ALU.mult, op1=ALU.mult)
                i_.then_inc(*E.done("yn_ready"))
                E.skip(8 + 4)
                v.wait_ge(*E.count("gate_ready").next())
                tt(O[:, :, lo_:hi], O[:, :, lo_:hi], SG[:, :, lo_:hi], ALU.mult).then_inc(*E.done())
                conv_tiles("rcw", 3)
                E.skip(2)
                own()
                v.memset(reset, 1.0).then_inc(*E.done())
                own()
                v.memset(e8(reset)[:, :, 0:1], 0.0).then_inc(*E.done())
                rwkv()
                v.wait_ge(*E.mine())
                v.sem_inc(*E.done("yr_ready"))
                E.skip(4)
                for b in range(4):
                    E.skip(1)
                    v.wait_ge(*E.count("gate_ready").next())
                    gated = SG[:, 2 * b:2 * b + 2, lo_:hi]
                    tt(gated, gated, lo[:, 0:2, 0:n], ALU.mult).then_inc(*E.done("out_ready"))
                    own()
                    tt(O[:, 2 * b:2 * b + 2, lo_:hi], O[:, 2 * b:2 * b + 2, lo_:hi], gated, ALU.add).then_inc(*E.done())
                own()
                v.sem_inc(*E.done("o_ready"))
                E.skip(4)
                v.wait_ge(*E.count("dma_x").next())
                postnorm(L, hT, "npost", 2, L == 1, lo_)
                if L == 0:
                    prenorm(L, "fpre", 3, False)
                else:
                    prenorm(L, "fpre", 3, False, lo_)

                def ffn_tile(s, t):
                    v.wait_ge(*E.count("tap2_ready").next())
                    first = True
                    if lo_ == 0:
                        src, dst = ps[:, 2 * s, 0:CTX], A[:, t, 0:CTX]
                        for o_, a, b in ((3, 1, 0), (5, 0, 1)):
                            stt(out=dst[:, a:a + 255], in0=src[:, b:b + 255], scalar=colr(L, "fcw", t + FF_T * o_), in1=dst[:, a:a + 255],
                                op0=ALU.mult, op1=ALU.add).then_inc(*E.done())
                            own()
                    src, dst = grid(ps[:, 2 * s, CTX - lo_:T - lo_]), grid(A[:, t, CTX:T])
                    for dr in (-1, 0, 1):
                        for dc in (-1, 0, 1):
                            if dr == dc == 0:
                                continue
                            r0, r1 = max(0, -dr), ROWS - max(0, dr)
                            c0, c1 = max(0, -dc), GRID_W - max(0, dc)
                            i_ = stt(out=dst[:, r0:r1, c0:c1], in0=src[:, r0 + dr:r1 + dr, c0 + dc:c1 + dc],
                                     scalar=colr(L, "fcw", t + FF_T * (3 * (dr + 1) + dc + 1)), in1=dst[:, r0:r1, c0:c1],
                                     op0=ALU.mult, op1=ALU.add)
                            if (dr, dc) != (1, 1):
                                i_.then_inc(*E.done())
                                own()
                    i_.then_inc(*E.done("conv_ready"))
                    v.wait_ge(*E.count("gelu_ready").next())
                    tt(A[:, t, lo_:hi], A[:, t, lo_:hi], ps[:, 2 * s + 1, 0:n], ALU.mult).then_inc(*E.freed(s))
                with E.loop(5) as i:
                    for b in range(4):
                        ffn_tile(E.full()[0], i * 4 + b)
                for t in range(20, 22):
                    ffn_tile(E.full()[0], t)
                own()
                v.sem_inc(*E.done("ffn_ready"))
                E.skip(4)
                postnorm(L, O, "fpost", 5, False, lo_)

        @block.gpsimd
        def _(g_):
            E = Engine(g_, "pool", sems, table)
            for dst, src in ((cond[:, :, :].rearrange("p k c -> p (k c)"), cond_in), (par[:, :, :].rearrange("p l n -> p (l n)"), par_in),
                             (cst[:, :], const_in), (headp[:, :, :, :, :].rearrange("p a b c d -> p (a b c d)"), headp_in),
                             (wdt[:, :, :, :].rearrange("p a b c -> p (a b c)"), wdt_in)):
                g_.dma_start(dst, src).then_inc(sems["dma_const"], 16)
            xv = X.rearrange("p k t -> p (k t)")
            g_.dma_start(xv, x_in).then_inc(*E.count("dma_x").sent())
            for L in range(DEPTH):
                lo_, hi = N_OUT[L]
                if L == 0:
                    g_.dma_start(lst[:, 0:2, :].rearrange("p a n -> p (a n)"), lora_in[0, :, 0:2 * P]).then_inc(*E.count("dma_wa").sent())
                g_.wait_ge(*E.count("conv_silu").next())
                E.count("conv_silu").n += 23
                g_.wait_ge(*E.count("conv_silu").so_far())
                g_.wait_ge(*E.count("scr_free").next())
                g_.wait_ge(*E.count("wdec_ready").next())
                with E.loop(GROUPS) as g:
                    g_.wait_ge(*E.count("y_ready").so_far())
                    E.count("y_ready").n += NCH
                    g_.tensor_copy(xg, A[:, bass.ds(g * 4, 4), :])
                    g_.tensor_copy(Bg, A[:, XS_T + g, :])
                    g_.tensor_copy(Cg, A[:, XS_T + 4 + g, :])
                    for d in range(2):
                        i_ = g_.tensor_copy(dtag[:, d], heads4(dta)[:, d, :, bass.ds(g * HPG, HPG)])
                    i_.then_inc(*E.done("staged"))
                    g_.wait_ge(*E.mine())
                    g_.wait_ge(*E.count("xw_ready").next())
                    E.count("xw_ready").n += 5
                    for c in range(NCH):
                        if c > 1:
                            g_.wait_ge(sems["y_ready"], E.count("y_ready").so_far()[1] - NCH + c - 1)
                        for d in range(2):
                            i_ = g_.tensor_tensor(xdt[c % 2][d], xtok[:, c], heads4(dtv)[:, d, c, bass.ds(g * HPG, HPG)].unsqueeze(2)
                                                  .to_broadcast((P, HPG, 64)), ALU.mult)
                        for d in range(2):
                            if SSD_ORDER[d].index(c):
                                g_.wait_ge(*E.count("ec_ready").next())
                                i_ = g_.tensor_tensor(Cb[c % 2][d], Cb[c % 2][d], Cg[:, Q * c:Q * (c + 1)].unsqueeze(1).to_broadcast((P, HPG, P)), ALU.mult)
                        i_.then_inc(*E.done("ct_ready"))
                def hold_v(c):
                    for p in range(2):
                        i_ = g_.tensor_copy(by_pq(vS)[:, 1 - p], by_pq(A[:, 16 + c, :])[:, p])
                    i_.then_inc(*E.done("vs_ready"))

                def load_g2(c):
                    g_.dma_start(lst[:, 2, :], lora_in[c + KT * L, :, 2 * P:3 * P]).then_inc(*E.count("dma_g2").sent())

                def load_wa(c):
                    for _ in range(2):
                        g_.wait_ge(*E.count("sa_ready").next())
                    g_.dma_start(lst[:, 0:2, :].rearrange("p a n -> p (a n)"), lora_in[c + KT * L, :, 0:2 * P]).then_inc(*E.count("dma_wa").sent())

                def rwkv_tile(c, front, tail):
                    if front:
                        for _ in range(2):
                            g_.wait_ge(*E.count("aa_ready").next())
                        hold_v(c + 1)
                    if tail:
                        g_.wait_ge(*E.count("ystd_ready").next())
                        load_g2(c)
                    if front:
                        load_wa(c + 2)

                g_.wait_ge(*E.count("lora_ready").next())
                hold_v(0)
                load_g2(0)
                load_wa(1)
                rwkv_tile(0, True, False)
                with E.loop(KT - 2) as i:
                    rwkv_tile(i + 1, True, True)
                rwkv_tile(KT - 1, False, True)
                E.count("aa_ready").n += 2
                E.count("ystd_ready").n += 1
                g_.wait_ge(*E.count("o_ready").next())
                g_.dma_start(xv, x_in if L == 0 else x_mid).then_inc(*E.count("dma_x").sent())
                g_.wait_ge(*E.count("x_ready").next())
                g_.wait_ge(*E.count("x_ready").next())
                if L == 0:
                    g_.dma_start(x_mid, xv).then_inc(*E.count("dma_out").sent())
                    g_.wait_ge(*E.count("dma_out").so_far())
            g_.dma_start(out.rearrange("p (k t) -> p k t", k=KT), X[:, :, CTX:T]).then_inc(*E.count("dma_out").sent())
            g_.wait_ge(*E.count("dma_out").so_far())


INS = ("stream", "x_in", "cond", "par", "consts", "headp", "wdt", "lora")


def constants():
    c = np.zeros((P, CONSTS), np.float32)

    def put(name, a, off=0):
        c[:, CCOL[name] + off:CCOL[name] + off + a.shape[1]] = a

    i = np.arange(P)
    put("ident", np.eye(P))
    put("ones", np.ones((P, P)))
    put("headones", (i[:, None] // 64 == i[None] // 64) * 1.0)
    r, t = i[:, None] % RC, np.arange(RC)[None]
    for d in range(2):
        put("tri", (i[:, None] <= i[None]) * 1.0 if d == 0 else (i[:, None] >= i[None]) * 1.0, P * d)
        put("mask2", np.concatenate([(r < t), (r <= t)] if d == 0 else [(r > t), (r >= t)], 1) * 1.0, P * d)
        r2, t2 = i[:, None] % HB, np.arange(HB)[None]
        for m in range(5):
            b = 1 << m
            same = r2 // (2 * b) == t2 // (2 * b)
            low = (r2 // b % 2 == 1) & (t2 // b % 2 == 0)
            high = (r2 // b % 2 == 0) & (t2 // b % 2 == 1)
            put("lvl", (same & (low if d == 0 else high)) * 1.0, HB * (2 * m + d))
    put("id32", (r2 == t2) * 1.0)
    put("half", (r // HB == t // HB) * 1.0)
    put("id64", (r == t) * 1.0)
    return c


def lay_out(inp):
    g = {k: np.asarray(v) for k, v in inp.items()}

    def cols256(w):
        n = w.shape[1]
        return w.reshape(KT, P, n // 256, 256).transpose(2, 1, 0, 3).reshape(n // 256, P, WBLK)

    def tab(a):
        return a.reshape(-1, P).T

    blocks = []
    pars, headp, wdt, lora = [], [], [], []
    for L in range(DEPTH):
        wi = g["w_in"][L]
        o = np.cumsum([0, 2048, 3072, 32, 3072, 128, 128, 128, 2048])
        z, xbc, dt, rkv, wd, ad, gd, gate = [wi[:, o[j]:o[j + 1]] for j in range(8)]
        blocks.append(g["ada_w"][L].reshape(2, 4, P, 12, 512).transpose(3, 0, 2, 1, 4).reshape(24, P, WBLK))
        blocks += [cols256(xbc), cols256(z)]
        blocks.append(g["ssm_out"][L].reshape(16, P, 8, P).transpose(2, 1, 0, 3).reshape(8, P, WBLK))
        blocks += [cols256(gate[:, :D]), cols256(rkv), cols256(np.concatenate([wd, ad], 1)),
                   cols256(np.concatenate([gd, np.zeros_like(gd)], 1)), cols256(g["rwkv_out"][L]), cols256(gate[:, D:]),
                   cols256(g["w_o"][L])]
        fi = g["ffn_w_in"][L]
        pair = np.concatenate([fi[:, :2816].reshape(D, FF_T, 1, P), fi[:, 2816:].reshape(D, FF_T, 1, P)], 2)
        blocks.append(cols256(pair.reshape(D, 2 * 2816)))
        blocks.append(g["ffn_w_out"][L].reshape(11, 2, P, D).transpose(0, 2, 1, 3).reshape(11, P, WBLK))
        wdt.append(dt.reshape(KT, P, HEADS).transpose(1, 0, 2).reshape(P, -1))
        p = np.zeros((P, PARAMS), np.float32)

        def put(name, a):
            p[:, COLS[name]:COLS[name] + a.shape[1]] = a

        for name, key in (("npre", "norm_mix_pre"), ("npost", "norm_mix_post"), ("fpre", "norm_ffn_pre"), ("fpost", "norm_ffn_post"),
                          ("scw", "ssm_conv_w"), ("scb", "ssm_conv_b"), ("snorm", "ssm_norm"), ("rcw", "rwkv_conv_w"),
                          ("w0", "rwkv_w0"), ("a0", "rwkv_a0"), ("kk", "rwkv_k_k"), ("ka", "rwkv_k_a"), ("rk", "rwkv_r_k"),
                          ("lnw", "rwkv_ln_w"), ("lnb", "rwkv_ln_b"), ("fcw", "ffn_conv_w"), ("fcb", "ffn_conv_b"), ("adab", "ada_b")):
            put(name, tab(g[key][L]))
        put("dskip", tab(np.repeat(g["ssm_d"][L], 64)))
        pars.append(p)
        headp.append(np.stack([g["ssm_dt_bias"][L], g["ssm_a_log"][L]]).reshape(-1))
        lora.append(np.stack([g["rwkv_w2"][L].reshape(P, KT, P), g["rwkv_a2"][L].reshape(P, KT, P), g["rwkv_g2"][L].reshape(P, KT, P)], 2)
                    .transpose(1, 0, 2, 3).reshape(KT, P, 3 * P))
    tokens = np.concatenate([g["ctx"][0], g["x"][0]], 0)
    return {
        "stream": np.concatenate(blocks, 0),
        "x_in": tokens.reshape(T, KT, P).transpose(2, 1, 0).reshape(P, -1),
        "cond": np.stack([g["c"][0], g["c_ctx"]], 0).reshape(2, KT, P).transpose(2, 1, 0).reshape(P, -1),
        "par": np.concatenate(pars, 1),
        "consts": constants(),
        "headp": np.repeat(np.concatenate(headp)[None], P, 0),
        "wdt": np.concatenate(wdt, 1),
        "lora": np.concatenate(lora + [np.zeros((1, P, 3 * P), np.float32)], 0),
    }


def program(nc, arrays, table):
    ins = [nc.dram_tensor("in_" + n, arrays[n].shape, F32, kind="ExternalInput").ap() for n in INS]
    out = nc.dram_tensor("out", (P, KT * LAT), F32, kind="ExternalOutput").ap()
    build(nc, ins, out, table)


def kernel(**inputs):
    import concourse.bacc as _bacc
    from concourse.bass_utils import run_bass_kernel_spmd as _run

    arrays = {k: np.ascontiguousarray(v) for k, v in lay_out(inputs).items()}
    table = {}
    for _ in range(2):
        nc = _bacc.Bacc("TRN2", target_bir_lowering=False, num_devices=1)
        program(nc, arrays, table)
    r = _run(nc, [{"in_" + k: v for k, v in arrays.items()}], core_ids=[0])
    got = r.results[0]["out"]
    return np.ascontiguousarray(got.reshape(P, KT, LAT).transpose(2, 1, 0).reshape(1, LAT, D))
```

```python
from contextlib import ExitStack, contextmanager

import numpy as np
import concourse.bass as bass
from concourse import mybir

F32 = mybir.dt.float32
ACT = mybir.ActivationFunctionType
ALU = mybir.AluOpType

P = 128
DEPTH = 2
D = 1024
KT = D // P
CTX, LAT = 256, 256
T = CTX + LAT
GRID_W = 64
ROWS = LAT // GRID_W
EPS = 1e-6
D_SSM, HEADS, GROUPS, HPG = 2048, 32, 4, 8
XS_T = D_SSM // P
XBC_T = XS_T + 8
Q = 128
NCH = T // Q
RC = 64
HB = 32
NRC = T // RC
RK_T = 24
LN_EPS = 64e-5
WSCALE = float(np.exp(-0.5))
FF_T = 2816 // P
SLOTS = 4
WSLOTS = 4
WBLK = 2048

B_ADA, B_XBC, B_Z, B_SO, B_GS, B_RKV, B_LORA, B_RO, B_GR, B_WO, B_FI, B_FO = 24, 12, 8, 8, 4, 12, 2, 4, 4, 4, 22, 11
TO_RWKV = B_ADA + B_XBC + B_Z + B_SO + B_GS + B_RKV + B_LORA
PER_LAYER = TO_RWKV + B_RO + B_GR + B_WO + B_FI + B_FO
NBLK = DEPTH * PER_LAYER
RING_STOPS = tuple(TO_RWKV + PER_LAYER * L for L in range(DEPTH))

COLS, _n = {}, 0
for _name, _w in (("npre", 8), ("npost", 8), ("fpre", 8), ("fpost", 8), ("scw", 72), ("scb", 24), ("snorm", 16),
                  ("rcw", 72), ("w0", 16), ("a0", 16), ("kk", 8), ("ka", 8), ("rk", 8), ("lnw", 8), ("lnb", 8),
                  ("fcw", 9 * FF_T), ("fcb", FF_T), ("adab", 48), ("dskip", 16)):
    COLS[_name] = _n
    _n += _w
PARAMS = _n

CCOL, _n = {}, 0
for _name, _w in (("ident", 128), ("ones", 128), ("headones", 128), ("tri", 256), ("mask2", 256),
                  ("lvl", 10 * 32), ("id32", 32), ("half", 64), ("id64", 64)):
    CCOL[_name] = _n
    _n += _w
CONSTS = _n

SSD_ORDER = ((0, 1, 2, 3), (1, 0, 3, 2))
RW_ORDER = ((0, 1, 2, 3, 4, 5, 6, 7), (3, 2, 1, 0, 7, 6, 5, 4))


PRIMED = ("slot_free", "y_ready", "yz_ready", "dve_done")


class Count:

    def __init__(self, sem, unit, primed):
        self.sem, self.unit, self.n, self.primed, self.i, self.per = sem, unit, primed, primed, None, 0

    def _value(self):
        if self.i is None or not self.per:
            return self.n
        assert self.n > 0, "a wait on a register's value stays above zero: prime the semaphore"
        return self.n + self.i * self.per

    def sent(self):
        self.n += self.unit
        return self.sem, self.unit

    def next(self):
        self.n += self.unit
        return self.sem, self._value()

    def so_far(self):
        return self.sem, self._value()


class Engine:

    def __init__(self, e, name, sems, table):
        self.e, self.name, self.sems, self.table = e, name, sems, table
        self.counts, self.loops, self.step_no, self.wblk, self.own = {}, 0, 0, 0, f"{name}_done"
        self.last = None

    def count(self, name):
        if name not in self.counts:
            c = Count(self.sems[name], 16 if name.startswith(("w_loaded", "dma")) else 1, int(name.startswith(PRIMED)))
            if self.loop_now:
                c.i, c.per = self.loop_now[0], self.loop_now[1].get(name, 0)
            self.counts[name] = c
        return self.counts[name]

    loop_now = None

    def done(self, name=None):
        c = self.count(name or self.own)
        out = c.sent()
        self.last = (c.sem, c._value())
        return out

    def mine(self):
        return self.last or self.count(self.own).so_far()

    def slot(self):
        s = self.step_no % SLOTS
        self.step_no += 1
        return s

    def skip(self, n=1):
        for _ in range(n):
            s = self.slot()
            self.count(f"slot_full{s}").n += 1
            self.count(f"slot_free{s}").n += 1

    def sit_out(self, n):
        self.step_no += n

    def full(self):
        s = self.slot()
        self.count(f"slot_free{s}").n += 1
        return s, self.count(f"slot_full{s}").next()

    def freed(self, s):
        c = self.count(f"slot_free{s}")
        self.last = (c.sem, c._value())
        return c.sem, 1

    @contextmanager
    def loop(self, trips):
        key = (self.name, self.loops)
        self.loops += 1
        per = self.table.get(key, {})
        start = {k: c.n for k, c in self.counts.items()}
        at, wat = self.step_no, self.wblk
        with self.e.Fori(0, trips) as i:
            self.loop_now = (i, per)
            for k, c in self.counts.items():
                c.i, c.per = i, per.get(k, 0)
            self.last = None
            yield i
        self.loop_now, self.last = None, None
        start = {k: start.get(k, c.primed) for k, c in self.counts.items()}
        found = {k: c.n - start[k] for k, c in self.counts.items() if c.n != start[k]}
        assert not per or per == found, (key, per, found)
        self.table[key] = found
        for k, c in self.counts.items():
            c.i, c.per = None, 0
            c.n = start[k] + trips * found.get(k, 0)
        assert (self.step_no - at) % SLOTS == 0 and (self.wblk - wat) % WSLOTS == 0, (key, self.step_no - at)
        self.step_no, self.wblk = at, wat


def build(nc, ins, out, table):
    stream, x_in, cond_in, par_in, const_in, headp_in, wdt_in, lora_in = ins
    x_mid = nc.dram_tensor("x_mid", (P, KT * T), F32, kind="Internal").ap()

    with ExitStack() as ctx:
        def sb(name, *shape):
            return ctx.enter_context(nc.sbuf_tensor(name, [P, *shape], F32))

        W = sb("W", WSLOTS, WBLK)
        A = sb("A", RK_T, T)
        hT = sb("hT", KT, T)
        O = sb("O", KT, T)
        lo = sb("lo", 3, T)
        scr = sb("scr", 16384)
        mod = sb("mod", 48, 2)
        par = sb("par", DEPTH, PARAMS)
        cst = sb("cst", CONSTS)
        headp = sb("headp", DEPTH, 2, 2, HEADS)
        wdt = sb("wdt", DEPTH, KT, HEADS)
        cond = sb("cond", KT, 2)
        uv_more = sb("uv_more", 512)
        gsc = sb("gsc", KT, 2)
        rst = sb("rst", T)
        lst = sb("lst", 3, P)
        rows = lo
        ps = ctx.enter_context(nc.psum_tensor("ps", [P, 2 * SLOTS, 512], F32))

        names = ([f"slot_full{s}" for s in range(SLOTS)] + [f"slot_free{s}" for s in range(SLOTS)]
                 + [f"w_loaded{s}" for s in range(WSLOTS)]
                 + ["w_used", "pe_passed", "act_passed", "pool_passed", "pe_done", "act_done", "dve_done", "pool_done",
                    "dma_cond", "dma_const", "dma_x", "dma_wa", "dma_g2", "dma_out",
                    "cond_ready", "row_ready", "sq_ready", "norm_ready", "h_ready",
                    "tap_ready", "conv_ready", "conv_silu", "abs_ready", "log_ready", 
                    "dta_ready", "dec_in_ready", "dec_ready", "wdec_ready", "staged", "xw_ready", "btok_ready",
                    "diff_ready", "e_ready", "ec_ready", "ct_ready", "w_ready",
                    "y_ready", "zs_ready", "yz_ready", "ysq_ready", "yn_ready", "out_ready", "gate_ready", "o_ready",
                    "lora_ready", "kksq_ready", "kkmax_ready", "kkstd_ready", "vs_ready", "vtok_ready", "sa_ready",
                    "cum_ready", "exps_ready", "ops_ready", "tok_ready", "aa_ready", "xn_ready", "q_ready", "r_ready",
                    "ug_ready", "s_ready", "rp_ready", "yb_ready", "yc_ready", "ycsq_ready",
                    "ystd_ready", "yr_ready", "ring_free", "gelu_ready", "tap2_ready", "ffn_ready",
                    "x_ready", "scr_free"])
        sems = {n: ctx.enter_context(nc.semaphore(n)) for n in names}

        def cc(name, w=None, off=0):
            return cst[:, CCOL[name] + off:CCOL[name] + off + w]

        ident, ones, headones = cc("ident", P), cc("ones", P), cc("headones", P)
        tri = [cc("tri", P, P * d) for d in range(2)]
        mask2 = [cc("mask2", P, P * d) for d in range(2)]
        lvl = [[cc("lvl", HB, HB * (2 * m + d)) for d in range(2)] for m in range(5)]
        id32, half = cc("id32", HB), cc("half", RC)
        id64 = cc("id64", RC)
        reset = rst[:, :]

        def col(L, name, k=0, w=1):
            return par[:, L, COLS[name] + k:COLS[name] + k + w]

        def colr(L, name, k):
            return par[:, L, bass.ds(COLS[name] + k, 1)]

        def span(a, w):
            return scr[:, a:a + w]

        X = span(0, KT * T).rearrange("p (k t) -> p k t", k=KT)
        SQ = span(KT * T, KT * T).rearrange("p (k t) -> p k t", k=KT)

        YQ = span(0, XS_T * T).rearrange("p (k t) -> p k t", k=XS_T)
        GR = [span(8192 + 512 * g, 512) for g in range(GROUPS)]
        ZS = span(12288, 2048).rearrange("p (r m t) -> p r m t", r=2, m=2)
        SG = span(0, KT * T).rearrange("p (k t) -> p k t", k=KT)

        Of = O[:, :, :].rearrange("p k t -> p (k t)")
        lof = lo[:, :, :].rearrange("p k t -> p (k t)")
        Wb = [[a[:, 1024 * d:1024 * (d + 1)].rearrange("p (h l) -> p h l", h=HPG) for d in range(2)] for a in (span(0, 2048), Of)]
        xg = span(0, 2048).rearrange("p (j t) -> p j t", j=4)
        Cb = [[a[:, 1024 * d:1024 * (d + 1)].rearrange("p (h l) -> p h l", h=HPG) for d in range(2)]
              for a in (span(2048, 2048), Of[:, 2048:4096])]
        Bg = span(4096, T)
        btok = span(5120, T).rearrange("p (c n) -> p c n", c=NCH)
        xtok = span(5632, 2048).rearrange("p (c h x) -> p c h x", c=NCH, h=HPG)
        Hs = [[span(7680 + 1536 * d + 512 * o, 512).rearrange("p (h x) -> p h x", h=HPG) for o in range(3)] for d in range(2)]
        xdt = [[a[:, 512 * d:512 * (d + 1)].rearrange("p (h x) -> p h x", h=HPG) for d in range(2)] for a in (span(10752, 1024), lof)]
        xw = [[a.rearrange("p (h x) -> p h x", h=HPG) for a in pair]
              for pair in ((span(11776, 512), span(12288, 512)), (lof[:, 1024:1536], uv_more[:, :]))]
        cbm = [span(12800 + 512 * d, 512).rearrange("p (c l) -> p c l", c=NCH) for d in range(2)]
        small = [span(13824 + 256 * j, 256) for j in range(8)]
        dtv, dta, ncs, wde, dec, sm_a, sm_b, sm_c = small
        dtag = span(13824 + 2048, 64).rearrange("p (d c h) -> p d c h", d=2, c=NCH)
        expA = span(13824 + 2048 + 64, 64)

        def heads4(ap):
            return ap.rearrange("p (d c h) -> p d c h", d=2, c=NCH)

        RD = 6144
        Wf = W[:, :, :].rearrange("p s n -> p (s n)")

        def ring(k, w=512):
            return Wf[:, k:k + w]

        at = [ring(2048 * d) for d in range(2)]
        rt = [ring(2048 * d + 512) for d in range(2)]
        bk = [ring(2048 * d + 1024, 1024) for d in range(2)]
        bt = [bk[d].rearrange("p (q f t) -> p q f t", q=4, f=4)[:, :, 0:4:3, :] for d in range(2)]
        kt = [bk[d].rearrange("p (q f t) -> p q f t", q=4, f=4)[:, :, 1:3, :] for d in range(2)]
        art = [ring(2048 * d, 1024).rearrange("p (two c t) -> p c two t", two=2, c=NRC) for d in range(2)]
        sg, asg, pre, exc, inc, kkn, kds, vS = [ring(4096 + 512 * j) for j in range(8)]
        rq = [span(RD * d + 512, 512) for d in range(2)]

        def e8(ap):
            return ap.rearrange("p (e t) -> p e t", e=8)

        Dh = [span(RD * d + 1792, 256).rearrange("p (e t) -> p e t", e=8) for d in range(2)]
        Qh = [span(RD * d + 1536, 256).rearrange("p (e t) -> p e t", e=8) for d in range(2)]
        Nh = [span(RD * d, 256).rearrange("p (e t) -> p e t", e=8) for d in range(2)]
        Xh = [span(RD * d + 256, 256).rearrange("p (e t) -> p e t", e=8) for d in range(2)]
        Ni = [e8(span(RD * d + 1024, 512)) for d in range(2)]
        Qi = [e8(span(RD * d + 1536, 512)) for d in range(2)]
        AA = [[span(RD * d + 2048 + 1024 * p, 1024).rearrange("p (e a t) -> p e a t", e=8, a=2) for p in range(2)] for d in range(2)]
        RA = [span(RD * d + 4096, 1024).rearrange("p (e a t) -> p e a t", e=8, a=2) for d in range(2)]
        RAq = [span(RD * d + 4096, 1024).rearrange("p (h q a t) -> p q h a t", h=2, q=4, a=2) for d in range(2)]
        MT = [e8(span(RD * d + 4096, 512)) for d in range(2)]
        Kv = [e8(span(RD * d + 4608, 512)) for d in range(2)]
        BK = [span(RD * d + 5120, 1024).rearrange("p (c h k) -> p c h k", c=NRC, h=2) for d in range(2)]
        UV = [[e8(span(12288 + 512 * p, 512) if d == 0 else (span(13312, 512), uv_more[:, :])[p]) for p in range(2)] for d in range(2)]
        yac, yc, ycsq, bonus = [span(13824 + 512 * j, 512) for j in range(4)]
        ystd = ycsq
        wc = [span(15872 + 8 * d, 8) for d in range(2)]
        wcu = [span(15888 + 8 * d, 8) for d in range(2)]

        def by_pq(ap):
            return ap.rearrange("p (q two t) -> p two q t", two=2, t=RC)

        def quads(ap):
            return ap.rearrange("p (q two t) -> p q two t", two=2, t=RC)

        def seg2(ap):
            return ap.rearrange("p (s t) -> p s t", s=2)

        def permuted(ap, perm):
            return ap.rearrange("p (w r) -> p r w", r=ROWS) if perm else ap.rearrange("p (r w) -> p r w", r=ROWS)

        def grid(ap):
            return ap.rearrange("p (r w) -> p r w", r=ROWS)

        N_OUT = {0: (0, T), 1: (CTX, T)}
        Y_CHUNKS = {L: range(N_OUT[L][0] // Q, NCH) for L in range(DEPTH)}
        across = [[(2 * HB * p + HB * d, 2 * HB * p + HB * d + HB) for p in range(2)] for d in range(2)]


        block = ctx.enter_context(nc.Block())

        @block.sync
        def _(sp):
            E = Engine(sp, "sp", sems, table)
            wv = stream
            first = 0
            for last in RING_STOPS + (NBLK,):
                if first:
                    sp.wait_ge(*E.count("ring_free").next())
                for b in range(first, first + WSLOTS):
                    sp.dma_start(W[:, b % WSLOTS, :], wv[b]).then_inc(sems[f"w_loaded{b % WSLOTS}"], 16)
                rounds = (last - first) // WSLOTS
                with sp.Fori(1, rounds) as i:
                    for j in range(WSLOTS):
                        sp.wait_ge(sems["w_used"], i * WSLOTS + (first + j - WSLOTS + 2))
                        s = (first + j) % WSLOTS
                        sp.dma_start(W[:, s, :], wv[i * WSLOTS + (first + j)]).then_inc(sems[f"w_loaded{s}"], 16)
                for b in range(first + rounds * WSLOTS, last):
                    sp.wait_ge(sems["w_used"], b - WSLOTS + 2)
                    sp.dma_start(W[:, b % WSLOTS, :], wv[b]).then_inc(sems[f"w_loaded{b % WSLOTS}"], 16)
                first = last

        @block.tensor
        def _(pe):
            E = Engine(pe, "pe", sems, table)

            def mm(o, l, r, start=True, stop=True):
                return pe.matmul(o, l, r, start=start, stop=stop)

            def passed():
                if E.loop_now:
                    pe.sem_inc(sems["pe_passed"], 1)

            def take():
                s = E.slot()
                pe.wait_ge(*E.count(f"slot_free{s}").so_far())
                passed()
                E.count(f"slot_free{s}").n += 1
                return s, ps[:, 2 * s:2 * s + 2, :]

            def full(s):
                return E.count(f"slot_full{s}").sent()

            def weights():
                s = E.wblk % WSLOTS
                E.wblk += 1
                pe.wait_ge(*E.count(f"w_loaded{s}").next())
                return W[:, s, :]

            def dense_block(src, lo_, hi, tiles=2, ready=None):
                w = weights().rearrange("p (k m) -> p k m", k=KT)
                s, o = take()
                for m in range(tiles):
                    for k in range(KT):
                        if ready and m == 0:
                            pe.wait_ge(*E.count(ready).next())
                        ins_ = mm(o[:, m, 0:hi - lo_], w[:, k, P * m:P * (m + 1)], src[:, k, lo_:hi], k == 0, k == KT - 1)
                        if m == 0 and k == 0:
                            ins_.then_inc(*E.count("w_used").sent())
                ins_.then_inc(*full(s))

            def dense(src, blocks, lo_=0, hi=T, ready=None):
                if ready:
                    for b in range(WSLOTS):
                        dense_block(src, lo_, hi, ready=None if b else ready)
                    blocks -= WSLOTS
                trips, rest = divmod(blocks, WSLOTS)
                if trips > 1:
                    with E.loop(trips):
                        for _ in range(WSLOTS):
                            dense_block(src, lo_, hi)
                else:
                    rest = blocks
                for _ in range(rest):
                    dense_block(src, lo_, hi)

            def channel_sum(src, n, lo_=0, hi=T, ready=None):
                s, o = take()
                for k in range(n):
                    if ready:
                        pe.wait_ge(*E.count(ready).next())
                    i_ = mm(o[:, 0, 0:hi - lo_], ones, src[:, k, lo_:hi], k == 0, k == n - 1)
                i_.then_inc(*full(s))

            def adaln():
                def row():
                    s, o = take()
                    for half in range(2):
                        w = weights().rearrange("p (k n) -> p k n", k=4)
                        for k in range(4):
                            i_ = mm(o[0:2, 0, :], cond[:, 4 * half + k, :], w[:, k, :], half + k == 0, half == 1 and k == 3)
                            if k == 0:
                                i_.then_inc(*E.count("w_used").sent())
                    i_.then_inc(*full(s))

                def transposed(n):
                    s, o = take()
                    pe.wait_ge(*E.count("row_ready").next())
                    passed()
                    for j in range(4):
                        i_ = pe.transpose(o[:, 0, 2 * j:2 * j + 2], rows[0:2, n, P * j:P * (j + 1)], ident[0:2, 0:2])
                    i_.then_inc(*full(s))

                row()
                row()
                pe.wait_ge(sems["dma_const"], 16 * 4)
                transposed(0)
                with E.loop(5):
                    for n in range(2):
                        row()
                        transposed(1 - n)
                transposed(1)

            def ssd():
                s, o = take()
                for c in range(NCH):
                    for k in range(KT):
                        i_ = mm(o[:, 0, HEADS * c:HEADS * (c + 1)], hT[:, k, Q * c:Q * (c + 1)], wdt[:, L, k, :], k == 0, k == KT - 1)
                i_.then_inc(*full(s))
                pe.wait_ge(*E.count("dta_ready").next())
                s, o = take()
                for d in range(2):
                    mm(o[:, 0, P * d:P * (d + 1)], tri[d], dta[:, P * d:P * (d + 1)])
                mm(o[:, 1, 0:256], ones, dta).then_inc(*full(s))
                chunks = Y_CHUNKS[L]
                with E.loop(GROUPS) as g:
                    pe.wait_ge(*E.count("staged").next())
                    for part in ((("B", 0),), (("x", 0), ("x", 1)), (("x", 2),), (("x", 3),)):
                        s, o = take()
                        for bank, (what, c) in enumerate(part):
                            for j in range(4):
                                src = Bg[:, Q * j:Q * (j + 1)] if what == "B" else xg[:, j, Q * c:Q * (c + 1)]
                                i_ = pe.transpose(o[:, bank, P * j:P * (j + 1)], src, ident)
                        i_.then_inc(*full(s))
                    def cumulated(c):
                        for d in range(2):
                            s, o = take()
                            for h in range(HPG):
                                i_ = mm(o[:, h // 4, P * (h % 4):P * (h % 4 + 1)],
                                        dtag[:, d, c, h:h + 1].to_broadcast((P, P)), tri[d])
                            i_.then_inc(*full(s))

                    def output(c):
                        s, o = take()
                        pe.wait_ge(*E.count("w_ready").next())
                        pe.wait_ge(*E.count("ct_ready").next())
                        for j in range(HPG // 2):
                            terms = []
                            for d in range(2):
                                terms.append((xdt[c % 2][d], Wb[c % 2][d]))
                                k = SSD_ORDER[d].index(c)
                                if k:
                                    terms.append((Hs[d][k - 1], Cb[c % 2][d]))
                            for n, (l, r) in enumerate(terms):
                                for e in range(2):
                                    i_ = mm(o[64 * e:64 * e + 64, 0, P * j:P * (j + 1)], l[:, 2 * j + e, :], r[:, 2 * j + e, :],
                                            n == 0, n == len(terms) - 1)
                        i_.then_inc(*full(s))

                    s, o = take()
                    for c in range(NCH):
                        i_ = mm(o[:, 0, Q * c:Q * (c + 1)], Bg[:, Q * c:Q * (c + 1)], A[:, XS_T + 4 + g, Q * c:Q * (c + 1)])
                    i_.then_inc(*full(s))
                    cumulated(chunks[0])
                    for o_ in range(3):
                        s, o = take()
                        for d in range(2):
                            pe.wait_ge(*E.count("xw_ready").next())
                            if o_ == 0 and d == 0:
                                pe.wait_ge(*E.count("btok_ready").next())
                            i_ = mm(o[:, d, :], btok[:, SSD_ORDER[d][o_], :], xw[o_ % 2][d])
                        i_.then_inc(*full(s))
                    for c in chunks:
                        if c + 1 < NCH:
                            cumulated(c + 1)
                        output(c)
                    E.sit_out(-(8 + 3 * len(chunks)) % SLOTS)

            def front_sum():
                s, o = take()
                pe.wait_ge(*E.count("kksq_ready").next())
                mm(o[:, 0, :], headones, exc).then_inc(*full(s))

            def front_lora(d):
                s, o = take()
                half = slice(64 * d, 64 * d + 64)
                if d == 0:
                    pe.wait_ge(*E.count("dma_wa").next())
                mm(o[:, 0, :], lst[half, 0, :], lo[half, 0, :])
                mm(o[:, 1, :], lst[half, 1, :], lo[half, 1, :]).then_inc(*full(s))

            def tail_mean(c):
                s, o = take()
                pe.wait_ge(*E.count("yb_ready").next())
                mm(o[:, 0, o_lo:T], headones, yac[:, o_lo:T])
                mm(o[:, 1, o_lo:T], headones, A[:, 8 + c, o_lo:T]).then_inc(*full(s))

            def tail_var():
                s, o = take()
                pe.wait_ge(*E.count("ycsq_ready").next())
                pe.wait_ge(*E.count("dma_g2").next())
                mm(o[:, 0, o_lo:T], headones, ycsq[:, o_lo:T])
                mm(o[:, 1, o_lo:T], lst[:, 2, :], lo[:, 2, o_lo:T]).then_inc(*full(s))

            def rwkv_tile(c, front, tail):
                for d in range(2):
                    pe.wait_ge(*E.count("ops_ready").next())
                    s, o = take()
                    for ch in range(NRC):
                        i_ = pe.transpose(o[:, ch // 4, P * (ch % 4):P * (ch % 4 + 1)], bk[d][:, P * ch:P * (ch + 1)], ident)
                    i_.then_inc(*full(s))
                    s, o = take()
                    if d == 0:
                        pe.wait_ge(*E.count("vs_ready").next())
                    for q in range(4):
                        i_ = pe.transpose(o[:, 0, P * q:P * (q + 1)], at[d][:, P * q:P * (q + 1)], ident)
                        if d == 0:
                            i_ = pe.transpose(o[:, 1, P * q:P * (q + 1)], vS[:, P * q:P * (q + 1)], ident)
                    i_.then_inc(*full(s))
                    for p in range(2):
                        s, o = take()
                        for q in range(4):
                            for h in range(2):
                                hs = slice(64 * h, 64 * h + 64)
                                ch = 2 * q + p
                                i_ = mm(o[:, h, P * q:P * (q + 1)].rearrange("p (a t) -> p a t", a=2), bk[d][hs, P * ch:P * (ch + 1)], art[d][hs, ch])
                        i_.then_inc(*full(s))

                def each(o, bank, l, r, w=RC, off=0):
                    for e in range(8):
                        for p in range(2):
                            pp = slice(64 * p, 64 * p + 64)
                            i2 = mm(o[pp, bank + (e * w) // 512, (e * w) % 512:(e * w) % 512 + w], l(pp, e), r(pp, e))
                    return i2

                def halves(o, off, l, r):
                    for e in range(8):
                        for g in range(4):
                            pp = slice(HB * g, HB * g + HB)
                            i2 = mm(o[pp, 0, off + HB * e:off + HB * (e + 1)], l[pp, e, :], r[pp, e, :])
                    return i2

                for d in range(2):
                    pe.wait_ge(*E.count("aa_ready").next())
                    s, o = take()
                    halves(o, 0, Dh[d], id32.unsqueeze(1).to_broadcast((P, 8, HB))).then_inc(*full(s))
                for m in range(1, 6):
                    if m == 1 and tail:
                        tail_mean(c - 1)
                    if m == 2 and front:
                        front_sum()
                    if m == 2 and tail:
                        tail_var()
                    if m == 2 and front:
                        front_lora(0)
                    if m == 5 and front:
                        front_lora(1)
                    for d in range(2):
                        pe.wait_ge(*E.count("xn_ready").next())
                        s, o = take()
                        if m < 5:
                            i_ = halves(o, 0, Dh[d], Xh[d])
                        else:
                            for e in range(8):
                                for p in range(2):
                                    a, b = slice(*across[d][p]), slice(*across[1 - d][p])
                                    i_ = mm(o[b, 0, HB * e:HB * (e + 1)], AA[d][p][a, e, 0, HB * (1 - d):HB * (2 - d)], Xh[d][a, e, :])
                        i_.then_inc(*full(s))
                    for d in range(2):
                        pe.wait_ge(*E.count("q_ready").next())
                        s, o = take()
                        if m < 5:
                            halves(o, 0, Qh[d], Nh[d])
                            i_ = halves(o, 256, Nh[d], Qh[d])
                        else:
                            for e in range(8):
                                for p in range(2):
                                    a, b = slice(*across[d][p]), slice(*across[1 - d][p])
                                    i_ = mm(o[a, 0, HB * e:HB * (e + 1)], Qh[d][b, e, :], Nh[d][b, e, :])
                        i_.then_inc(*full(s))
                for d in range(2):
                    if d == 0:
                        pe.wait_ge(*E.count("vtok_ready").next())
                    s, o = take()
                    for e in range(8):
                        for p in range(2):
                            kh, hs = slice(64 - 64 * p, 128 - 64 * p), slice(64 * p, 64 * p + 64)
                            i_ = mm(o[hs, 0, RC * e:RC * (e + 1)], AA[d][p][kh, e, 0, :], UV[d][p][kh, e, :])
                    i_.then_inc(*full(s))
                for d in range(2):
                    pe.wait_ge(*E.count("xn_ready").next())
                    pe.wait_ge(*E.count("r_ready").next())
                    pe.wait_ge(*E.count("tok_ready").next())
                    s, o = take()
                    each(o, 0, lambda pp, e: Ni[d][pp, e, :], lambda pp, e: RA[d][pp, e], w=P).then_inc(*full(s))

                def cross(o, l, r, whole, qs=range(4)):
                    for q in qs:
                        for p, h in ((0, 0), (1, 1), (0, 1), (1, 0)):
                            pp = slice(0, P) if whole else slice(64 * p, 64 * p + 64)
                            i2 = mm(o[64 * h:64 * h + 64, p, RC * q:RC * (q + 1)], l(pp, p, h, q), r(pp, p, h, q))
                    return i2

                def G(pp, p, h, q):
                    return Qi[d][pp, 4 * h + q, :]

                def uv(pp, p, h, q):
                    return UV[d][p][pp, 4 * h + q, :]

                def b_k(pp, p, h, q):
                    return BK[d][pp, 2 * q + p, h, :]

                def inclusive(pp, p, h, q):
                    return AA[d][p][pp, 4 * h + q, 1, :]

                for d in range(2):
                    pe.wait_ge(*E.count("ug_ready").next())
                    s, o = take()
                    cross(o, G, b_k, False).then_inc(*full(s))
                for d in range(2):
                    s, o = take()
                    cross(o, b_k, uv, True).then_inc(*full(s))
                qs = range(o_lo // P, 4)
                for k in range(2, NRC):
                    for d in range(2):
                        prev = RW_ORDER[d][k - 1]
                        pe.wait_ge(*E.count("s_ready").next())
                        s, o = take()
                        for h in range(2):
                            hs = slice(64 * h, 64 * h + 64)
                            i_ = mm(o[hs, 0, 0:RC], MT[d][hs, prev, :], Ni[d][hs, prev, :])
                        i_.then_inc(*full(s))
                    if k < 6:
                        d = k % 2
                        s, o = take()
                        if k < 4:
                            cross(o, G, inclusive, False, qs).then_inc(*full(s))
                        else:
                            cross(o, uv, inclusive, True, qs).then_inc(*full(s))
                s, o = take()
                for d in range(2):
                    pe.wait_ge(*E.count("s_ready").next())
                    pe.wait_ge(*E.count("rp_ready").next())
                    passed()
                    for ch in range(o_lo // RC, NRC):
                        for h in range(2):
                            hs = slice(64 * h, 64 * h + 64)
                            i_ = mm(o[hs, d, RC * ch:RC * (ch + 1)], Ni[d][hs, ch, :], rq[d][hs, RC * ch:RC * (ch + 1)])
                i_.then_inc(*full(s))

            def rwkv():
                front_sum()
                front_lora(0)
                front_lora(1)
                rwkv_tile(0, True, False)
                with E.loop(KT - 2) as i:
                    rwkv_tile(i + 1, True, True)
                rwkv_tile(KT - 1, False, True)
                tail_mean(KT - 1)
                tail_var()

            def ffn_down(lo_, hi):
                slots = [take() for _ in range(SLOTS)]

                for b in range(B_FO):
                    w = weights().rearrange("p (k m) -> p k m", k=2)
                    for k in range(2):
                        for m in range(8):
                            s, o = slots[m // 2]
                            i_ = mm(o[:, m % 2, 0:hi - lo_], w[:, k, P * m:P * (m + 1)], A[:, 2 * b + k, lo_:hi],
                                    b + k == 0, b == B_FO - 1 and k == 1)
                            if k == 0 and m == 0:
                                i_.then_inc(*E.count("w_used").sent())
                            if b == B_FO - 1 and k == 1 and m % 2:
                                i_.then_inc(*full(s))

            pe.wait_ge(*E.count("cond_ready").next())
            for L in range(DEPTH):
                o_lo, o_hi = N_OUT[L]
                adaln()
                channel_sum(SQ, KT, ready="sq_ready")
                dense(hT, B_XBC, ready="h_ready")
                pe.wait_ge(*E.count("scr_free").next())
                ssd()
                dense(hT, B_Z, o_lo, o_hi)
                for g in range(GROUPS):
                    s, o = take()
                    for k in range(4):
                        if k % 2 == 0:
                            pe.wait_ge(*E.count("ysq_ready").next())
                        i_ = mm(o[:, 0, 0:o_hi - o_lo], ones, YQ[:, 4 * g + k, o_lo:o_hi], k == 0, k == 3)
                    i_.then_inc(*full(s))
                for b in range(B_SO):
                    w = weights().rearrange("p (k m) -> p k m", k=XS_T)
                    s, o = take()
                    for k in range(XS_T):
                        if b == 0:
                            pe.wait_ge(*E.count("yn_ready").next())
                        i_ = mm(o[:, 0, 0:o_hi - o_lo], w[:, k, :], A[:, k, o_lo:o_hi], k == 0, k == XS_T - 1)
                        if k == 0:
                            i_.then_inc(*E.count("w_used").sent())
                    i_.then_inc(*full(s))
                dense(hT, B_GS, o_lo, o_hi)
                dense(hT, B_RKV)
                dense_block(hT, 0, T)
                dense_block(hT, 0, T, tiles=1)
                pe.wait_ge(*E.count("lora_ready").next())
                rwkv()
                pe.wait_ge(*E.count("yr_ready").next())
                dense(A, B_RO, o_lo, o_hi)
                dense(hT, B_GR, o_lo, o_hi)
                pe.wait_ge(*E.count("o_ready").next())
                dense(O, B_WO, o_lo, o_hi)
                channel_sum(SQ, KT, o_lo, o_hi, ready="sq_ready")
                channel_sum(SQ, KT, o_lo, o_hi, ready="sq_ready")
                dense(hT, B_FI, o_lo, o_hi, ready="h_ready")
                pe.wait_ge(*E.count("ffn_ready").next())
                ffn_down(o_lo, o_hi)
                channel_sum(SQ, KT, o_lo, o_hi, ready="sq_ready")

        @block.scalar
        def _(act):
            E = Engine(act, "act", sems, table)
            go = act.activation

            def rstd(lo_, hi, scale, eps, out_, bank=0):
                s, w = E.full()
                act.wait_ge(*w)
                go(out_[:, 0:hi - lo_], ps[:, 2 * s + bank, 0:hi - lo_], ACT.Sqrt, bias=eps, scale=scale).then_inc(*E.freed(s))

            def squares(src, lo_, hi, tiles=range(KT), ready=None):
                for k in tiles:
                    if ready:
                        act.wait_ge(*E.count(ready).next())
                    go(SQ[:, k, lo_:hi], src[:, k, lo_:hi], ACT.Square).then_inc(*E.done("sq_ready"))

            def copied(dst, lo_, hi):
                for b in range(4):
                    s, w = E.full()
                    act.wait_ge(*w)
                    go(dst[:, 2 * b:2 * b + 2, lo_:hi], ps[:, 2 * s:2 * s + 2, 0:hi - lo_], ACT.Copy).then_inc(*E.freed(s))
                    act.wait_ge(*E.mine())
                    squares(dst, lo_, hi, range(2 * b, 2 * b + 2))

            def modulate(shift, lo_, perm):
                for k in range(KT):
                    act.wait_ge(*E.count("norm_ready").next())
                    if lo_ == 0:
                        go(hT[:, k, 0:CTX], SQ[:, k, 0:CTX], ACT.Identity, bias=mod[:, 8 * shift + k, 1:2], scale=gsc[:, k, 1:2])
                    go(permuted(hT[:, k, CTX:T], perm), grid(SQ[:, k, CTX:T]), ACT.Identity, bias=mod[:, 8 * shift + k, 0:1], scale=gsc[:, k, 0:1])\
                        .then_inc(*E.done("h_ready"))

            def passed():
                if E.loop_now:
                    act.sem_inc(sems["act_passed"], 1)

            def conv_tiles(name, bias, silu, trips):
                with E.loop(trips) as i:
                    for b in range(4):
                        s, w = E.full()
                        act.wait_ge(*w)
                        passed()
                        for m in range(2):
                            t = i * 8 + (2 * b + m)
                            go(A[:, t, :], ps[:, 2 * s + m, :], ACT.Identity, bias=colr(L, bias, t) if bias else 0.0,
                               scale=colr(L, name, 24 + t)).then_inc(*E.done("tap_ready"))
                        if silu:
                            for m in range(2):
                                t = i * 8 + (2 * b + m)
                                act.wait_ge(*E.count("conv_ready").next())
                                passed()
                                go(A[:, t, :], A[:, t, :], ACT.Silu).then_inc(*E.done("conv_silu"))

            def ssd():
                E.skip(1)
                act.wait_ge(*E.count("abs_ready").next())
                go(sm_a, sm_a, ACT.Abs).then_inc(*E.done())
                act.wait_ge(*E.mine())
                go(sm_a, sm_a, ACT.Exp, scale=-1.0).then_inc(*E.done())
                go(expA, headp[:, L, 1], ACT.Exp).then_inc(*E.done())
                act.wait_ge(*E.mine())
                go(sm_b, sm_a, ACT.Ln, bias=1.0).then_inc(*E.done("log_ready"))
                E.skip(1)
                act.wait_ge(*E.count("dec_in_ready").next())
                go(dec, dec, ACT.Exp).then_inc(*E.done())
                go(wde, wde, ACT.Exp).then_inc(*E.done("dec_ready"))
                act.wait_ge(*E.count("scr_free").next())
                if L:
                    act.wait_ge(*E.count("dma_out").next())
                chunks = Y_CHUNKS[L]
                with E.loop(GROUPS) as g:
                    act.wait_ge(*E.count("y_ready").so_far())
                    E.count("y_ready").n += len(chunks)
                    passed()
                    for d in range(2):
                        go(dtag[:, d], heads4(dta)[:, d, :, bass.ds(g * HPG, HPG)], ACT.Copy).then_inc(*E.done())
                    go(Bg, A[:, XS_T + g, :], ACT.Copy).then_inc(*E.done())
                    go(xg, A[:, bass.ds(g * 4, 4), :], ACT.Copy).then_inc(*E.done("staged"))
                    s, w = E.full()
                    act.wait_ge(*w)
                    go(btok.rearrange("p c n -> p (c n)"), ps[:, 2 * s, :], ACT.Copy).then_inc(*E.done("btok_ready"))
                    act.wait_ge(*E.mine())
                    act.sem_inc(*E.freed(s))
                    for part in ((0, 1), (2,), (3,)):
                        s, w = E.full()
                        act.wait_ge(*w)
                        c, n = part[0], len(part)
                        go(scr[:, 5632 + 512 * c:5632 + 512 * (c + n)], ps[:, 2 * s:2 * s + n, :].rearrange("p b t -> p (b t)"), ACT.Copy)\
                            .then_inc(*E.freed(s))
                    E.skip(1)
                    for c in chunks:
                        for d in range(2):
                            s, w = E.full()
                            act.wait_ge(*w)
                            act.wait_ge(*E.count("diff_ready").next())
                            if SSD_ORDER[d].index(c):
                                go(Cb[c % 2][d], ps[:, 2 * s:2 * s + 2, :].rearrange("p b (h l) -> p (b h) l", h=4), ACT.Exp)\
                                    .then_inc(*E.done("ec_ready"))
                                act.wait_ge(*E.mine())
                            act.sem_inc(*E.freed(s))
                            go(Wb[c % 2][d], Wb[c % 2][d], ACT.Exp).then_inc(*E.done("e_ready"))
                        E.skip(1 if c > chunks[0] else 3)
                    E.skip(1)
                    E.sit_out(-(8 + 3 * len(chunks)) % SLOTS)

            def front_norm():
                E.skip(1)
                act.wait_ge(*E.count("kkmax_ready").next())
                go(exc, exc, ACT.Sqrt).then_inc(*E.done("kkstd_ready"))

            def front_sigmoids(c, d):
                s, w = E.full()
                act.wait_ge(*w)
                if front_sigmoids.later:
                    act.wait_ge(*E.count("ops_ready").next())
                front_sigmoids.later = True
                passed()
                go(sg, ps[:, 2 * s, :], ACT.Sigmoid, bias=colr(L, "w0", c + 8 * d)).then_inc(*E.done())
                go(asg, ps[:, 2 * s + 1, :], ACT.Sigmoid, bias=colr(L, "a0", c + 8 * d)).then_inc(*E.freed(s))
                act.wait_ge(*E.mine())
                act.sem_inc(*E.done("sa_ready"))
            front_sigmoids.later = False

            def front_decays(d):
                act.wait_ge(*E.count("cum_ready").next())
                go(wc[d], e8(pre)[:, :, RC - 1], ACT.Exp, scale=-WSCALE).then_inc(*E.done())
                go(exc, exc, ACT.Exp, scale=-WSCALE).then_inc(*E.done())
                go(sg, inc, ACT.Exp, scale=-WSCALE).then_inc(*E.done())
                act.wait_ge(*E.mine())
                go(inc, inc, ACT.Exp, scale=WSCALE).then_inc(*E.done("exps_ready"))

            def tail_square():
                E.skip(1)
                act.wait_ge(*E.count("yc_ready").next())
                go(ycsq[:, lo_:T], yc[:, lo_:T], ACT.Square).then_inc(*E.done("ycsq_ready"))

            def tail_std():
                s, w = E.full()
                act.wait_ge(*w)
                go(yac[:, lo_:T], ps[:, 2 * s + 1, lo_:T], ACT.Copy).then_inc(*E.done())
                go(ystd[:, lo_:T], ps[:, 2 * s, lo_:T], ACT.Sqrt, bias=LN_EPS, scale=1.0 / 64).then_inc(*E.done("ystd_ready"))
                act.wait_ge(*E.mine())
                act.sem_inc(*E.freed(s))

            def rwkv_tile(c, front, tail):
                if tail:
                    act.wait_ge(*E.count("yb_ready").next())
                for d in range(2):
                    s, w = E.full()
                    act.wait_ge(*w)
                    go(BK[d].rearrange("p c h k -> p (c h k)"), ps[:, 2 * s:2 * s + 2, :].rearrange("p b x -> p (b x)"), ACT.Copy).then_inc(*E.freed(s))
                    s, w = E.full()
                    act.wait_ge(*w)
                    if d == 0:
                        for p in range(2):
                            kh = slice(64 - 64 * p, 128 - 64 * p)
                            for d_ in range(2):
                                i_ = go(UV[d_][p][kh].rearrange("p (h q) k -> p q h k", h=2),
                                        ps[kh, 2 * s + 1, :].rearrange("p (q h k) -> p q h k", q=4, h=2), ACT.Copy)
                        i_.then_inc(*E.done("vtok_ready"))
                    go(RAq[d][:, :, :, 1, :], ps[:, 2 * s, :].rearrange("p (q h k) -> p q h k", q=4, h=2), ACT.Copy).then_inc(*E.done("tok_ready"))
                    act.wait_ge(*E.mine())
                    act.sem_inc(*E.freed(s))
                    E.skip(2)
                E.skip(2)
                for m in range(1, 6):
                    if m == 1 and tail:
                        tail_square()
                    if m == 2 and front:
                        front_norm()
                    if m == 2 and tail:
                        tail_std()
                    if m == 2 and front:
                        front_sigmoids(c + 1, 0)
                    if m == 4 and front:
                        front_decays(0)
                    if m == 5 and front:
                        front_sigmoids(c + 1, 1)
                    E.skip(4)
                if front:
                    front_decays(1)
                for d in range(2):
                    s, w = E.full()
                    act.wait_ge(*w)
                    go(RA[d][:, :, 0, :], e8(ps[:, 2 * s, :]), ACT.Copy).then_inc(*E.done("r_ready"))
                    act.wait_ge(*E.mine())
                    act.sem_inc(*E.freed(s))
                for d in range(2):
                    s, w = E.full()
                    act.wait_ge(*w)
                    ug = ps[:, 2 * s:2 * s + 2, :].rearrange("p b (e a t) -> p (b e) a t", e=4, a=2)
                    for p in range(2):
                        hs = slice(64 * p, 64 * p + 64)
                        go(UV[d][p][hs], ug[hs, :, 0, :], ACT.Copy).then_inc(*E.done())
                    go(Qi[d], ug[:, :, 1, :], ACT.Copy).then_inc(*E.done("ug_ready"))
                    act.wait_ge(*E.mine())
                    act.sem_inc(*E.freed(s))
                E.skip(2 + 2 + 12 + 2 + 2 + 1)

            def rwkv():
                front_norm()
                for d in range(2):
                    front_sigmoids(0, d)
                    front_decays(d)
                rwkv_tile(0, True, False)
                with E.loop(KT - 2) as i:
                    rwkv_tile(i + 1, True, True)
                rwkv_tile(KT - 1, False, True)
                tail_square()
                tail_std()
                E.count("yb_ready").n += 1

            act.wait_ge(*E.count("dma_cond").next())
            go(cond[:, :, :], cond[:, :, :], ACT.Silu).then_inc(*E.done("cond_ready"))
            for L in range(DEPTH):
                lo_, hi = N_OUT[L]
                n = hi - lo_
                def copy_row(r):
                    s, w = E.full()
                    act.wait_ge(*w)
                    go(rows[0:2, r, :], ps[0:2, 2 * s, :], ACT.Copy).then_inc(*E.done("row_ready"))
                    act.wait_ge(*E.mine())
                    act.sem_inc(*E.freed(s))
                copy_row(0)
                copy_row(1)
                E.skip(1)
                with E.loop(5):
                    for r in range(2):
                        copy_row(r)
                        E.skip(1)
                E.skip(1)
                act.wait_ge(sems["dma_const"], 16 * 4)
                act.wait_ge(*(E.count("dma_x").next() if L == 0 else E.count("x_ready").so_far()))
                squares(X, 0, T)
                rstd(0, T, 1.0 / D, EPS, rst)
                modulate(0, 0, L == 1)
                conv_tiles("scw", "scb", True, 3)
                ssd()
                with E.loop(2) as i:
                    for b in range(4):
                        s, w = E.full()
                        act.wait_ge(*w)
                        go(ZS[:, b % 2, :, 0:n], ps[:, 2 * s:2 * s + 2, 0:n], ACT.Silu).then_inc(*E.done("zs_ready"))
                        act.wait_ge(*E.mine())
                        act.sem_inc(*E.freed(s))
                        E.count("yz_ready").n += 1
                        act.wait_ge(*E.count("yz_ready").so_far())
                        passed()
                        go(YQ[:, bass.ds(i * 8 + 2 * b, 2), lo_:hi], A[:, bass.ds(i * 8 + 2 * b, 2), lo_:hi], ACT.Square).then_inc(*E.done("ysq_ready"))
                for g in range(GROUPS):
                    rstd(lo_, hi, 4.0 / D_SSM, EPS, GR[g])
                with E.loop(2) as i:
                    for b in range(4):
                        s, w = E.full()
                        act.wait_ge(*w)
                        passed()
                        go(O[:, i * 4 + b, lo_:hi], ps[:, 2 * s, 0:n], ACT.Copy).then_inc(*E.freed(s))
                for b in range(4):
                    s, w = E.full()
                    act.wait_ge(*w)
                    go(SG[:, 2 * b:2 * b + 2, lo_:hi], ps[:, 2 * s:2 * s + 2, 0:n], ACT.Sigmoid).then_inc(*E.freed(s))
                act.wait_ge(*E.mine())
                act.sem_inc(*E.done("gate_ready"))
                conv_tiles("rcw", None, False, 3)
                E.count("conv_ready").n += RK_T
                s, w = E.full()
                act.wait_ge(*w)
                go(lo[:, 0, :], ps[:, 2 * s, :], ACT.Tanh).then_inc(*E.done())
                go(lo[:, 1, :], ps[:, 2 * s + 1, :], ACT.Copy).then_inc(*E.freed(s))
                s, w = E.full()
                act.wait_ge(*w)
                go(lo[:, 2, :], ps[:, 2 * s, :], ACT.Sigmoid).then_inc(*E.freed(s))
                act.wait_ge(*E.mine())
                act.sem_inc(*E.done("lora_ready"))
                rwkv()
                for b in range(4):
                    s, w = E.full()
                    act.wait_ge(*w)
                    go(SG[:, 2 * b:2 * b + 2, lo_:hi], ps[:, 2 * s:2 * s + 2, 0:n], ACT.Copy).then_inc(*E.freed(s))
                for b in range(4):
                    s, w = E.full()
                    act.wait_ge(*w)
                    go(lo[:, 0:2, 0:n], ps[:, 2 * s:2 * s + 2, 0:n], ACT.Sigmoid).then_inc(*E.done("gate_ready"))
                    act.wait_ge(*E.count("out_ready").next())
                    act.wait_ge(*E.mine())
                    act.sem_inc(*E.freed(s))
                copied(hT, lo_, hi)
                rstd(lo_, hi, 1.0 / D, EPS, rst)
                squares(X, lo_, hi, ready="x_ready")
                rstd(lo_, hi, 1.0 / D, EPS, rst)
                modulate(3, lo_, False)
                def ffn_tile(s, w, t):
                    act.wait_ge(*w)
                    passed()
                    go(A[:, t, lo_:hi], ps[:, 2 * s, 0:n], ACT.Identity, bias=colr(L, "fcb", t), scale=colr(L, "fcw", 4 * FF_T + t))\
                        .then_inc(*E.done("tap2_ready"))
                    act.wait_ge(*E.count("conv_ready").next())
                    passed()
                    go(A[:, t, lo_:hi], A[:, t, lo_:hi], ACT.Gelu_apprx_tanh).then_inc(*E.done("gelu_ready"))
                with E.loop(5) as i:
                    for b in range(4):
                        ffn_tile(*E.full(), i * 4 + b)
                for t in range(20, 22):
                    ffn_tile(*E.full(), t)
                copied(O, lo_, hi)
                rstd(lo_, hi, 1.0 / D, EPS, rst)
                E.count("x_ready").n += KT


        @block.vector
        def _(v):
            E = Engine(v, "dve", sems, table)
            tt, ts, stt = v.tensor_tensor, v.tensor_scalar, v.scalar_tensor_tensor

            def own():
                v.wait_ge(*E.mine())

            def recip(lo_, hi):
                s, w = E.full()
                v.wait_ge(sems[f"slot_free{s}"], E.count(f"slot_free{s}").so_far()[1])
                v.reciprocal(rst[:, 0:hi - lo_], rst[:, 0:hi - lo_]).then_inc(*E.done())

            def prenorm(L, gain, shift, lo_=0):
                own()
                stt(out=gsc[:, :, :], in0=mod[:, 8 * (shift + 1):8 * (shift + 2), :], scalar=1.0,
                    in1=par[:, L, COLS[gain]:COLS[gain] + 8].unsqueeze(2).to_broadcast((P, KT, 2)), op0=ALU.add, op1=ALU.mult)\
                    .then_inc(*E.done())
                recip(lo_, T)
                own()
                for k in range(KT):
                    tt(SQ[:, k, lo_:T], X[:, k, lo_:T], rst[:, 0:T - lo_], ALU.mult).then_inc(*E.done("norm_ready"))

            def postnorm(L, src, gain, gate, perm, lo_):
                own()
                tt(gsc[:, :, :], mod[:, 8 * gate:8 * gate + 8, :],
                   par[:, L, COLS[gain]:COLS[gain] + 8].unsqueeze(2).to_broadcast((P, KT, 2)), ALU.mult).then_inc(*E.done())
                recip(lo_, T)
                own()
                def scaled(k):
                    tt(SQ[:, k, lo_:T], src[:, k, lo_:T], rst[:, 0:T - lo_], ALU.mult).then_inc(*E.done())
                    return E.mine()

                ready = scaled(0)
                for k in range(KT):
                    this, ready = ready, scaled(k + 1) if k + 1 < KT else None
                    v.wait_ge(*this)
                    if lo_ == 0:
                        stt(out=X[:, k, 0:CTX], in0=SQ[:, k, 0:CTX], scalar=gsc[:, k, 1:2], in1=X[:, k, 0:CTX], op0=ALU.mult, op1=ALU.add)
                    stt(out=grid(X[:, k, CTX:T]), in0=permuted(SQ[:, k, CTX:T], perm), scalar=gsc[:, k, 0:1],
                        in1=grid(X[:, k, CTX:T]), op0=ALU.mult, op1=ALU.add).then_inc(*E.done("x_ready"))

            def conv_tiles(name, trips):
                with E.loop(trips) as i:
                    for b in range(4):
                        s, w = E.full()
                        for m in range(2):
                            t = i * 8 + (2 * b + m)
                            v.wait_ge(*E.count("tap_ready").next())
                            src, dst = seg2(ps[:, 2 * s + m, :]), seg2(A[:, t, :])
                            stt(out=dst[:, :, 1:256], in0=src[:, :, 0:255], scalar=colr(L, name, t), in1=dst[:, :, 1:256],
                                op0=ALU.mult, op1=ALU.add).then_inc(*E.done())
                            own()
                            i_ = stt(out=dst[:, :, 0:255], in0=src[:, :, 1:256], scalar=colr(L, name, 48 + t), in1=dst[:, :, 0:255],
                                     op0=ALU.mult, op1=ALU.add)
                            i_.then_inc(*E.done("conv_ready"))
                        own()
                        v.sem_inc(*E.freed(s))

            def ssd():
                s, w = E.full()
                v.wait_ge(*w)
                raw = ps[:, 2 * s, 0:P].rearrange("p (c h) -> p c h", c=NCH)
                for d in range(2):
                    i_ = tt(heads4(sm_a)[:, d], raw, headp[:, L, 0, d, :].unsqueeze(1).to_broadcast((P, NCH, HEADS)), ALU.add)
                i_.then_inc(*E.freed(s))
                own()
                ts(dtv, sm_a, 0.0, None, ALU.max).then_inc(*E.done("abs_ready"))
                v.wait_ge(*E.count("log_ready").next())
                ts(sm_c, sm_a, 1.0, None, ALU.add).then_inc(*E.done())
                own()
                stt(out=sm_a, in0=sm_c, scalar=-1.0, in1=sm_a, op0=ALU.add, op1=ALU.subtract).then_inc(*E.done())
                own()
                v.reciprocal(sm_c, sm_c).then_inc(*E.done())
                own()
                tt(sm_a, sm_a, sm_c, ALU.mult).then_inc(*E.done())
                tt(dtv, dtv, sm_b, ALU.add).then_inc(*E.done())
                own()
                tt(dtv, dtv, sm_a, ALU.subtract).then_inc(*E.done())
                own()
                for d in range(2):
                    i_ = stt(out=heads4(dta)[:, d], in0=heads4(dtv)[:, d], scalar=-1.0,
                             in1=expA[:, HEADS * d:HEADS * (d + 1)].unsqueeze(1).to_broadcast((P, NCH, HEADS)), op0=ALU.mult, op1=ALU.mult)
                i_.then_inc(*E.done("dta_ready"))
                s, w = E.full()
                v.wait_ge(*w)
                ts(ncs, ps[:, 2 * s, 0:256], -1.0, None, ALU.mult).then_inc(*E.done())
                v.tensor_copy(dec, ps[:, 2 * s + 1, 0:256]).then_inc(*E.freed(s))
                own()
                tt(wde, dec, ncs, ALU.add).then_inc(*E.done("dec_in_ready"))
                v.wait_ge(*E.count("dec_ready").next())
                tt(wde, wde, dtv, ALU.mult).then_inc(*E.done("wdec_ready"))
                own()
                chunks = Y_CHUNKS[L]
                with E.loop(GROUPS) as g:
                    hsl = bass.ds(g * HPG, HPG)

                    def per_head(ap, d, c):
                        return heads4(ap)[:, d, c, hsl].unsqueeze(2).to_broadcast((P, HPG, 64))

                    E.skip(2)
                    for _ in range(2):
                        s, w = E.full()
                    v.wait_ge(sems[f"slot_free{(s - 2) % SLOTS}"], E.count(f"slot_free{(s - 2) % SLOTS}").so_far()[1])
                    v.wait_ge(sems[f"slot_free{(s - 1) % SLOTS}"], E.count(f"slot_free{(s - 1) % SLOTS}").so_far()[1])
                    v.wait_ge(sems[f"slot_free{s}"], E.count(f"slot_free{s}").so_far()[1])
                    def weighted(o_):
                        for d in range(2):
                            c = SSD_ORDER[d][o_]
                            tt(xw[o_ % 2][d], xtok[:, c], per_head(wde, d, c), ALU.mult).then_inc(*E.done("xw_ready"))

                    def differences(c):
                        for d in range(2):
                            s, w = E.full()
                            v.wait_ge(*w)
                            tt(Wb[c % 2][d], ps[:, 2 * s:2 * s + 2, :].rearrange("p b (h l) -> p (b h) l", h=4),
                               heads4(ncs)[:, d, c, hsl].unsqueeze(2).to_broadcast((P, HPG, P)), ALU.add).then_inc(*E.done())
                            own()
                            ts(Wb[c % 2][d], Wb[c % 2][d], 0.0, None, ALU.min).then_inc(*E.done("diff_ready"))

                    weighted(0)
                    weighted(1)
                    s, w = E.full()
                    v.wait_ge(*w)
                    for d in range(2):
                        i_ = tt(cbm[d], ps[:, 2 * s, :].rearrange("p (c l) -> p c l", c=NCH), tri[d].unsqueeze(1).to_broadcast((P, NCH, P)), ALU.mult)
                    i_.then_inc(*E.freed(s))
                    differences(chunks[0])
                    for o_ in range(3):
                        s, w = E.full()
                        v.wait_ge(*w)
                        if o_ == 0:
                            weighted(2)
                        for d in range(2):
                            c = SSD_ORDER[d][o_]
                            st = ps[:, 2 * s + d, :].rearrange("p (h x) -> p h x", h=HPG)
                            if o_ == 0:
                                v.tensor_copy(Hs[d][0], st).then_inc(*E.done())
                            else:
                                tt(Hs[d][o_], Hs[d][o_ - 1], per_head(dec, d, c), ALU.mult).then_inc(*E.done())
                                own()
                                tt(Hs[d][o_], Hs[d][o_], st, ALU.add).then_inc(*E.done())
                        own()
                        v.sem_inc(*E.freed(s))
                    for c in chunks:
                        for d in range(2):
                            v.wait_ge(*E.count("e_ready").next())
                            i_ = tt(Wb[c % 2][d], Wb[c % 2][d], cbm[d][:, c, :].unsqueeze(1).to_broadcast((P, HPG, P)), ALU.mult)
                        i_.then_inc(*E.done("w_ready"))
                        if c + 1 < NCH:
                            differences(c + 1)
                        s, w = E.full()
                        v.wait_ge(*w)
                        for j in range(4):
                            i_ = stt(out=A[:, g * 4 + j, Q * c:Q * (c + 1)], in0=A[:, g * 4 + j, Q * c:Q * (c + 1)],
                                     scalar=colr(L, "dskip", g * 4 + j), in1=ps[:, 2 * s, P * j:P * (j + 1)], op0=ALU.mult, op1=ALU.add)
                        i_.then_inc(*E.done("y_ready"))
                        own()
                        v.sem_inc(*E.freed(s))
                    E.sit_out(-(8 + 3 * len(chunks)) % SLOTS)

            def front_square(c):
                own()
                ts(kkn, A[:, 8 + c, :], colr(L, "kk", c), None, ALU.mult).then_inc(*E.done())
                own()
                tt(exc, kkn, kkn, ALU.mult).then_inc(*E.done("kksq_ready"))

            def front_max():
                s, w = E.full()
                v.wait_ge(*w)
                ts(exc, ps[:, 2 * s, :], 1e-24, None, ALU.max).then_inc(*E.done("kkmax_ready"))
                own()
                v.sem_inc(*E.freed(s))

            def front_norm():
                v.wait_ge(*E.count("kkstd_ready").next())
                v.reciprocal(exc, exc).then_inc(*E.done())
                own()
                tt(kkn, kkn, exc, ALU.mult).then_inc(*E.done())

            def front_cumulate(d):
                own()
                v.wait_ge(*E.count("sa_ready").next())
                v.tensor_tensor_scan(pre, reset, sg, 0.0, ALU.mult, ALU.add).then_inc(*E.done())
                own()
                if d == 0:
                    tt(exc, pre, sg, ALU.subtract).then_inc(*E.done())
                    i_ = v.tensor_copy(inc, pre)
                else:
                    tt(e8(exc), e8(pre)[:, :, RC - 1:RC].to_broadcast((P, 8, RC)), e8(pre), ALU.subtract).then_inc(*E.done())
                    own()
                    i_ = tt(inc, exc, sg, ALU.add)
                i_.then_inc(*E.done("cum_ready"))

            def front_operands(c, d):
                r_, k_ = A[:, c, :], A[:, 8 + c, :]
                v.wait_ge(*E.count("exps_ready").next())
                kd = pre
                ts(kd, asg, -1.0, colr(L, "ka", c), ALU.add, ALU.mult).then_inc(*E.done())
                own()
                stt(out=kd, in0=kd, scalar=1.0, in1=k_, op0=ALU.add, op1=ALU.mult).then_inc(*E.done())
                stt(out=at[d], in0=kkn, scalar=-1.0, in1=exc, op0=ALU.mult, op1=ALU.mult)
                tt(rt[d], r_, sg, ALU.mult)
                tt(bt[d], quads(kkn), quads(asg), ALU.mult).then_inc(*E.done())
                own()
                if d == 0:
                    v.tensor_copy(kds, kd)
                else:
                    tt(kds, kds, kd, ALU.add).then_inc(*E.done())
                    own()
                    stt(out=k_, in0=kds, scalar=colr(L, "rk", c), in1=r_, op0=ALU.mult, op1=ALU.mult)
                tt(bt[d], bt[d], quads(inc), ALU.mult)
                tt(kt[d], quads(kd), quads(inc), ALU.mult).then_inc(*E.done("ops_ready"))

            def tail_center(c):
                s, w = E.full()
                v.wait_ge(*w)
                stt(out=yc[:, lo_:T], in0=ps[:, 2 * s, lo_:T], scalar=-1.0 / 64, in1=yac[:, lo_:T], op0=ALU.mult, op1=ALU.add).then_inc(*E.done("yc_ready"))
                tt(bonus[:, lo_:T], ps[:, 2 * s + 1, lo_:T], A[:, 16 + c, lo_:T], ALU.mult).then_inc(*E.freed(s))

            def tail_rstd():
                v.wait_ge(*E.count("ystd_ready").next())
                v.reciprocal(ystd[:, lo_:T], ystd[:, lo_:T]).then_inc(*E.done())

            def tail_norm(c):
                y = yc[:, lo_:T]
                own()
                tt(y, y, ystd[:, lo_:T], ALU.mult).then_inc(*E.done())
                own()
                ts(y, y, colr(L, "lnw", c), colr(L, "lnb", c), ALU.mult, ALU.add).then_inc(*E.done())
                own()
                tt(y, y, bonus[:, lo_:T], ALU.add).then_inc(*E.done())
                own()
                tt(A[:, c, lo_:T], y, yac[:, lo_:T], ALU.mult).then_inc(*E.done())

            def rwkv_tile(c, front, tail):
                own()
                for d in range(2):
                    v.tensor_copy(rq[d], rt[d]).then_inc(*E.done())
                    v.tensor_copy(wcu[d], wc[d]).then_inc(*E.done())
                own()
                for d in range(2):
                    E.skip(2)
                    for p in range(2):
                        s, w = E.full()
                        v.wait_ge(*w)
                        tt(AA[d][p].rearrange("p e a t -> p e (a t)"), ps[:, 2 * s:2 * s + 2, :].rearrange("p b (q x) -> p (b q) x", q=4),
                           mask2[d].unsqueeze(1).to_broadcast((P, 8, P)), ALU.mult).then_inc(*E.freed(s))
                    own()
                    for p in range(2):
                        hs = slice(64 * p, 64 * p + 64)
                        ts(Nh[d][hs], AA[d][p][hs, :, 0, 0:HB], half[hs, 0:1], None, ALU.mult).then_inc(*E.done())
                    own()
                    for p in range(2):
                        hs = slice(64 * p, 64 * p + 64)
                        i_ = stt(out=Dh[d][hs], in0=AA[d][p][hs, :, 0, HB:RC], scalar=half[hs, HB:HB + 1], in1=Nh[d][hs], op0=ALU.mult, op1=ALU.add)
                    i_.then_inc(*E.done("aa_ready"))
                if not front:
                    own()
                    v.sem_inc(*E.done("ring_free"))
                idb = id32.unsqueeze(1).to_broadcast((P, 8, HB))
                for d in range(2):
                    s, w = E.full()
                    v.wait_ge(*w)
                    own()
                    tt(Xh[d], ps[:, 2 * s, 0:256].rearrange("p (e t) -> p e t", e=8), lvl[0][d].unsqueeze(1).to_broadcast((P, 8, HB)), ALU.mult)\
                        .then_inc(*E.freed(s))
                    tt(Nh[d], Dh[d], lvl[0][1 - d].unsqueeze(1).to_broadcast((P, 8, HB)), ALU.mult).then_inc(*E.done())
                    own()
                    tt(Xh[d], Xh[d], idb, ALU.add)
                    tt(Nh[d], Nh[d], idb, ALU.add).then_inc(*E.done("xn_ready"))
                for m in range(1, 6):
                    if m == 1 and tail:
                        tail_center(c - 1)
                    if m == 2 and front:
                        front_max()
                    if m == 2:
                        E.skip(tail + front)
                    if m == 3 and tail:
                        tail_norm(c - 1)
                    if m == 4 and front:
                        front_cumulate(0)
                    if m == 5 and front:
                        E.skip(1)
                    for d in range(2):
                        s, w = E.full()
                        v.wait_ge(*w)
                        product = ps[:, 2 * s, 0:256].rearrange("p (e t) -> p e t", e=8)
                        if m < 5:
                            tt(Qh[d], product, lvl[m][d].unsqueeze(1).to_broadcast((P, 8, HB)), ALU.mult).then_inc(*E.done("q_ready"))
                            own()
                            v.sem_inc(*E.freed(s))
                        else:
                            for a, b in across[1 - d]:
                                i_ = v.tensor_copy(Qh[d][a:b], product[a:b])
                            i_.then_inc(*E.done("q_ready"))
                            tt(Ni[d].rearrange("p e (b t) -> p e b t", b=2), Nh[d].unsqueeze(2).to_broadcast((P, 8, 2, HB)),
                               half.rearrange("p (b t) -> p b t", b=2).unsqueeze(1).to_broadcast((P, 8, 2, HB)), ALU.mult).then_inc(*E.freed(s))
                    if m == 1 and front:
                        front_square(c + 1)
                    if m == 2 and tail:
                        tail_rstd()
                    if m == 3 and front:
                        front_norm()
                    if m == 4 and front:
                        front_operands(c + 1, 0)
                    for d in range(2):
                        s, w = E.full()
                        v.wait_ge(*w)
                        if m < 5:
                            nx = scr[:, RD * d:RD * d + 512]
                            i_ = tt(nx, nx, ps[:, 2 * s, :], ALU.add)
                        else:
                            own()
                            for a, b in across[d]:
                                i_ = v.tensor_copy(Ni[d][a:b, :, HB * (1 - d):HB * (2 - d)],
                                                   ps[a:b, 2 * s, 0:256].rearrange("p (e t) -> p e t", e=8))
                        i_.then_inc(*E.done("xn_ready"))
                        own()
                        v.sem_inc(*E.freed(s))
                if front:
                    front_cumulate(1)
                    front_operands(c + 1, 1)
                E.skip(4)
                idpq = id64.unsqueeze(1).unsqueeze(1).to_broadcast((P, 2, 4, RC))
                for d in range(2):
                    s, w = E.full()
                    v.wait_ge(*w)
                    for p in range(2):
                        i_ = tt(MT[d].rearrange("p (q two) t -> p two q t", two=2)[:, p], ps[:, 2 * s + p, 0:256].rearrange("p (q t) -> p q t", q=4),
                                idpq[:, 0], ALU.add)
                    i_.then_inc(*E.freed(s))
                for d in range(2):
                    s, w = E.full()
                    v.wait_ge(*w)
                    for p in range(2):
                        i_ = tt(Kv[d].rearrange("p (q two) t -> p two q t", two=2)[:, p], ps[:, 2 * s + p, 0:256].rearrange("p (q t) -> p q t", q=4),
                                wcu[d].rearrange("p (q two) -> p two q", two=2)[:, p].unsqueeze(2).to_broadcast((P, 4, RC)), ALU.mult)
                    i_.then_inc(*E.freed(s))
                own()
                for d in range(2):
                    v.memset(Ni[d][:, RW_ORDER[d][0], :], 0.0)
                    v.tensor_copy(Ni[d][:, RW_ORDER[d][1], :], Kv[d][:, RW_ORDER[d][0], :]).then_inc(*E.done("s_ready"))
                q0 = lo_ // P
                for k in range(2, NRC):
                    for d in range(2):
                        prev, here = RW_ORDER[d][k - 1], RW_ORDER[d][k]
                        s, w = E.full()
                        v.wait_ge(*w)
                        stt(out=Ni[d][:, here, :], in0=ps[:, 2 * s, 0:RC], scalar=wcu[d][:, prev:prev + 1], in1=Kv[d][:, prev, :],
                            op0=ALU.mult, op1=ALU.add).then_inc(*E.done("s_ready"))
                        own()
                        v.sem_inc(*E.freed(s))
                    if k < 6:
                        d = k % 2
                        s, w = E.full()
                        v.wait_ge(*w)
                        if k == 5:
                            own()
                        dst = rq[d] if k < 4 else yac
                        for p in range(2):
                            part, new = by_pq(dst)[:, p, q0:4], ps[:, 2 * s + p, RC * q0:256].rearrange("p (q t) -> p q t", t=RC)
                            if k == 4:
                                i_ = v.tensor_copy(part, new)
                            else:
                                i_ = tt(part, part, new, ALU.add)
                        i_.then_inc(*(E.done("rp_ready") if k < 4 else E.freed(s)))
                        if k < 4:
                            own()
                            v.sem_inc(*E.freed(s))
                s, w = E.full()
                v.wait_ge(*w)
                own()
                tt(yac[:, lo_:T], yac[:, lo_:T], ps[:, 2 * s, lo_:T], ALU.add).then_inc(*E.done())
                own()
                tt(yac[:, lo_:T], yac[:, lo_:T], ps[:, 2 * s + 1, lo_:T], ALU.add).then_inc(*E.freed(s))
                own()
                v.sem_inc(*E.done("yb_ready"))

            def rwkv():
                v.wait_ge(*E.count("lora_ready").next())
                front_square(0)
                front_max()
                front_norm()
                for d in range(2):
                    E.skip(1)
                    front_cumulate(d)
                    front_operands(0, d)
                rwkv_tile(0, True, False)
                with E.loop(KT - 2) as i:
                    rwkv_tile(i + 1, True, True)
                rwkv_tile(KT - 1, False, True)
                tail_center(KT - 1)
                E.skip(1)
                tail_rstd()
                tail_norm(KT - 1)

            for name in names:
                if name.startswith(PRIMED):
                    v.sem_inc(sems[name], 1)
            v.wait_ge(sems["dma_const"], 16 * 4)
            v.wait_ge(*E.count("dma_x").next())
            for L in range(DEPTH):
                lo_, hi = N_OUT[L]
                n = hi - lo_
                def add_bias(first):
                    s, w = E.full()
                    v.wait_ge(*w)
                    tt(mod[:, bass.ds(first, 4), :], ps[:, 2 * s, 0:8].rearrange("p (j c) -> p j c", j=4),
                       par[:, L, bass.ds(first + COLS["adab"], 4)].unsqueeze(2).to_broadcast((P, 4, 2)), ALU.add).then_inc(*E.freed(s))
                E.skip(2)
                add_bias(0)
                with E.loop(5) as i:
                    for r in range(2):
                        E.skip(1)
                        add_bias((i * 2 + (r + 1)) * 4)
                add_bias(44)
                own()
                prenorm(L, "npre", 0)
                conv_tiles("scw", 3)
                E.count("h_ready").n += KT
                v.wait_ge(*E.count("h_ready").so_far())
                v.wait_ge(*E.mine())
                v.sem_inc(*E.done("scr_free"))
                ssd()
                with E.loop(2) as i:
                    for b in range(4):
                        E.skip(1)
                        v.wait_ge(*E.count("zs_ready").next())
                        for m in range(2):
                            t = i * 8 + (2 * b + m)
                            i_ = tt(A[:, t, lo_:hi], A[:, t, lo_:hi], ZS[:, b % 2, m, 0:n], ALU.mult)
                        i_.then_inc(*E.done("yz_ready"))
                for g in range(GROUPS):
                    s, w = E.full()
                    v.wait_ge(sems[f"slot_free{s}"], E.count(f"slot_free{s}").so_far()[1])
                    rg = GR[g][:, 0:n]
                    v.reciprocal(rg, rg).then_inc(*E.done())
                    own()
                    for j in range(4):
                        t = 4 * g + j
                        stt(out=A[:, t, lo_:hi], in0=A[:, t, lo_:hi], scalar=col(L, "snorm", t), in1=rg, op0=ALU.mult, op1=ALU.mult)\
                            .then_inc(*E.done("yn_ready"))
                E.skip(8 + 4)
                v.wait_ge(*E.count("gate_ready").next())
                tt(O[:, :, lo_:hi], O[:, :, lo_:hi], SG[:, :, lo_:hi], ALU.mult).then_inc(*E.done())
                conv_tiles("rcw", 3)
                E.skip(2)
                own()
                v.memset(reset, 1.0).then_inc(*E.done())
                own()
                v.memset(e8(reset)[:, :, 0:1], 0.0).then_inc(*E.done())
                rwkv()
                v.wait_ge(*E.mine())
                v.sem_inc(*E.done("yr_ready"))
                E.skip(4)
                for b in range(4):
                    E.skip(1)
                    v.wait_ge(*E.count("gate_ready").next())
                    gated = SG[:, 2 * b:2 * b + 2, lo_:hi]
                    tt(gated, gated, lo[:, 0:2, 0:n], ALU.mult).then_inc(*E.done("out_ready"))
                    own()
                    tt(O[:, 2 * b:2 * b + 2, lo_:hi], O[:, 2 * b:2 * b + 2, lo_:hi], gated, ALU.add).then_inc(*E.done())
                own()
                v.sem_inc(*E.done("o_ready"))
                E.skip(4)
                v.wait_ge(*E.count("dma_x").next())
                postnorm(L, hT, "npost", 2, L == 1, lo_)
                prenorm(L, "fpre", 3, lo_)

                def ffn_tile(s, t):
                    v.wait_ge(*E.count("tap2_ready").next())
                    first = True
                    if lo_ == 0:
                        src, dst = ps[:, 2 * s, 0:CTX], A[:, t, 0:CTX]
                        for o_, a, b in ((3, 1, 0), (5, 0, 1)):
                            stt(out=dst[:, a:a + 255], in0=src[:, b:b + 255], scalar=colr(L, "fcw", t + FF_T * o_), in1=dst[:, a:a + 255],
                                op0=ALU.mult, op1=ALU.add).then_inc(*E.done())
                            own()
                    src, dst = grid(ps[:, 2 * s, CTX - lo_:T - lo_]), grid(A[:, t, CTX:T])
                    for dr in (-1, 0, 1):
                        for dc in (-1, 0, 1):
                            if dr == dc == 0:
                                continue
                            r0, r1 = max(0, -dr), ROWS - max(0, dr)
                            c0, c1 = max(0, -dc), GRID_W - max(0, dc)
                            i_ = stt(out=dst[:, r0:r1, c0:c1], in0=src[:, r0 + dr:r1 + dr, c0 + dc:c1 + dc],
                                     scalar=colr(L, "fcw", t + FF_T * (3 * (dr + 1) + dc + 1)), in1=dst[:, r0:r1, c0:c1],
                                     op0=ALU.mult, op1=ALU.add)
                            if (dr, dc) != (1, 1):
                                i_.then_inc(*E.done())
                                own()
                    i_.then_inc(*E.done("conv_ready"))
                    v.wait_ge(*E.count("gelu_ready").next())
                    tt(A[:, t, lo_:hi], A[:, t, lo_:hi], ps[:, 2 * s + 1, 0:n], ALU.mult).then_inc(*E.freed(s))
                with E.loop(5) as i:
                    for b in range(4):
                        ffn_tile(E.full()[0], i * 4 + b)
                for t in range(20, 22):
                    ffn_tile(E.full()[0], t)
                own()
                v.sem_inc(*E.done("ffn_ready"))
                E.skip(4)
                postnorm(L, O, "fpost", 5, False, lo_)

        @block.gpsimd
        def _(g_):
            E = Engine(g_, "pool", sems, table)
            g_.dma_start(cond[:, :, :].rearrange("p k c -> p (k c)"), cond_in).then_inc(*E.count("dma_cond").sent())
            for dst, src in ((cst[:, :], const_in), (par[:, :, :].rearrange("p l n -> p (l n)"), par_in),
                             (headp[:, :, :, :, :].rearrange("p a b c d -> p (a b c d)"), headp_in),
                             (wdt[:, :, :, :].rearrange("p a b c -> p (a b c)"), wdt_in)):
                g_.dma_start(dst, src).then_inc(sems["dma_const"], 16)
            xv = X.rearrange("p k t -> p (k t)")
            g_.dma_start(xv, x_in).then_inc(*E.count("dma_x").sent())
            for L in range(DEPTH):
                lo_, hi = N_OUT[L]
                if L == 0:
                    g_.dma_start(lst[:, 0:2, :].rearrange("p a n -> p (a n)"), lora_in[0, :, 0:2 * P]).then_inc(*E.count("dma_wa").sent())
                g_.wait_ge(*E.count("conv_silu").next())
                E.count("conv_silu").n += 23
                g_.wait_ge(*E.count("conv_silu").so_far())
                g_.wait_ge(*E.count("scr_free").next())
                g_.wait_ge(*E.count("wdec_ready").next())
                with E.loop(GROUPS) as g:
                    g_.wait_ge(*E.count("y_ready").so_far())
                    chunks = Y_CHUNKS[L]
                    E.count("y_ready").n += len(chunks)
                    g_.wait_ge(*E.count("xw_ready").next())
                    E.count("xw_ready").n += 5
                    for n, c in enumerate(chunks):
                        if n > 1:
                            g_.wait_ge(sems["y_ready"], E.count("y_ready").so_far()[1] - len(chunks) + n - 1)
                        for d in range(2):
                            i_ = g_.tensor_tensor(xdt[c % 2][d], xtok[:, c], heads4(dtv)[:, d, c, bass.ds(g * HPG, HPG)].unsqueeze(2)
                                                  .to_broadcast((P, HPG, 64)), ALU.mult)
                        for d in range(2):
                            if SSD_ORDER[d].index(c):
                                g_.wait_ge(*E.count("ec_ready").next())
                                g_.sem_inc(sems["pool_passed"], 1)
                                i_ = g_.tensor_tensor(Cb[c % 2][d], Cb[c % 2][d], A[:, XS_T + 4 + g, Q * c:Q * (c + 1)].unsqueeze(1).to_broadcast((P, HPG, P)), ALU.mult)
                        i_.then_inc(*E.done("ct_ready"))
                def hold_v(c):
                    for p in range(2):
                        i_ = g_.tensor_copy(by_pq(vS)[:, 1 - p], by_pq(A[:, 16 + c, :])[:, p])
                    i_.then_inc(*E.done("vs_ready"))

                def load_g2(c):
                    g_.dma_start(lst[:, 2, :], lora_in[c + KT * L, :, 2 * P:3 * P]).then_inc(*E.count("dma_g2").sent())

                def load_wa(c):
                    for _ in range(2):
                        g_.wait_ge(*E.count("sa_ready").next())
                    g_.dma_start(lst[:, 0:2, :].rearrange("p a n -> p (a n)"), lora_in[c + KT * L, :, 0:2 * P]).then_inc(*E.count("dma_wa").sent())

                def rwkv_tile(c, front, tail):
                    if front:
                        for _ in range(2):
                            g_.wait_ge(*E.count("aa_ready").next())
                        hold_v(c + 1)
                    if tail:
                        g_.wait_ge(*E.count("ystd_ready").next())
                        load_g2(c)
                    if front:
                        load_wa(c + 2)

                g_.wait_ge(*E.count("lora_ready").next())
                hold_v(0)
                load_g2(0)
                load_wa(1)
                rwkv_tile(0, True, False)
                with E.loop(KT - 2) as i:
                    rwkv_tile(i + 1, True, True)
                rwkv_tile(KT - 1, False, True)
                E.count("aa_ready").n += 2
                E.count("ystd_ready").n += 1
                g_.wait_ge(*E.count("o_ready").next())
                g_.dma_start(xv, x_in if L == 0 else x_mid).then_inc(*E.count("dma_x").sent())
                E.count("x_ready").n += 2 * KT
                g_.wait_ge(*E.count("x_ready").so_far())
                if L == 0:
                    g_.dma_start(x_mid, xv).then_inc(*E.count("dma_out").sent())
                    g_.wait_ge(*E.count("dma_out").so_far())
            g_.dma_start(out.rearrange("p (k t) -> p k t", k=KT), X[:, :, CTX:T]).then_inc(*E.count("dma_out").sent())
            g_.wait_ge(*E.count("dma_out").so_far())


INS = ("stream", "x_in", "cond", "par", "consts", "headp", "wdt", "lora")


def constants():
    c = np.zeros((P, CONSTS), np.float32)

    def put(name, a, off=0):
        c[:, CCOL[name] + off:CCOL[name] + off + a.shape[1]] = a

    i = np.arange(P)
    put("ident", np.eye(P))
    put("ones", np.ones((P, P)))
    put("headones", (i[:, None] // 64 == i[None] // 64) * 1.0)
    r, t = i[:, None] % RC, np.arange(RC)[None]
    for d in range(2):
        put("tri", (i[:, None] <= i[None]) * 1.0 if d == 0 else (i[:, None] >= i[None]) * 1.0, P * d)
        put("mask2", np.concatenate([(r < t), (r <= t)] if d == 0 else [(r > t), (r >= t)], 1) * 1.0, P * d)
        r2, t2 = i[:, None] % HB, np.arange(HB)[None]
        for m in range(5):
            b = 1 << m
            same = r2 // (2 * b) == t2 // (2 * b)
            low = (r2 // b % 2 == 1) & (t2 // b % 2 == 0)
            high = (r2 // b % 2 == 0) & (t2 // b % 2 == 1)
            put("lvl", (same & (low if d == 0 else high)) * 1.0, HB * (2 * m + d))
    put("id32", (r2 == t2) * 1.0)
    put("half", (r // HB == t // HB) * 1.0)
    put("id64", (r == t) * 1.0)
    return c


def lay_out(inp):
    g = {k: np.asarray(v) for k, v in inp.items()}

    def cols256(w):
        n = w.shape[1]
        return w.reshape(KT, P, n // 256, 256).transpose(2, 1, 0, 3).reshape(n // 256, P, WBLK)

    def tab(a):
        return a.reshape(-1, P).T

    blocks = []
    pars, headp, wdt, lora = [], [], [], []
    for L in range(DEPTH):
        wi = g["w_in"][L]
        o = np.cumsum([0, 2048, 3072, 32, 3072, 128, 128, 128, 2048])
        z, xbc, dt, rkv, wd, ad, gd, gate = [wi[:, o[j]:o[j + 1]] for j in range(8)]
        blocks.append(g["ada_w"][L].reshape(2, 4, P, 12, 512).transpose(3, 0, 2, 1, 4).reshape(24, P, WBLK))
        blocks += [cols256(xbc), cols256(z)]
        blocks.append(g["ssm_out"][L].reshape(16, P, 8, P).transpose(2, 1, 0, 3).reshape(8, P, WBLK))
        blocks += [cols256(gate[:, :D]), cols256(rkv), cols256(np.concatenate([wd, ad], 1)),
                   cols256(np.concatenate([gd, np.zeros_like(gd)], 1)), cols256(g["rwkv_out"][L]), cols256(gate[:, D:]),
                   cols256(g["w_o"][L])]
        fi = g["ffn_w_in"][L]
        pair = np.concatenate([fi[:, :2816].reshape(D, FF_T, 1, P), fi[:, 2816:].reshape(D, FF_T, 1, P)], 2)
        blocks.append(cols256(pair.reshape(D, 2 * 2816)))
        blocks.append(g["ffn_w_out"][L].reshape(11, 2, P, D).transpose(0, 2, 1, 3).reshape(11, P, WBLK))
        wdt.append(dt.reshape(KT, P, HEADS).transpose(1, 0, 2).reshape(P, -1))
        p = np.zeros((P, PARAMS), np.float32)

        def put(name, a):
            p[:, COLS[name]:COLS[name] + a.shape[1]] = a

        for name, key in (("npre", "norm_mix_pre"), ("npost", "norm_mix_post"), ("fpre", "norm_ffn_pre"), ("fpost", "norm_ffn_post"),
                          ("scw", "ssm_conv_w"), ("scb", "ssm_conv_b"), ("snorm", "ssm_norm"), ("rcw", "rwkv_conv_w"),
                          ("w0", "rwkv_w0"), ("a0", "rwkv_a0"), ("kk", "rwkv_k_k"), ("ka", "rwkv_k_a"), ("rk", "rwkv_r_k"),
                          ("lnw", "rwkv_ln_w"), ("lnb", "rwkv_ln_b"), ("fcw", "ffn_conv_w"), ("fcb", "ffn_conv_b"), ("adab", "ada_b")):
            put(name, tab(g[key][L]))
        put("dskip", tab(np.repeat(g["ssm_d"][L], 64)))
        pars.append(p)
        headp.append(np.stack([g["ssm_dt_bias"][L], g["ssm_a_log"][L]]).reshape(-1))
        lora.append(np.stack([g["rwkv_w2"][L].reshape(P, KT, P), g["rwkv_a2"][L].reshape(P, KT, P), g["rwkv_g2"][L].reshape(P, KT, P)], 2)
                    .transpose(1, 0, 2, 3).reshape(KT, P, 3 * P))
    tokens = np.concatenate([g["ctx"][0], g["x"][0]], 0)
    return {
        "stream": np.concatenate(blocks, 0),
        "x_in": tokens.reshape(T, KT, P).transpose(2, 1, 0).reshape(P, -1),
        "cond": np.stack([g["c"][0], g["c_ctx"]], 0).reshape(2, KT, P).transpose(2, 1, 0).reshape(P, -1),
        "par": np.concatenate(pars, 1),
        "consts": constants(),
        "headp": np.repeat(np.concatenate(headp)[None], P, 0),
        "wdt": np.concatenate(wdt, 1),
        "lora": np.concatenate(lora + [np.zeros((1, P, 3 * P), np.float32)], 0),
    }


def program(nc, arrays, table):
    ins = [nc.dram_tensor("in_" + n, arrays[n].shape, F32, kind="ExternalInput").ap() for n in INS]
    out = nc.dram_tensor("out", (P, KT * LAT), F32, kind="ExternalOutput").ap()
    build(nc, ins, out, table)


def kernel(**inputs):
    import concourse.bacc as _bacc
    from concourse.bass_utils import run_bass_kernel_spmd as _run

    arrays = {k: np.ascontiguousarray(v) for k, v in lay_out(inputs).items()}
    table = {}
    for _ in range(2):
        nc = _bacc.Bacc("TRN2", target_bir_lowering=False, num_devices=1)
        program(nc, arrays, table)
    r = _run(nc, [{"in_" + k: v for k, v in arrays.items()}], core_ids=[0])
    got = r.results[0]["out"]
    return np.ascontiguousarray(got.reshape(P, KT, LAT).transpose(2, 1, 0).reshape(1, LAT, D))
```
